# Optimizing a Trainium2 kernel written in Bass

```python
import jax, jax.numpy as jnp
from jax import lax
import numpy as np
import math

D_MODEL = 1024
BATCH = 1
SEQ = 512
DEPTH = 2

CTX_LEN = 256
GRID_W = 64
HEAD_DIM = 64
N_MOD = 9
D_FF = 2816
EPS = 1e-6
NEG_INF = -1e30
NA_HEADS = 4
NA_WIN_H_MAX = 8
NA_WIN_W = 16
NA_QCB = 16
NA_KCB = 32
NA_WIDTH = NA_HEADS * HEAD_DIM
POOL_WINDOWS = (2, 4, 8, 16)
POOL_GROUPS = 4
POOL_WIDTH = 256
POOL_GC = POOL_WIDTH // POOL_GROUPS
GQA_Q_HEADS = 8
GQA_KV_HEADS = 2
GQA_GROUP = GQA_Q_HEADS // GQA_KV_HEADS
GQA_QB = 128
GQA_Q_WIDTH = GQA_Q_HEADS * HEAD_DIM
GQA_KV_WIDTH = GQA_KV_HEADS * HEAD_DIM
ROPE_THETA = 10000.0
OFF_A_Q = 0
OFF_A_K = OFF_A_Q + NA_WIDTH
OFF_A_V = OFF_A_K + NA_WIDTH
OFF_B_U = OFF_A_V + NA_WIDTH
OFF_C_Q = OFF_B_U + POOL_WIDTH
OFF_C_K = OFF_C_Q + GQA_Q_WIDTH
OFF_C_V = OFF_C_K + GQA_KV_WIDTH
D_IN = OFF_C_V + GQA_KV_WIDTH
D_MIX = NA_WIDTH + POOL_WIDTH + GQA_Q_WIDTH


def _rmsnorm(x, g):
    x32 = x.astype(jnp.float32)
    y = x32 * lax.rsqrt(jnp.mean(x32 * x32, axis=-1, keepdims=True) + EPS)
    return (y * g.astype(jnp.float32)).astype(x.dtype)

def _modulate(h, shift, scale):
    return h * (1 + scale) + shift

def _swiglu(h, w_up, w_down):
    a, b = jnp.split(h @ w_up, 2, axis=-1)
    return (jax.nn.silu(a) * b) @ w_down

def _half_ffn(h, g, shift, scale, gate, w_up, w_down):
    return h + 0.5 * gate * _swiglu(_modulate(_rmsnorm(h, g), shift, scale), w_up, w_down)

def _rope_axis(x, ang):
    m = x.shape[-1] // 2
    x32 = x.astype(jnp.float32)
    x1, x2 = x32[..., :m], x32[..., m:]
    cos = jnp.cos(ang)[:, None, :]
    sin = jnp.sin(ang)[:, None, :]
    return jnp.concatenate([x1 * cos - x2 * sin, x1 * sin + x2 * cos], axis=-1)

def _rope_2d(x, ang_row, ang_col):
    half = x.shape[-1] // 2
    out = jnp.concatenate([_rope_axis(x[..., :half], ang_row), _rope_axis(x[..., half:], ang_col)], axis=-1)
    return out.astype(x.dtype)

def _gqa_attend(q, k, v):
    s = jnp.einsum('bqkgd,bskd->bkgqs', q, k, preferred_element_type=jnp.float32) * (q.shape[-1] ** -0.5)
    p = jax.nn.softmax(s, axis=-1).astype(v.dtype)
    return jnp.einsum('bkgqs,bskd->bqkgd', p, v)

def _gqa_blocks(q, k_all, v_all):
    bn, n = q.shape[0], q.shape[1]
    nqb = n // GQA_QB
    qb = q.reshape(bn, nqb, GQA_QB, GQA_KV_HEADS, GQA_GROUP, HEAD_DIM).transpose(1, 0, 2, 3, 4, 5)
    o = lax.map(lambda blk: _gqa_attend(blk, k_all, v_all), qb)
    return o.transpose(1, 0, 2, 3, 4, 5).reshape(bn, n, GQA_Q_WIDTH)

def _neighbourhood_attn(q, k, v, k_ctx, v_ctx, rpb):
    bn, n, nh, dh = q.shape
    rows = n // GRID_W
    kh = min(NA_WIN_H_MAX, rows)
    ncb = GRID_W // NA_QCB
    col = jnp.arange(GRID_W)
    win_c0 = jnp.clip(col - NA_WIN_W // 2, 0, GRID_W - NA_WIN_W)
    blk_c0 = jnp.clip(win_c0[::NA_QCB], 0, GRID_W - NA_KCB)
    key_col = blk_c0[:, None] + jnp.arange(NA_KCB)
    q_c0 = win_c0.reshape(ncb, NA_QCB)[:, :, None]
    kc = key_col[:, None, :]
    valid = (kc >= q_c0) & (kc < q_c0 + NA_WIN_W)
    dx = kc - col.reshape(ncb, NA_QCB)[:, :, None]
    dx_idx = jnp.clip(dx, -(NA_WIN_W - 1), NA_WIN_W - 1) + NA_WIN_W - 1
    scale = dh ** -0.5
    q_grid = q.reshape(bn, rows, ncb, NA_QCB, nh, dh)

    def one_row(r):
        q_r = lax.dynamic_index_in_dim(q_grid, r, axis=1, keepdims=False)
        r0 = jnp.clip(r - kh // 2, 0, rows - kh)
        key_row = r0 + jnp.arange(kh)
        tok = key_row[None, :, None] * GRID_W + key_col[:, None, :]
        k_blk = k[:, tok]
        v_blk = v[:, tok]
        s_lat = jnp.einsum('bjqhd,bjykhd->bhjqyk', q_r, k_blk, preferred_element_type=jnp.float32) * scale
        dy_idx = key_row - r + NA_WIN_H_MAX - 1
        bias = rpb[:, dy_idx[None, None, :, None], dx_idx[:, :, None, :]]
        s_lat = jnp.where(valid[:, :, None, :], s_lat + bias.astype(jnp.float32), NEG_INF)
        s_lat = s_lat.reshape(bn, nh, ncb, NA_QCB, kh * NA_KCB)
        s_ctx = jnp.einsum('bjqhd,bchd->bhjqc', q_r, k_ctx, preferred_element_type=jnp.float32) * scale
        p = jax.nn.softmax(jnp.concatenate([s_lat, s_ctx], axis=-1), axis=-1).astype(v.dtype)
        p_lat = p[..., :kh * NA_KCB].reshape(bn, nh, ncb, NA_QCB, kh, NA_KCB)
        p_ctx = p[..., kh * NA_KCB:]
        o = jnp.einsum('bhjqyk,bjykhd->bjqhd', p_lat, v_blk) + jnp.einsum('bhjqc,bchd->bjqhd', p_ctx, v_ctx)
        return o.reshape(bn, GRID_W, nh, dh)

    o = lax.map(one_row, jnp.arange(rows))
    return o.transpose(1, 0, 2, 3, 4).reshape(bn, n, nh * dh)

def _pool_mix(u, w_pool, scale):
    bn, n, _ = u.shape
    u32 = u.astype(jnp.float32)
    cs = jnp.concatenate([jnp.zeros_like(u32[:, :1]), jnp.cumsum(u32, axis=1)], axis=1)
    cs = cs.reshape(bn, n + 1, POOL_GROUPS, POOL_GC)
    t = jnp.arange(n)[:, None]
    win = jnp.array(POOL_WINDOWS, dtype=jnp.int32)[None, :]
    lo = jnp.clip(t - win // 2, 0, n)
    hi = jnp.clip(t - win // 2 + win, 0, n)
    g_idx = jnp.arange(POOL_GROUPS)[None, :]
    sums = cs[:, hi, g_idx] - cs[:, lo, g_idx]
    mean = sums / (hi - lo).astype(jnp.float32)[None, :, :, None]
    y = (mean - u32.reshape(bn, n, POOL_GROUPS, POOL_GC)).astype(u.dtype)
    y = jnp.einsum('blgc,gcd->blgd', y, w_pool)
    return y.reshape(bn, n, POOL_WIDTH) * scale

def first_inputs(seed: int = 0) -> dict:
    key = jax.random.key(seed)
    ks = jax.random.split(key, 20)
    nrm = jax.random.normal
    f32 = jnp.float32
    return {
        'x': nrm(ks[0], (BATCH, SEQ, D_MODEL), f32),
        'c': nrm(ks[1], (BATCH, D_MODEL), f32),
        'ctx': nrm(ks[2], (BATCH, CTX_LEN, D_MODEL), f32),
        'c_ctx': nrm(ks[3], (D_MODEL,), f32),
        'w_ada': nrm(ks[4], (DEPTH, D_MODEL, N_MOD * D_MODEL), f32) * D_MODEL ** -0.5,
        'b_ada': nrm(ks[5], (DEPTH, N_MOD * D_MODEL), f32) * 0.02,
        'norm_g': 1.0 + 0.05 * nrm(ks[6], (DEPTH, 3, D_MODEL), f32),
        'ffn1_up': nrm(ks[7], (DEPTH, D_MODEL, 2 * D_FF), f32) * D_MODEL ** -0.5,
        'ffn1_down': nrm(ks[8], (DEPTH, D_FF, D_MODEL), f32) * D_FF ** -0.5,
        'ffn2_up': nrm(ks[9], (DEPTH, D_MODEL, 2 * D_FF), f32) * D_MODEL ** -0.5,
        'ffn2_down': nrm(ks[10], (DEPTH, D_FF, D_MODEL), f32) * D_FF ** -0.5,
        'w_in': nrm(ks[11], (DEPTH, D_MODEL, D_IN), f32) * D_MODEL ** -0.5,
        'w_out': nrm(ks[12], (DEPTH, D_MIX, D_MODEL), f32) * D_MIX ** -0.5,
        'na_rpb': nrm(ks[13], (DEPTH, NA_HEADS, 2 * NA_WIN_H_MAX - 1, 2 * NA_WIN_W - 1), f32) * 0.1,
        'pool_w': nrm(ks[14], (DEPTH, POOL_GROUPS, POOL_GC, POOL_GC), f32) * POOL_GC ** -0.5,
        'pool_scale': 1.0 + 0.1 * nrm(ks[15], (DEPTH, POOL_WIDTH), f32),
        'q_norm_g': 1.0 + 0.05 * nrm(ks[16], (DEPTH, HEAD_DIM), f32),
        'k_norm_g': 1.0 + 0.05 * nrm(ks[17], (DEPTH, HEAD_DIM), f32),
        'final_g': 1.0 + 0.05 * nrm(ks[18], (D_MODEL,), f32),
    }

def first_block(x, c, ctx, c_ctx, w_ada, b_ada, norm_g, ffn1_up, ffn1_down, ffn2_up, ffn2_down,
              w_in, w_out, na_rpb, pool_w, pool_scale, q_norm_g, k_norm_g, final_g):
    bn, n, d = x.shape
    ncx = ctx.shape[1]
    pos = jnp.arange(n)
    inv_freq = ROPE_THETA ** (-jnp.arange(0, HEAD_DIM // 2, 2, dtype=jnp.float32) / (HEAD_DIM // 2))
    ang_row = (pos // GRID_W).astype(jnp.float32)[:, None] * inv_freq[None, :]
    ang_col = (pos % GRID_W).astype(jnp.float32)[:, None] * inv_freq[None, :]
    h_x, h_c = x, ctx
    for l in range(DEPTH):
        last = l == DEPTH - 1
        mod_x = (jax.nn.silu(c) @ w_ada[l] + b_ada[l]).reshape(bn, 1, N_MOD, d)
        mod_c = (jax.nn.silu(c_ctx) @ w_ada[l] + b_ada[l]).reshape(1, 1, N_MOD, d)
        h_x = _half_ffn(h_x, norm_g[l, 0], mod_x[:, :, 0], mod_x[:, :, 1], mod_x[:, :, 2], ffn1_up[l], ffn1_down[l])
        h_c = _half_ffn(h_c, norm_g[l, 0], mod_c[:, :, 0], mod_c[:, :, 1], mod_c[:, :, 2], ffn1_up[l], ffn1_down[l])
        a_x = _modulate(_rmsnorm(h_x, norm_g[l, 1]), mod_x[:, :, 3], mod_x[:, :, 4])
        a_c = _modulate(_rmsnorm(h_c, norm_g[l, 1]), mod_c[:, :, 3], mod_c[:, :, 4])
        p_x = a_x @ w_in[l]
        kv_a_c = a_c @ w_in[l][:, OFF_A_K:OFF_B_U]
        kv_c_c = a_c @ w_in[l][:, OFF_C_K:D_IN]
        q_a = p_x[..., OFF_A_Q:OFF_A_K].reshape(bn, n, NA_HEADS, HEAD_DIM)
        k_a = p_x[..., OFF_A_K:OFF_A_V].reshape(bn, n, NA_HEADS, HEAD_DIM)
        v_a = p_x[..., OFF_A_V:OFF_B_U].reshape(bn, n, NA_HEADS, HEAD_DIM)
        k_a_c = kv_a_c[..., :NA_WIDTH].reshape(bn, ncx, NA_HEADS, HEAD_DIM)
        v_a_c = kv_a_c[..., NA_WIDTH:].reshape(bn, ncx, NA_HEADS, HEAD_DIM)
        q_c = _rope_2d(_rmsnorm(p_x[..., OFF_C_Q:OFF_C_K].reshape(bn, n, GQA_Q_HEADS, HEAD_DIM), q_norm_g[l]), ang_row, ang_col)
        q_c = q_c.reshape(bn, n, GQA_KV_HEADS, GQA_GROUP, HEAD_DIM)
        k_c = _rope_2d(_rmsnorm(p_x[..., OFF_C_K:OFF_C_V].reshape(bn, n, GQA_KV_HEADS, HEAD_DIM), k_norm_g[l]), ang_row, ang_col)
        v_c = p_x[..., OFF_C_V:D_IN].reshape(bn, n, GQA_KV_HEADS, HEAD_DIM)
        k_c_c = _rmsnorm(kv_c_c[..., :GQA_KV_WIDTH].reshape(bn, ncx, GQA_KV_HEADS, HEAD_DIM), k_norm_g[l])
        v_c_c = kv_c_c[..., GQA_KV_WIDTH:].reshape(bn, ncx, GQA_KV_HEADS, HEAD_DIM)
        o_a = _neighbourhood_attn(q_a, k_a, v_a, k_a_c, v_a_c, na_rpb[l])
        o_b = _pool_mix(p_x[..., OFF_B_U:OFF_C_Q], pool_w[l], pool_scale[l])
        o_c = _gqa_blocks(q_c, jnp.concatenate([k_c, k_c_c], axis=1), jnp.concatenate([v_c, v_c_c], axis=1))
        h_x = h_x + mod_x[:, :, 5] * (jnp.concatenate([o_a, o_b, o_c], axis=-1) @ w_out[l])
        h_x = _half_ffn(h_x, norm_g[l, 2], mod_x[:, :, 6], mod_x[:, :, 7], mod_x[:, :, 8], ffn2_up[l], ffn2_down[l])
        if not last:
            q_a_c = (a_c @ w_in[l][:, OFF_A_Q:OFF_A_K]).reshape(bn, ncx, NA_HEADS, 1, HEAD_DIM)
            u_c = a_c @ w_in[l][:, OFF_B_U:OFF_C_Q]
            q_c_c = _rmsnorm((a_c @ w_in[l][:, OFF_C_Q:OFF_C_K]).reshape(bn, ncx, GQA_Q_HEADS, HEAD_DIM), q_norm_g[l])
            q_c_c = q_c_c.reshape(bn, ncx, GQA_KV_HEADS, GQA_GROUP, HEAD_DIM)
            oa_c = _gqa_attend(q_a_c, k_a_c, v_a_c).reshape(bn, ncx, NA_WIDTH)
            ob_c = _pool_mix(u_c, pool_w[l], pool_scale[l])
            oc_c = _gqa_attend(q_c_c, k_c_c, v_c_c).reshape(bn, ncx, GQA_Q_WIDTH)
            h_c = h_c + mod_c[:, :, 5] * (jnp.concatenate([oa_c, ob_c, oc_c], axis=-1) @ w_out[l])
            h_c = _half_ffn(h_c, norm_g[l, 2], mod_c[:, :, 6], mod_c[:, :, 7], mod_c[:, :, 8], ffn2_up[l], ffn2_down[l])
    return _rmsnorm(h_x, final_g)


DEPTH_2 = 1

D_ATTN = D_MODEL // 2
N_HEADS = D_ATTN // HEAD_DIM
DILATED_GROUPS = ((128, 1), (512, 4), (2048, 16))
N_GROUPS = len(DILATED_GROUPS)
N_QKV = 3 * N_GROUPS * N_HEADS * HEAD_DIM
D_HYENA = D_MODEL // 2
HYENA_ORDER = 2
FILTER_EMB = 33
FILTER_WIDTH = 64
DECAY_TARGET = 1e-2
FAST_DECAY_PCT = 0.3
SLOW_DECAY_PCT = 1.5
N_IN = N_QKV + D_ATTN + 3 * D_HYENA + D_HYENA + 2 * D_MODEL
DEEPNORM_ALPHA = (2 * DEPTH_2) ** 0.25
DEEPNORM_BETA = (8 * DEPTH_2) ** -0.25
LN_EPS = 1e-5


def _layer_norm(x):
    xf = x.astype(jnp.float32)
    mu = jnp.mean(xf, axis=-1, keepdims=True)
    var = jnp.mean(jnp.square(xf - mu), axis=-1, keepdims=True)
    return (xf - mu) * lax.rsqrt(var + LN_EPS)

def _alibi_slopes(n_heads):
    return jnp.asarray(2.0 ** (-8.0 * (np.arange(n_heads) + 1) / n_heads), dtype=jnp.float32)

def dilated_window_attention(q, k, v, slopes, dilation, radius):
    B, S, H, E = q.shape
    L = S // dilation
    nb = -(-L // radius)
    Lp = nb * radius

    def by_residue(a):
        return a.reshape(B, L, dilation, H, E).transpose(0, 2, 1, 3, 4)

    qs, ks, vs = by_residue(q), by_residue(k), by_residue(v)
    qb = jnp.pad(qs, ((0, 0), (0, 0), (0, Lp - L), (0, 0), (0, 0))).reshape(B, dilation, nb, radius, H, E)

    def windows(a):
        ap = jnp.pad(a, ((0, 0), (0, 0), (radius, Lp - L + radius), (0, 0), (0, 0)))
        ap = ap.reshape(B, dilation, nb + 2, radius, H, E)
        return jnp.concatenate([ap[:, :, :-2], ap[:, :, 1:-1], ap[:, :, 2:]], axis=3)

    kw, vw = windows(ks), windows(vs)
    qi = jnp.arange(nb)[:, None] * radius + jnp.arange(radius)[None, :]
    ki = jnp.arange(nb)[:, None] * radius - radius + jnp.arange(3 * radius)[None, :]
    rel = ki[:, None, :] - qi[:, :, None]
    valid = (jnp.abs(rel) <= radius) & (ki[:, None, :] >= 0) & (ki[:, None, :] < L)
    dist = (jnp.abs(rel) * dilation).astype(jnp.float32)

    s = jnp.einsum('bdnqhe,bdnkhe->bdnhqk', qb, kw).astype(jnp.float32) * (E ** -0.5)
    s = s - slopes[:, None, None] * dist[:, None]
    s = jnp.where(valid[:, None], s, -jnp.inf)
    lse = jax.nn.logsumexp(s, axis=-1)
    p = jnp.exp(s - lse[..., None]).astype(v.dtype)
    o = jnp.einsum('bdnhqk,bdnkhe->bdnqhe', p, vw)

    o = o.reshape(B, dilation, Lp, H, E)[:, :, :L].transpose(0, 2, 1, 3, 4).reshape(B, S, H, E)
    lse = lse.transpose(0, 1, 2, 4, 3).reshape(B, dilation, Lp, H)[:, :, :L]
    lse = lse.transpose(0, 2, 1, 3).reshape(B, S, H)
    return o, lse

def _hyena_pos_features(L):
    t = jnp.linspace(0.0, 1.0, L, dtype=jnp.float32)[:, None]
    bands = (FILTER_EMB - 1) // 2
    w = 2.0 * math.pi * jnp.arange(L, dtype=jnp.float32)[:, None] / L
    f = jnp.linspace(1e-4, bands - 1, bands, dtype=jnp.float32)[None, :]
    return jnp.concatenate([t, jnp.cos(f * w), -jnp.sin(f * w)], axis=-1)

def implicit_filters(L, w1, b1, w2, b2, w3, b3, w4, freq):
    f32 = jnp.float32
    freq = freq.astype(f32)
    h = jnp.sin(freq * (_hyena_pos_features(L) @ w1.astype(f32) + b1.astype(f32)))
    h = jnp.sin(freq * (h @ w2.astype(f32) + b2.astype(f32)))
    h = jnp.sin(freq * (h @ w3.astype(f32) + b3.astype(f32)))
    h = h @ w4.astype(f32)
    t = jnp.linspace(0.0, 1.0, L, dtype=f32)[:, None]
    deltas = jnp.linspace(math.log(DECAY_TARGET) / SLOW_DECAY_PCT,
                          math.log(DECAY_TARGET) / FAST_DECAY_PCT, D_HYENA, dtype=f32)
    decay = jnp.exp(-t * jnp.abs(deltas)[None, :])
    return h.reshape(L, HYENA_ORDER, 2, D_HYENA) * decay[:, None, None, :]

def bidirectional_long_conv(z, h_fwd, h_bwd):
    L, C = h_fwd.shape
    circ = jnp.concatenate([h_fwd, jnp.zeros((1, C), jnp.float32), h_bwd[:0:-1]], axis=0)
    hf = jnp.fft.rfft(circ, axis=0)
    zf = jnp.fft.rfft(z.astype(jnp.float32), n=2 * L, axis=1)
    y = jnp.fft.irfft(zf * hf[None], n=2 * L, axis=1)[:, :L]
    return y.astype(z.dtype)

def centred_conv3(u, w, b):
    up = jnp.pad(u, ((0, 0), (1, 1), (0, 0)))
    return w[0] * up[:, :-2] + w[1] * up[:, 1:-1] + w[2] * up[:, 2:] + b

def hybrid_layer(x, c, w_ada, b_ada, w_in, b_in, conv_w, conv_b,
                 filt_w1, filt_b1, filt_w2, filt_b2, filt_w3, filt_b3, filt_w4, filt_freq, filt_bias,
                 w_proj_attn, w_proj_hyena, w_out, b_out, ln_g, ln_b):
    B, S, _ = x.shape
    mod = (c @ w_ada + b_ada)[:, None, :]
    shift, scale, gate = jnp.split(mod, 3, axis=-1)
    h = (_layer_norm(x) * (1.0 + scale) + shift).astype(x.dtype)

    p = h @ w_in + b_in
    i1 = N_QKV
    i2 = i1 + D_ATTN
    i3 = i2 + 3 * D_HYENA
    i4 = i3 + D_HYENA
    p_qkv, g_attn, p_hy, g_hy, r_merge = jnp.split(p, [i1, i2, i3, i4], axis=-1)
    r_attn, r_hy = jnp.split(r_merge, 2, axis=-1)

    qkv = p_qkv.reshape(B, S, 3, N_GROUPS, N_HEADS, HEAD_DIM)
    slopes = _alibi_slopes(N_HEADS)
    outs, lses = [], []
    for g, (window, dilation) in enumerate(DILATED_GROUPS):
        radius = window // (2 * dilation)
        o_g, lse_g = dilated_window_attention(qkv[:, :, 0, g], qkv[:, :, 1, g], qkv[:, :, 2, g],
                                              slopes, dilation, radius)
        outs.append(o_g)
        lses.append(lse_g)
    wts = jax.nn.softmax(jnp.stack(lses, axis=0), axis=0)
    o_attn = jnp.einsum('gbsh,gbshe->bshe', wts.astype(x.dtype), jnp.stack(outs, axis=0))
    y_attn = o_attn.reshape(B, S, D_ATTN) * jax.nn.silu(g_attn)

    u = centred_conv3(p_hy, conv_w, conv_b)
    v, x1, x2 = jnp.split(u, 3, axis=-1)
    filters = implicit_filters(S, filt_w1, filt_b1, filt_w2, filt_b2, filt_w3, filt_b3, filt_w4, filt_freq)
    z = v
    for o, gate_o in enumerate((x1, x2)):
        z = gate_o * (bidirectional_long_conv(z, filters[:, o, 0], filters[:, o, 1]) + filt_bias[o] * z)
    y_hy = z * jax.nn.silu(g_hy)

    merged = jax.nn.sigmoid(r_attn) * (y_attn @ w_proj_attn) + jax.nn.sigmoid(r_hy) * (y_hy @ w_proj_hyena)
    out = merged @ w_out + b_out

    res = DEEPNORM_ALPHA * x.astype(jnp.float32) + (gate * out).astype(jnp.float32)
    return (_layer_norm(res) * ln_g + ln_b).astype(x.dtype)

def second_inputs(seed: int = 0) -> dict:
    key = jax.random.key(seed)
    ks = jax.random.split(key, 24)
    f32 = jnp.float32

    def nrm(k, shape, scale):
        return jax.random.normal(k, shape, f32) * scale

    return {
        "x": nrm(ks[0], (BATCH, SEQ, D_MODEL), 1.0),
        "c": nrm(ks[1], (BATCH, D_MODEL), 1.0),
        "w_ada": nrm(ks[2], (DEPTH_2, D_MODEL, 3 * D_MODEL), 0.5 * D_MODEL ** -0.5),
        "b_ada": nrm(ks[3], (DEPTH_2, 3 * D_MODEL), 0.01),
        "w_in": nrm(ks[4], (DEPTH_2, D_MODEL, N_IN), D_MODEL ** -0.5),
        "b_in": nrm(ks[5], (DEPTH_2, N_IN), 0.01),
        "conv_w": nrm(ks[6], (DEPTH_2, 3, 3 * D_HYENA), 3 ** -0.5),
        "conv_b": nrm(ks[7], (DEPTH_2, 3 * D_HYENA), 0.01),
        "filt_w1": nrm(ks[8], (DEPTH_2, FILTER_EMB, FILTER_WIDTH), FILTER_EMB ** -0.5),
        "filt_b1": nrm(ks[9], (DEPTH_2, FILTER_WIDTH), 0.1),
        "filt_w2": nrm(ks[10], (DEPTH_2, FILTER_WIDTH, FILTER_WIDTH), FILTER_WIDTH ** -0.5),
        "filt_b2": nrm(ks[11], (DEPTH_2, FILTER_WIDTH), 0.1),
        "filt_w3": nrm(ks[12], (DEPTH_2, FILTER_WIDTH, FILTER_WIDTH), FILTER_WIDTH ** -0.5),
        "filt_b3": nrm(ks[13], (DEPTH_2, FILTER_WIDTH), 0.1),
        "filt_w4": nrm(ks[14], (DEPTH_2, FILTER_WIDTH, HYENA_ORDER * 2 * D_HYENA), 0.1 * FILTER_WIDTH ** -0.5),
        "filt_freq": 1.0 + nrm(ks[15], (DEPTH_2, FILTER_WIDTH), 0.05),
        "filt_bias": nrm(ks[16], (DEPTH_2, HYENA_ORDER, D_HYENA), 0.1),
        "w_proj_attn": nrm(ks[17], (DEPTH_2, D_ATTN, D_MODEL), DEEPNORM_BETA * D_ATTN ** -0.5),
        "w_proj_hyena": nrm(ks[18], (DEPTH_2, D_HYENA, D_MODEL), DEEPNORM_BETA * D_HYENA ** -0.5),
        "w_out": nrm(ks[19], (DEPTH_2, D_MODEL, D_MODEL), DEEPNORM_BETA * D_MODEL ** -0.5),
        "b_out": nrm(ks[20], (DEPTH_2, D_MODEL), 0.01),
        "ln_g": 1.0 + nrm(ks[21], (DEPTH_2, D_MODEL), 0.05),
        "ln_b": nrm(ks[22], (DEPTH_2, D_MODEL), 0.01),
    }

def second_block(x, c, w_ada, b_ada, w_in, b_in, conv_w, conv_b,
              filt_w1, filt_b1, filt_w2, filt_b2, filt_w3, filt_b3, filt_w4, filt_freq, filt_bias,
              w_proj_attn, w_proj_hyena, w_out, b_out, ln_g, ln_b):
    for l in range(DEPTH_2):
        x = hybrid_layer(x, c, w_ada[l], b_ada[l], w_in[l], b_in[l], conv_w[l], conv_b[l],
                         filt_w1[l], filt_b1[l], filt_w2[l], filt_b2[l], filt_w3[l], filt_b3[l],
                         filt_w4[l], filt_freq[l], filt_bias[l],
                         w_proj_attn[l], w_proj_hyena[l], w_out[l], b_out[l], ln_g[l], ln_b[l])
    return x


def setup_inputs(seed=0):
    out = dict(first_inputs(seed))
    for name, value in second_inputs(seed + 1).items():
        if name != "x":
            out[name + "_2"] = value
    return out


def reference(
    x, c, ctx, c_ctx, w_ada, b_ada, norm_g, ffn1_up, ffn1_down, ffn2_up, ffn2_down, w_in, w_out,
    na_rpb, pool_w, pool_scale, q_norm_g, k_norm_g, final_g, c_2, w_ada_2, b_ada_2, w_in_2,
    b_in_2, conv_w_2, conv_b_2, filt_w1_2, filt_b1_2, filt_w2_2, filt_b2_2, filt_w3_2,
    filt_b3_2, filt_w4_2, filt_freq_2, filt_bias_2, w_proj_attn_2, w_proj_hyena_2, w_out_2,
    b_out_2, ln_g_2, ln_b_2,
):
    x = first_block(
        x, c, ctx, c_ctx, w_ada, b_ada, norm_g, ffn1_up, ffn1_down, ffn2_up, ffn2_down, w_in,
        w_out, na_rpb, pool_w, pool_scale, q_norm_g, k_norm_g, final_g,
    )
    return second_block(
        x, c_2, w_ada_2, b_ada_2, w_in_2, b_in_2, conv_w_2, conv_b_2, filt_w1_2, filt_b1_2,
        filt_w2_2, filt_b2_2, filt_w3_2, filt_b3_2, filt_w4_2, filt_freq_2, filt_bias_2,
        w_proj_attn_2, w_proj_hyena_2, w_out_2, b_out_2, ln_g_2, ln_b_2,
    )


_drawn_inputs = setup_inputs


def setup_inputs(seed=0):
    import zlib

    import numpy as np

    out = dict(_drawn_inputs(seed))
    spreads = {}
    factors = {'na_rpb': 8.0,
     'q_norm_g': 8.0,
     'k_norm_g': 8.0,
     'b_ada_2': 22.942,
     'b_in_2': 46.972,
     'conv_b_2': 54.204,
     'filt_freq_2': 5.054,
     'filt_bias_2': 5.985,
     'b_out_2': 8.0,
     'ln_b_2': 5.916}
    for name, (base, spread) in spreads.items():
        noise = np.random.default_rng([zlib.crc32(name.encode()), seed]).standard_normal(out[name].shape)
        drawn = base * np.exp(spread * noise) if base else spread * noise
        out[name] = __import__('jax').numpy.asarray(drawn.astype(out[name].dtype))
    for name, factor in factors.items():
        out[name] = (out[name] * factor).astype(out[name].dtype)
    return out
```

```python
import math
from contextlib import ExitStack

import numpy as np

import concourse.bass as bass
from concourse import mybir

F32 = mybir.dt.float32
ALU = mybir.AluOpType
ACT = mybir.ActivationFunctionType
AX = mybir.AxisListType
ds = bass.ds

P = 128
D = 1024
KC = D // P
NX, NCTX = 512, 256
T = NX + NCTX
DEPTH = 2
FF = 2816
FC = FF // P
NMOD = 9
HD = 64
EPS, LN_EPS = 1e-6, 1e-5
GRID = 64
NEG = -1e30
SCORE_SCALE = HD ** -0.5
PAD = 16
POOL_X, POOL_C, POOL_W = PAD, 2 * PAD + NX, 3 * PAD + T
ALPHA = 2 ** 0.25
NG, NH2 = 3, 8
RES = 4
KEYS2 = NX + 2 * P
AHEAD = 3
RING, SLOT = 4, FC * P
FREE, FREE_HID = 4, 2
QC = NX // P
TWO_PI_HI = 6.28125
TWO_PI_LO = 2 * math.pi - TWO_PI_HI
ROUND_MAGIC = 12582912.0
PI_BELOW = 3.1415925

QA, KA, UU, QG, KG, NPROJ = 0, 2, 4, 6, 10, 11


def weight_plan():
    plan, at = {}, 0

    def add(name, n):
        nonlocal at
        plan[name] = (at, n)
        at += n

    for l in range(DEPTH):
        add(f"ada{l}", NMOD * KC // 2)
        add(f"up1_{l}", FC)
        add(f"down1_{l}", KC)
        add(f"in{l}", 8)
        add(f"out{l}", KC // 2)
        add(f"up2_{l}", FC)
        add(f"down2_{l}", KC)
    add("ada_h", 3 * KC // 2)
    add("q_h", 6)
    add("k_h", 6)
    add("v_h", 6)
    add("gattn_h", 2)
    add("conv_h", 6)
    add("ghy_h", 2)
    add("merge_h", 3 * KC // 2)
    add("out_h", KC // 2)
    return plan


class Chain:

    def __init__(self, eng, sem):
        self.eng, self.sem, self.n, self.i = eng, sem, 0, None

    def mark(self, ins):
        ins.then_inc(self.sem, 1)
        self.n += 1

    def wait(self):
        self.eng.wait_ge(self.sem, self.n if self.i is None else self.i * self.per + self.n)

    def link(self, ins):
        self.mark(ins)
        self.wait()

    def enter(self, i, per):
        self.i, self.per, self.n0 = i, per, self.n

    def leave(self, trips):
        assert self.n - self.n0 == self.per, (self.n - self.n0, self.per)
        self.n, self.i = self.n0 + trips * self.per, None


def for_units(eng, plan, name, body):
    g0, n = plan[name]
    trips = n // RING if n >= 2 * RING else 0
    if trips:
        with eng.Fori(0, trips) as i:
            for j in range(RING):
                k = g0 + j
                body(i * RING + j, i * RING + k, k % RING, i + k // RING)
    for u in range(trips * RING, n):
        body(u, g0 + u, (g0 + u) % RING, (g0 + u) // RING)


class Attention:

    def __init__(self, tiles, jobs, width, own_steps, before):
        self.own_steps, self.tiles, self.jobs, self.width = own_steps, tiles, jobs, width
        self.pieces = -(-width // 512)
        self.on_act = [p for p in range(self.pieces) if p % 2 == 0]
        self.on_dve = [p for p in range(self.pieces) if p % 2 == 1]
        b = before
        self.tile0 = b.tile0 + b.tiles if b else 0
        self.job0 = b.job0 + b.tiles * b.jobs if b else 0
        self.job_end = self.job0 + tiles * jobs
        self.piece0 = b.piece0 + b.tiles * b.jobs * b.pieces if b else 0
        self.act0 = b.act0 + b.tiles * b.jobs * len(b.on_act) if b else 0
        self.dve0 = b.dve0 + b.tiles * b.jobs * len(b.on_dve) if b else 0

    def scores_at(self, j):
        return 1024 * (j % 2)

    def keys_of(self, p):
        return 512 * p, min(512 * (p + 1), self.width)

    def evacuated(self, i, j, p):
        mine = self.on_act if p % 2 == 0 else self.on_dve
        first = self.act0 if p % 2 == 0 else self.dve0
        return i * (self.jobs * len(mine)) + (first + j * len(mine) + mine.index(p) + 1)


def hybrid_kernel(nc, io, out, stop=None):
    plan = weight_plan()
    first = {k: v[0] for k, v in plan.items()}
    after = {k: v[0] + v[1] for k, v in plan.items()}
    att_x0 = Attention(QC, 12, T, 1 + 2 * 4 + 12, None)
    att_c0 = Attention(NCTX // P, 12, NCTX, 1 + 12, att_x0)
    att_x1 = Attention(QC, 12, T, 1 + 2 * 4 + 12, att_c0)
    att_h = Attention(QC, NH2, KEYS2, 2 + 2 * NH2 + NH2, att_x1)
    att_x = [att_x0, att_x1]
    TAB_MIX, TAB_QKV = (64, 128), 160
    TAB_FEATS, TAB_DFT, TAB_W4 = 208, 224, (208, 240)

    ctx = ExitStack()
    with ctx:
        def sb(name, shape):
            return ctx.enter_context(nc.sbuf_tensor(name, shape, F32))

        def sem(name):
            return ctx.enter_context(nc.semaphore(name))

        ring = [sb(f"ring{i}", [P, SLOT]) for i in range(RING)]
        arena = sb("arena", [P, 39440])

        def view(at, *dims):
            n = int(np.prod(dims))
            assert at + n <= 39440, (at, dims)
            v = arena[:, at:at + n]
            if len(dims) == 2:
                return v.rearrange("p (a b) -> p a b", a=dims[0])
            if len(dims) == 3:
                return v.rearrange("p (a b c) -> p a b c", a=dims[0], b=dims[1])
            return v

        A0 = KC * T
        G0 = 2 * KC * T
        W0 = G0 + FC * T
        h = view(0, KC, T)
        a = view(A0, KC, T)
        hid = view(G0, FC, T)
        proj = view(G0, NPROJ, T)
        v_tok = view(G0 + NPROJ * T, T // P, 384)
        rpb = view(G0 + NPROJ * T + T // P * 384, 4, 15 * GRID)
        cos_t = view(W0 - 2 * NX, NX)
        sin_t = view(W0 - NX, NX)
        sil = view(W0, 2, T)
        rstd = view(W0 + 2 * T, T)
        upad = view(W0, 2, POOL_W)
        qk_sq = view(W0 + 2 * POOL_W, 2, T)
        qk_rs = view(W0 + 2 * POOL_W + 2 * T, 2, T)
        rope_t = view(W0 + 2 * POOL_W + 4 * T, 2, NX)
        win2 = view(W0 + 2 * POOL_W, 2, POOL_W)
        win4 = view(W0 + 4 * POOL_W, 2, POOL_W)
        win8 = view(W0 + 6 * POOL_W, POOL_W)
        win16 = view(W0 + 7 * POOL_W, POOL_W)
        pool_y = view(W0 + 8 * POOL_W, 2, POOL_W)
        pool_inv = view(W0 + 10 * POOL_W, 2, POOL_W)
        probs_1 = view(W0, 3, T)
        keysT_1 = view(W0 + 3 * T, 2, T)
        qst_1 = view(W0 + 5 * T, 6, P)

        h2 = view(0, KC, NX)
        h2r = h2.rearrange("p c (u r) -> p c r u", r=RES)
        y_attn = view(4096, 4, NX)
        x2 = view(A0, KC, NX)
        B0 = A0 + KC * NX
        qh = view(B0, 12, NX)
        kh = view(B0 + 12 * NX, 12, NX)
        vh = view(B0 + 24 * NX, QC, 1536)
        alibi = view(B0 + 24 * NX + QC * 1536, 9 * P)
        H0 = B0 + 24 * NX + QC * 1536 + 9 * P
        probs_2 = view(H0, 3, KEYS2)
        keysT_2 = view(H0 + 3 * KEYS2, 2, KEYS2)
        qst_2 = view(H0 + 5 * KEYS2, 12, P)
        kst = view(H0 + 5 * KEYS2 + 12 * P, 8, P)
        vst = view(H0 + 5 * KEYS2 + 20 * P, 2, NX)
        vbias = view(H0, 1536)
        sq2 = view(B0, KC, NX)
        rstd2 = view(B0 + KC * NX, NX)
        dft = view(B0, 16, NX)
        vxx = view(B0 + 8192, 12, NX)
        hf = view(B0 + 8192 + 6144, 4, NX)
        hb = view(B0 + 8192 + 8192, 4, NX)
        y_re, y_im = hf, hb
        decay = view(B0 + 18432, 4, NX)
        H_re = view(B0 + 20480, 4, NX)
        H_im = view(B0 + 22528, 4, NX)
        z_tok = view(B0 + 24576, 4, NX)
        cpad = view(B0 + 26624, 2, 520)
        gate_t = view(B0 + 26624, 2, NX)
        mul_t = view(B0 + 26624 + 1040, 2, NX)
        f_hid = view(B0 + 28688, NX)
        f_tmp = view(B0 + 26624, 3, NX)
        w4 = view(B0 + 24576, 2 * NX)
        merged = view(B0, KC, NX)
        res = view(B0 + 4096, KC, NX)
        res_sq = view(B0, KC, NX)
        sg_t = view(B0 + 14336, 2, 2 * NX)
        mt_t = view(B0 + 16384, 2, NX)
        fin = view(B0 + 18432, KC, NX)

        cst = sb("cst", [P, 3 * P])
        ident, rot, pairs = (cst[:, k * P:(k + 1) * P] for k in range(3))
        ones = sb("ones", [P, P])
        cvec = sb("cvec", [P, KC * 3])
        cv = cvec[:].rearrange("p (k s) -> p k s", s=3)
        b_ada = sb("b_ada", [P, DEPTH * NMOD * KC * 2])
        mods = [sb(f"mods{l}", [P, NMOD * KC * 2]) for l in range(DEPTH)]
        mod = [m[:].rearrange("p (n c s) -> p n c s", n=NMOD, s=2) for m in mods]
        ng = sb("ng", [P, DEPTH * 3 * KC * 2 + KC])
        ngv = ng[:, 0:DEPTH * 3 * KC * 2].rearrange("p (l k c s) -> p l k c s", l=DEPTH, k=3, s=2)
        final_g = ng[:, DEPTH * 3 * KC * 2:]
        gain = sb("gain", [P, 3 * KC * 2])
        gainv = gain[:].rearrange("p (k c s) -> p k c s", k=3, s=2)
        half_gate = sb("half_gate", [P, 2 * KC * 2])
        hgate = half_gate[:].rearrange("p (k c s) -> p k c s", k=2, s=2)
        small = sb("small", [P, 4 * DEPTH])
        qkg = sb("qkg", [P, 2 * DEPTH])
        poolw = sb("poolw", [P, DEPTH * 2 * P])
        pw = poolw[:].rearrange("p (l k m) -> p l k m", l=DEPTH, k=2)
        nmax = sb("nmax", [P, 4])
        rsum = sb("rsum", [P, 4])
        rinv = sb("rinv", [P, 4])
        vec2 = sb("vec2", [P, 176])
        OB_ADA, OB_IN, OCW, OCB, OFB, OBO, OLG, OLB = 0, 24, 96, 132, 144, 152, 160, 168
        mod2 = sb("mod2", [P, 3 * KC])
        gain2 = sb("gain2", [P, KC])
        bq = sb("bq", [P, 12])
        eps = sb("eps", [P, 2])
        feats = view(B0, NX)
        fw = sb("fw", [HD, 3 * HD + 4])

        psum = ctx.enter_context(nc.psum_tensor("psum", [P, 4096], F32))

        def bank(b, n=512):
            return psum[:, 512 * b:512 * b + n]

        w_landed = [sem(f"w_landed{i}") for i in range(RING)]
        unit_done = sem("unit_done")
        consts_in = sem("consts_in")
        table_in = sem("table_in")
        act_own, dve_own = sem("act_own"), sem("dve_own")
        setup_done = sem("setup_done")
        silu_c = sem("silu_c")
        mod_ready = sem("mod_ready")
        mean_done, mean_done_0, centred = sem("mean_done"), sem("mean_done_0"), sem("centred")
        sq_done, ss_done, root_done = sem("sq_done"), sem("ss_done"), sem("root_done")
        scaled_done, normed = sem("scaled_done"), sem("normed")
        silu_done = sem("silu_done")
        hid_done = sem("hid_done")
        res_done = sem("res_done")
        upad_ready = sem("upad_ready")
        proj_done = sem("proj_done")
        qk_sq_done, qk_ss_done, qk_root_done = sem("qk_sq_done"), sem("qk_ss_done"), sem("qk_root_done")
        qk_normed, qk_rotated, qk_roped = sem("qk_normed"), sem("qk_rotated"), sem("qk_roped")
        pool_ready, pool_done, pool_out = sem("pool_ready"), sem("pool_done"), sem("pool_out")
        q_staged = sem("q_staged")
        scores_done, max_done, exp_done = sem("scores_done"), sem("max_done"), sem("exp_done")
        turned, turned_act, turned_dve = sem("turned"), sem("turned_act"), sem("turned_dve")
        probs_ready = sem("probs_ready")
        heads_done, heads_out = sem("heads_done"), sem("heads_out")
        qk2_out, v2_out = sem("qk2_out"), sem("v2_out")
        f_mm, f_arg, f_sin = sem("f_mm"), sem("f_arg"), sem("f_sin")
        cpad_zero, conv_in, conv_out = sem("cpad_zero"), sem("conv_in"), sem("conv_out")
        fh_mm, fh_out, fh_ready = sem("fh_mm"), sem("fh_out"), sem("fh_ready")
        ft_mm, ft_out = sem("ft_mm"), sem("ft_out")
        zt_mm, zt_out = sem("zt_mm"), sem("zt_out")
        zf_mm, zf_out = sem("zf_mm"), sem("zf_out")
        zi_mm, zi_out = sem("zi_mm"), sem("zi_out")
        gate_act, gate_mul = sem("gate_act"), sem("gate_mul")
        merge_sig, merge_out, out2_done = sem("merge_sig"), sem("merge_out"), sem("out2_done")
        stored = sem("stored")

        N_CONSTS = 16 * 10
        PER_PROJ = NPROJ + 2 * (T // P)
        RMS = 3 * DEPTH + 1
        both_in = [l < DEPTH - 1 for l in range(DEPTH)]

        def keeps_ctx(l, c):
            return both_in[l] or c in (KA, KA + 1, KG)

        def blocks_of(slot, n, k):
            return ring[slot][:, 0:n * k * P].rearrange("p (n k m) -> p n k m", n=n, k=k)

        phases = ["ada0", "ffn1_0", "mix0", "ffn2_0", "ada1", "ffn1_1", "mix1", "ffn2_1", "final",
                  "qkv_h", "att_h", "hyena", "merge"]

        def on(name):
            return stop is None or phases.index(name) <= phases.index(stop)

        block = ctx.enter_context(nc.Block())

        @block.sync
        def _(sp):
            def stream(name, floats):
                def load(u, g, slot, turn):
                    sp.wait_ge(unit_done, g + 1)
                    sp.dma_start(ring[slot][:, 0:floats],
                                 io[name][ds(u, 1), :, :].rearrange("u p n -> (u p) n")).then_inc(w_landed[slot], 16)
                for_units(sp, plan, name, load)

            for l in range(DEPTH):
                if on(f"ada{l}"):
                    stream(f"ada{l}", 2 * D)
                if on(f"ffn1_{l}"):
                    stream(f"up1_{l}", 2 * D)
                    stream(f"down1_{l}", FC * P)
                if on(f"mix{l}"):
                    stream(f"in{l}", 2 * D)
                    stream(f"out{l}", 2 * D)
                if on(f"ffn2_{l}"):
                    stream(f"up2_{l}", 2 * D)
                    stream(f"down2_{l}", FC * P)
            if on("qkv_h"):
                for name in ("ada_h", "q_h", "k_h", "v_h"):
                    stream(name, 2 * D)
            if on("att_h"):
                stream("gattn_h", 2 * D)
            if on("hyena"):
                stream("conv_h", 2 * D)
                stream("ghy_h", 2 * D)
            if on("merge"):
                stream("merge_h", 2 * D)
                stream("out_h", 2 * D)

        @block.gpsimd
        def _(gp):
            def load(dst, src, s=consts_in):
                gp.dma_start(dst, src).then_inc(s, 16)

            load(cvec[:], io["cvec"])
            load(b_ada[:], io["b_ada"])
            load(ng[:], io["ng"])
            load(h[:, :, 0:NX], io["xT"])
            load(h[:, :, NX:T], io["ctxT"])
            load(cst[:], io["cst"])
            load(small[:], io["small"])
            load(poolw[:], io["poolw"])
            load(vec2[:], io["vec2"])
            load(fw[:], io["fw"])
            for l in range(DEPTH):
                if on(f"mix{l}"):
                    gp.wait_ge(unit_done, after[f"down1_{l}"] + RING)
                    load(cos_t, io["cos_t"], table_in)
                    load(sin_t, io["sin_t"], table_in)
                    load(rpb, io[f"rpb{l}"], table_in)
                    load(pool_inv, io["pool_inv"], table_in)
            if on("qkv_h"):
                gp.wait_ge(normed, KC * RMS)
                load(alibi, io["alibi"], table_in)
                load(vbias, io["vbias"], table_in)
            if on("hyena"):
                gp.wait_ge(heads_out, att_h.job_end)
                load(feats[0:33, :], io["feats"], table_in)
                load(decay, io["decay"], table_in)
                load(w4[0:HD, :], io["w4_0"], table_in)
                gp.wait_ge(f_mm, 1)
                load(dft, io["dft"], table_in)
                gp.wait_ge(zf_mm, 4)
                load(w4[0:HD, :], io["w4_1"], table_in)
            if on("merge"):
                for c in range(KC):
                    gp.wait_ge(normed, KC * (RMS + 1) + c + 1)
                    gp.dma_start(out[c], fin[:, c, :]).then_inc(stored, 16)
                gp.wait_ge(stored, 16 * KC)

        @block.tensor
        def _(pe):
            def landed(slot, turn):
                pe.wait_ge(w_landed[slot], 16 * turn + 16)

            def accumulate(out_ap, pairs_):
                for k, (w, x) in enumerate(pairs_):
                    mm = pe.matmul(out_ap, w, x, start=(k == 0), stop=(k == len(pairs_) - 1))
                return mm

            def ada(name, vec, cols):
                def unit(u, g, slot, turn):
                    landed(slot, turn)
                    w = blocks_of(slot, 2, KC)
                    for j in range(2):
                        mm = accumulate(psum[:, ds(u * (2 * cols) + (3584 + j * cols), cols)],
                                        [(w[:, j, k, :], vec[:, k, :]) for k in range(KC)])
                    mm.then_inc(unit_done, 1)
                for_units(pe, plan, name, unit)

            def sum_chunks(n, src, width, at, s_in, s_out):
                for c in range(KC):
                    pe.wait_ge(s_in, n + c + 1)
                    mm = pe.matmul(psum[:, at:at + NX], ones[:], src[:, c, 0:NX], start=(c == 0), stop=(c == KC - 1))
                    if width > NX:
                        mm = pe.matmul(psum[:, at + NX:at + T], ones[:], src[:, c, NX:T], start=(c == 0), stop=(c == KC - 1))
                mm.then_inc(s_out, 1)

            def ffn_up(name, n, both):
                g0 = first[name]

                def unit(u, g, slot, turn):
                    landed(slot, turn)
                    pe.wait_ge(hid_done, u + (FC * n + 1))
                    w = blocks_of(slot, 2, KC)
                    s = (slot - g0) % 2
                    for j in range(2):
                        at_c = (3 * s + 2) * 512 + j * NCTX
                        for k in range(KC):
                            mm = pe.matmul(bank(3 * s + j), w[:, j, k, :], a[:, k, 0:NX], start=(k == 0), stop=(k == KC - 1))
                            if both:
                                mm = pe.matmul(psum[:, at_c:at_c + NCTX], w[:, j, k, :], a[:, k, NX:T],
                                               start=(k == 0), stop=(k == KC - 1))
                    mm.then_inc(unit_done, 1)
                for_units(pe, plan, name, unit)

            def residual(name, n, src, blocks, per_unit, both):
                g0 = first[name]

                def unit(u, g, slot, turn):
                    landed(slot, turn)
                    w = blocks_of(slot, per_unit, blocks)
                    pe.wait_ge(res_done, u * per_unit + (KC * n + FREE - per_unit))
                    for j in range(per_unit):
                        s = (slot - g0) % 2 * per_unit + j
                        for k in range(blocks):
                            mm = pe.matmul(bank(2 * s), w[:, j, k, :], src[:, k, 0:NX], start=(k == 0), stop=(k == blocks - 1))
                            if both:
                                mm = pe.matmul(bank(2 * s + 1, NCTX), w[:, j, k, :], src[:, k, NX:T],
                                               start=(k == 0), stop=(k == blocks - 1))
                    mm.then_inc(unit_done, 1)
                for_units(pe, plan, name, unit)

            def attention(att, jobs, qst, probs, keysT):
                NJ, NP = att.jobs, att.pieces
                with pe.Fori(0, att.tiles) as i:
                    def scores(j):
                        if j >= 2:
                            pe.wait_ge(exp_done, i * NJ + (att.job0 + j - 1))
                        base = att.scores_at(j)
                        for q, half, keys, lo, hi in jobs[j][0]:
                            mm = pe.matmul(psum[:, base + lo:base + hi], qst[64 * half:64 * half + 64, q, :], keys,
                                           start=True, stop=True)
                        mm.then_inc(scores_done, 1)

                    def turn(j):
                        pe.wait_ge(probs_ready, i * NJ + (att.job0 + j + 1))
                        for p in range(NP):
                            if j >= 1:
                                pe.wait_ge(turned_act if p % 2 == 0 else turned_dve, att.evacuated(i, j - 1, p))
                            lo, hi = att.keys_of(p)
                            for k in range(lo, hi, P):
                                mm = pe.transpose(psum[:, 2048 + k:2048 + k + P], probs[:, j % 3, k:k + P], ident)
                            mm.then_inc(turned, 1)

                    def values(j):
                        if j == NJ - 1:
                            for p in range(NP):
                                pe.wait_ge(turned_act if p % 2 == 0 else turned_dve, att.evacuated(i, j, p))
                        if j >= 2:
                            pe.wait_ge(heads_out, i * NJ + (att.job0 + j - 1))
                        half = j % 2
                        out_ = psum[64 * half:64 * half + 64, 3072 + 512 * (j % 2):3072 + 512 * (j % 2) + P]
                        for k in range(0, att.width, P):
                            mm = pe.matmul(out_, jobs[j][1][k // P], keysT[:, j % 2, k:k + P],
                                           start=(k == 0), stop=(k + P == att.width))
                        mm.then_inc(heads_done, 1)

                    pe.wait_ge(q_staged, i + (att.tile0 + 1))
                    for j in range(AHEAD):
                        scores(j)
                    turn(0)
                    for j in range(NJ):
                        if j + AHEAD < NJ:
                            scores(j + AHEAD)
                        if j + 1 < NJ:
                            turn(j + 1)
                        values(j)
                    pe.wait_ge(heads_out, i * NJ + (att.job0 + NJ))

            def block1_jobs(k0):
                jobs = []
                for n in range(12):
                    if n < 4:
                        q, half, kc, vcol = n // 2, n % 2, KA + n // 2, n * HD
                    else:
                        q, half, kc, vcol = 2 + (n - 4) // 2, n % 2, KG, 256 + n % 2 * HD
                    pieces = [(q, half, proj[64 * half:64 * half + 64, kc, lo:hi], lo - k0, hi - k0)
                              for lo, hi in ((k0, NX), (NX, T)) if hi > lo]
                    jobs.append((pieces, [v_tok[:, t, vcol:vcol + HD] for t in range(k0 // P, T // P)]))
                return jobs

            def mix(l):
                g0 = first[f"in{l}"]
                both = both_in[l]
                pe.wait_ge(normed, KC * (3 * l + 2))
                for c in range(NPROJ):
                    slot = (g0 + c // 2) % RING
                    if c % 2 == 0:
                        landed(slot, (g0 + c // 2) // RING)
                    if c >= 4:
                        pe.wait_ge(proj_done, PER_PROJ * l + c - 3)
                    w = blocks_of(slot, 2, KC)
                    for k in range(KC):
                        mm = pe.matmul(bank(2 * (c % 4)), w[:, c % 2, k, :], a[:, k, 0:NX], start=(k == 0), stop=(k == KC - 1))
                        if keeps_ctx(l, c):
                            mm = pe.matmul(bank(2 * (c % 4) + 1, NCTX), w[:, c % 2, k, :], a[:, k, NX:T],
                                           start=(k == 0), stop=(k == KC - 1))
                    if c % 2 == 1 or c == NPROJ - 1:
                        mm.then_inc(unit_done, 1)
                for n, cols in ((0, 256), (1, 128)):
                    slot = (g0 + 6 + n) % RING
                    landed(slot, (g0 + 6 + n) // RING)
                    w = ring[slot][:, 0:KC * cols].rearrange("p (k n) -> p k n", k=KC)
                    for t in range(T // P):
                        pe.wait_ge(proj_done, PER_PROJ * l + NPROJ + (t + 1 if n else 0))
                        mm = accumulate(bank(t, cols), [(a[:, k, t * P:(t + 1) * P], w[:, k, :]) for k in range(KC)])
                    mm.then_inc(unit_done, 1)
                for n in range(5):
                    c = QG + n
                    pe.wait_ge(qk_sq_done, 5 * l + n + 1)
                    if n == 0:
                        pe.wait_ge(proj_done, PER_PROJ * (l + 1))
                    else:
                        pe.wait_ge(qk_root_done, 5 * l + n)
                    mm = pe.matmul(bank(4), pairs, qk_sq[:, n % 2, 0:NX], start=True, stop=True)
                    if keeps_ctx(l, c):
                        mm = pe.matmul(bank(5, NCTX), pairs, qk_sq[:, n % 2, NX:T], start=True, stop=True)
                    mm.then_inc(qk_ss_done, 1)
                    pe.wait_ge(qk_normed, 5 * l + n + 1)
                    if n >= 2:
                        pe.wait_ge(qk_roped, 5 * l + n - 1)
                    pe.matmul(bank(6 + n % 2), rot, proj[:, c, 0:NX], start=True, stop=True).then_inc(qk_rotated, 1)
                for k in range(2):
                    pe.wait_ge(pool_ready, 2 * l + k + 1)
                    mm = pe.matmul(bank(2 * k), pw[:, l, k, :], pool_y[:, k, POOL_X:POOL_X + NX], start=True, stop=True)
                    if both:
                        mm = pe.matmul(bank(2 * k + 1, NCTX), pw[:, l, k, :], pool_y[:, k, POOL_C:POOL_C + NCTX],
                                       start=True, stop=True)
                    mm.then_inc(pool_done, 1)
                pe.wait_ge(pool_out, 2 * l + 2)
                attention(att_x[l], block1_jobs(0), qst_1, probs_1, keysT_1)
                if both:
                    attention(att_c0, block1_jobs(NX), qst_1, probs_1, keysT_1)
                residual(f"out{l}", 3 * l + 1, a, KC, 2, both)

            def wide(name, c0, n_chunks, s_read, read0, epilogue_banks=4):
                g0 = first[name]
                for c in range(n_chunks):
                    slot = (g0 + c // 2) % RING
                    if c % 2 == 0:
                        landed(slot, (g0 + c // 2) // RING)
                    if c0 + c >= 4:
                        pe.wait_ge(s_read, read0 + c0 + c - 3)
                    w = blocks_of(slot, 2, KC)
                    mm = accumulate(bank(c % 4), [(w[:, c % 2, k, :], h2[:, k, :]) for k in range(KC)])
                    if c % 2 == 1:
                        mm.then_inc(unit_done, 1)

            def hyena():
                for n in range(3):
                    if n == 0:
                        pe.wait_ge(table_in, TAB_FEATS)
                        pe.wait_ge(gate_act, 4)
                        pe.matmul(psum[0:HD, 0:NX], fw[0:33, 0:HD], feats[0:33, :], start=True, stop=True).then_inc(f_mm, 1)
                    else:
                        pe.wait_ge(f_sin, n)
                        pe.matmul(psum[0:HD, 0:NX], fw[0:HD, n * HD:(n + 1) * HD], f_hid[0:HD, :],
                                  start=True, stop=True).then_inc(f_mm, 1)
                pe.wait_ge(f_sin, 3)
                wide("conv_h", 0, 12, conv_in, 0)
                for o in range(2):
                    pe.wait_ge(table_in, TAB_W4[o])
                    if o == 0:
                        pe.wait_ge(conv_in, 12)
                    for t in range(QC):
                        for r in range(2):
                            n = 8 * o + 2 * t + r
                            if n % 8 >= 4:
                                pe.wait_ge(fh_out, n - 3)
                            pe.matmul(bank(n % 4), f_hid[0:HD, t * P:(t + 1) * P], w4[0:HD, r * NX:(r + 1) * NX],
                                      start=True, stop=True).then_inc(fh_mm, 1)
                    pe.wait_ge(table_in, TAB_DFT)
                    pe.wait_ge(fh_ready, 4 * (o + 1))
                    for q in range(4):
                        n = 4 * o + q
                        if q >= 2:
                            pe.wait_ge(ft_out, n - 1)
                        accumulate(bank(2 * (q % 2)), [(dft[:, t, q * P:(q + 1) * P], hf[:, t, :]) for t in range(QC)])
                        accumulate(bank(2 * (q % 2) + 1), [(dft[:, 4 + t, q * P:(q + 1) * P], hb[:, t, :])
                                                           for t in range(QC)]).then_inc(ft_mm, 1)
                    if o == 0:
                        pe.wait_ge(conv_out, 12)
                    else:
                        pe.wait_ge(zi_out, 4)
                    for c in range(4):
                        n = 4 * o + c
                        if c >= 2:
                            pe.wait_ge(zt_out, n - 1)
                        for t in range(QC):
                            mm = pe.transpose(psum[:, 2048 + 512 * (c % 2) + t * P:2048 + 512 * (c % 2) + (t + 1) * P],
                                              vxx[:, c, t * P:(t + 1) * P], ident)
                        mm.then_inc(zt_mm, 1)
                    pe.wait_ge(zt_out, 4 * (o + 1))
                    pe.wait_ge(ft_out, 4 * (o + 1))
                    for q in range(4):
                        n = 4 * o + q
                        if q >= 2:
                            pe.wait_ge(zf_out, n - 1)
                        accumulate(bank(2 * (q % 2)), [(dft[:, t, q * P:(q + 1) * P], z_tok[:, t, :]) for t in range(QC)])
                        accumulate(bank(2 * (q % 2) + 1), [(dft[:, 4 + t, q * P:(q + 1) * P], z_tok[:, t, :])
                                                           for t in range(QC)]).then_inc(zf_mm, 1)
                    pe.wait_ge(zf_out, 4 * (o + 1))
                    for c in range(4):
                        n = 4 * o + c
                        if c >= 2:
                            pe.wait_ge(zi_out, n - 1)
                        accumulate(bank(4 + c % 2),
                                   [(y_re[:, q, c * P:(c + 1) * P], dft[:, 8 + q, :]) for q in range(4)]
                                   + [(y_im[:, q, c * P:(c + 1) * P], dft[:, 12 + q, :]) for q in range(4)]).then_inc(zi_mm, 1)
                wide("ghy_h", 4, 4, gate_mul, 0)

            def merge():
                g0 = first["merge_h"]
                pe.wait_ge(gate_mul, 8)
                for q in range(KC // 2):
                    for j in range(2):
                        c, g = 2 * q + j, g0 + 3 * q + j
                        landed(g % RING, g // RING)
                        if c >= 2:
                            pe.wait_ge(merge_sig, c - 1)
                        w = blocks_of(g % RING, 2, KC)
                        for r in range(2):
                            mm = accumulate(bank(2 * j + r), [(w[:, r, k, :], h2[:, k, :]) for k in range(KC)])
                        mm.then_inc(unit_done, 1)
                    g = g0 + 3 * q + 2
                    landed(g % RING, g // RING)
                    if q >= 1:
                        pe.wait_ge(merge_out, 2 * q)
                    w = blocks_of(g % RING, 4, 4)
                    for j in range(2):
                        for r, y in enumerate((y_attn, vxx)):
                            mm = accumulate(bank(4 + 2 * j + r), [(w[:, 2 * j + r, k, :], y[:, k, :]) for k in range(4)])
                    mm.then_inc(unit_done, 1)
                pe.wait_ge(merge_out, KC)
                g0 = first["out_h"]
                for c in range(KC):
                    g = g0 + c // 2
                    if c % 2 == 0:
                        landed(g % RING, g // RING)
                    if c >= 4:
                        pe.wait_ge(out2_done, c - 3)
                    w = blocks_of(g % RING, 2, KC)
                    mm = accumulate(bank(c % 4), [(w[:, c % 2, k, :], merged[:, k, :]) for k in range(KC)])
                    if c % 2 == 1:
                        mm.then_inc(unit_done, 1)
                sum_chunks(0, res, NX, 2048, out2_done, mean_done)
                sum_chunks(KC * (RMS + 1), res_sq, NX, 3072, sq_done, ss_done)

            pe.nop().then_inc(unit_done, RING)
            pe.wait_ge(consts_in, N_CONSTS)
            pe.wait_ge(setup_done, 1)
            pe.wait_ge(silu_c, 1)
            for l in range(DEPTH):
                if on(f"ada{l}"):
                    if l > 0:
                        pe.wait_ge(res_done, FREE + KC * 3 * l)
                    ada(f"ada{l}", cv[:, :, 0:2], 2)
                if on(f"ffn1_{l}"):
                    pe.wait_ge(mod_ready, l + 1)
                    sum_chunks(KC * 3 * l, a, T, 3072, sq_done, ss_done)
                    pe.wait_ge(normed, KC * (3 * l + 1))
                    ffn_up(f"up1_{l}", 2 * l, True)
                    pe.wait_ge(hid_done, FREE_HID + FC * (2 * l + 1))
                    residual(f"down1_{l}", 3 * l, hid, FC, 1, True)
                if on(f"mix{l}"):
                    sum_chunks(KC * (3 * l + 1), a, T, 3072, sq_done, ss_done)
                    mix(l)
                if on(f"ffn2_{l}"):
                    pe.wait_ge(res_done, FREE + KC * (3 * l + 2))
                    sum_chunks(KC * (3 * l + 2), hid, T if both_in[l] else NX, 3072, sq_done, ss_done)
                    pe.wait_ge(normed, KC * (3 * l + 3))
                    ffn_up(f"up2_{l}", 2 * l + 1, both_in[l])
                    pe.wait_ge(hid_done, FREE_HID + FC * (2 * l + 2))
                    residual(f"down2_{l}", 3 * l + 2, hid, FC, 1, both_in[l])
            if on("final"):
                sum_chunks(KC * (RMS - 1), a, NX, 3072, sq_done, ss_done)
            if on("qkv_h"):
                pe.wait_ge(root_done, RMS)
                ada("ada_h", cv[:, :, 2:3], 1)
                sum_chunks(KC * (RMS - 1), x2, NX, 2048, normed, mean_done_0)
                sum_chunks(KC * RMS, sq2, NX, 3072, sq_done, ss_done)
                pe.wait_ge(normed, KC * (RMS + 1))
                wide("q_h", 0, 12, qk2_out, 0)
                wide("k_h", 12, 12, qk2_out, 0)
                for u in range(6):
                    g = first["v_h"] + u
                    landed(g % RING, g // RING)
                    w = ring[g % RING][:, 0:KC * 256].rearrange("p (k n) -> p k n", k=KC)
                    for t in range(QC):
                        if u >= 1:
                            pe.wait_ge(v2_out, 4 * (u - 1) + t + 1)
                        mm = accumulate(bank(4 + t, 256), [(h2r[:, k, t, :], w[:, k, :]) for k in range(KC)])
                    mm.then_inc(unit_done, 1)
            if on("att_h"):
                pe.wait_ge(qk2_out, 24)
                pe.wait_ge(v2_out, 24)
                jobs = []
                for n in range(NH2):
                    c, rows, cols = n // 2, slice(64 * (n % 2), 64 * (n % 2) + 64), slice(n * HD, (n + 1) * HD)
                    jobs.append((
                        [(c, n % 2, kh[rows, c, :], 0, NX)]
                        + [(4 * g + c, n % 2, kst[rows, 4 * (g - 1) + c, :], NX + (g - 1) * P, NX + g * P) for g in (1, 2)],
                        [vh[:, r, cols] for r in range(RES)] + [vst[:, g, cols] for g in range(2)]))
                attention(att_h, jobs, qst_2, probs_2, keysT_2)
                wide("gattn_h", 0, 4, gate_mul, 0)
            if on("hyena"):
                hyena()
            if on("merge"):
                merge()

        @block.scalar
        def _(act):
            def squares(n, src, dst, width, ready):
                for c in range(KC):
                    ready(c)
                    act.activation(dst[:, c, 0:width], src[:, c, 0:width], ACT.Square).then_inc(sq_done, 1)

            def root(n, dst, width, eps_col):
                act.wait_ge(ss_done, n + 1)
                act.activation(dst[:, 0:width], psum[:, 3072:3072 + width], ACT.Sqrt, scale=1.0 / D,
                               bias=eps_col).then_inc(root_done, 1)

            def modulate(n, src, dst, both, gain_of, shift_of):
                for c in range(KC):
                    act.wait_ge(scaled_done, KC * n + c + 1)
                    ins = act.activation(dst[:, c, 0:NX], src[:, c, 0:NX], ACT.Identity, scale=gain_of(c, 0), bias=shift_of(c, 0))
                    if both:
                        ins = act.activation(dst[:, c, NX:T], src[:, c, NX:T], ACT.Identity, scale=gain_of(c, 1), bias=shift_of(c, 1))
                    ins.then_inc(normed, 1)

            def rms(n, width, gain_of, shift_of):
                def ready(c):
                    if n == 0:
                        return
                    act.wait_ge(res_done, FREE + KC * (n - 1) + c + 1)
                squares(n, h, hid if n % 3 == 2 else a, width, ready)
                root(n, rstd, width, eps[:, 0:1])
                modulate(n, a, a, width > NX, gain_of, shift_of)

            def ffn_gate(name, n, both):
                g0 = first[name]

                def unit(u, g, slot, turn):
                    s = (slot - g0) % 2
                    act.wait_ge(unit_done, g + 1 + RING)
                    act.wait_ge(hid_done, u + (FC * n + 1))
                    ins = act.activation(sil[:, s, 0:NX], bank(3 * s), ACT.Silu)
                    if both:
                        ins = act.activation(sil[:, s, NX:T], bank(3 * s + 2, NCTX), ACT.Silu)
                    ins.then_inc(silu_done, 1)
                for_units(act, plan, name, unit)

            def attention(att, probs, keysT, biased, head_dst):
                NJ, NP = att.jobs, att.pieces
                with act.Fori(0, att.tiles) as i:
                    def exp(j):
                        act.wait_ge(max_done, i * NJ + (att.job0 + j + 1))
                        if j >= 3:
                            act.wait_ge(turned, i * (NJ * NP) + (att.piece0 + (j - 2) * NP))
                        at = att.scores_at(j)
                        src = probs[:, j % 3, 0:att.width] if biased(j) else psum[:, at:at + att.width]
                        act.activation(probs[:, j % 3, 0:att.width], src, ACT.Exp, bias=nmax[:, j % 4:j % 4 + 1],
                                       accum_out=rsum[:, j % 4:j % 4 + 1]).then_inc(exp_done, 1)

                    def take(j):
                        for p in att.on_act:
                            act.wait_ge(turned, i * (NJ * NP) + (att.piece0 + j * NP + p + 1))
                            lo, hi = att.keys_of(p)
                            act.activation(keysT[:, j % 2, lo:hi], psum[:, 2048 + lo:2048 + hi], ACT.Copy).then_inc(turned_act, 1)

                    for j in range(AHEAD):
                        exp(j)
                    take(0)
                    for j in range(NJ):
                        if j + AHEAD < NJ:
                            exp(j + AHEAD)
                        if j + 1 < NJ:
                            take(j + 1)
                        act.wait_ge(heads_done, i * NJ + (att.job0 + j + 1))
                        rows, at = slice(64 * (j % 2), 64 * (j % 2) + 64), 3072 + 512 * (j % 2)
                        act.activation(head_dst(i, j, rows), psum[rows, at:at + P], ACT.Copy).then_inc(heads_out, 1)

            def block1_attention(att, t0, latent):
                def head_dst(i, j, rows):
                    c = j // 2 if j < 4 else 2 + j // 2
                    return a[rows, c, ds(i * P + t0, P)]
                attention(att, probs_1, keysT_1, lambda j: latent and j < 4, head_dst)

            def mix(l):
                g0 = first[f"in{l}"]
                act.wait_ge(upad_ready, l + 1)
                for c in range(NPROJ):
                    act.wait_ge(unit_done, g0 + c // 2 + 1 + RING)
                    b0 = 1024 * (c % 4)
                    if c in (UU, UU + 1):
                        ins = act.activation(upad[:, c - UU, POOL_X:POOL_X + NX], psum[:, b0:b0 + NX], ACT.Copy)
                        if both_in[l]:
                            ins = act.activation(upad[:, c - UU, POOL_C:POOL_C + NCTX], psum[:, b0 + NX:b0 + T], ACT.Copy)
                    else:
                        w = T if keeps_ctx(l, c) else NX
                        ins = act.activation(proj[:, c, 0:w], psum[:, b0:b0 + w], ACT.Copy,
                                             scale=SCORE_SCALE if c in (QA, QA + 1) else 1.0)
                    ins.then_inc(proj_done, 1)
                for n, lo, cols in ((0, 0, 256), (1, 256, 128)):
                    act.wait_ge(unit_done, g0 + 6 + n + 1 + RING)
                    for t in range(T // P):
                        act.activation(v_tok[:, t, lo:lo + cols], bank(t, cols), ACT.Copy).then_inc(proj_done, 1)
                act.wait_ge(proj_done, PER_PROJ * (l + 1))
                for n in range(5):
                    c = QG + n
                    w = T if keeps_ctx(l, c) else NX
                    if n >= 2:
                        act.wait_ge(qk_ss_done, 5 * l + n - 1)
                    act.activation(qk_sq[:, n % 2, 0:w], proj[:, c, 0:w], ACT.Square).then_inc(qk_sq_done, 1)
                    act.wait_ge(qk_ss_done, 5 * l + n + 1)
                    if n >= 2:
                        act.wait_ge(qk_normed, 5 * l + n - 1)
                    act.activation(qk_rs[:, n % 2, 0:w], psum[:, 2048:2048 + w], ACT.Sqrt, scale=1.0 / HD,
                                   bias=eps[:, 0:1]).then_inc(qk_root_done, 1)
                for k in range(2):
                    act.wait_ge(pool_done, 2 * l + k + 1)
                    scale = small[:, 4 * l + k:4 * l + k + 1]
                    ins = act.activation(a[:, 2 + k, 0:NX], bank(2 * k), ACT.Copy, scale=scale)
                    if both_in[l]:
                        ins = act.activation(a[:, 2 + k, NX:T], bank(2 * k + 1, NCTX), ACT.Copy, scale=scale)
                    ins.then_inc(pool_out, 1)
                block1_attention(att_x[l], 0, True)
                if both_in[l]:
                    block1_attention(att_c0, NX, False)

            def gates(name, n0, bias0):
                g0 = first[name]
                for c in range(4):
                    act.wait_ge(unit_done, g0 + c // 2 + 1 + RING)
                    if n0 + c >= 2:
                        act.wait_ge(gate_mul, n0 + c - 1)
                    act.activation(gate_t[:, c % 2, :], bank(c % 4), ACT.Silu,
                                   bias=vec2[:, bias0 + c:bias0 + c + 1]).then_inc(gate_act, 1)

            def hyena():
                for n in range(3):
                    act.wait_ge(f_arg, n + 1)
                    act.activation(f_hid[0:HD, :], f_tmp[0:HD, 0, :], ACT.Sin).then_inc(f_sin, 1)
                act.wait_ge(cpad_zero, 1)
                g0 = first["conv_h"]
                for c in range(12):
                    act.wait_ge(unit_done, g0 + c // 2 + 1 + RING)
                    if c >= 2:
                        act.wait_ge(conv_out, c - 1)
                    act.activation(cpad[:, c % 2, 1:NX + 1], bank(c % 4), ACT.Identity,
                                   bias=vec2[:, OB_IN + 40 + c:OB_IN + 41 + c]).then_inc(conv_in, 1)
                for o in range(2):
                    for q in range(4):
                        act.wait_ge(ft_mm, 4 * o + q + 1)
                        if o == 1 and q == 0:
                            act.wait_ge(zf_out, 4)
                        act.activation(H_re[:, q, :], bank(2 * (q % 2)), ACT.Copy)
                        act.activation(H_im[:, q, :], bank(2 * (q % 2) + 1), ACT.Copy).then_inc(ft_out, 1)
                    for c in range(4):
                        act.wait_ge(zt_mm, 4 * o + c + 1)
                        act.activation(z_tok[:, :, c * P:(c + 1) * P],
                                       bank(4 + c % 2).rearrange("p (t m) -> p t m", t=4), ACT.Copy).then_inc(zt_out, 1)
                gates("ghy_h", 4, OB_IN + 52)

            def merge():
                g0 = first["merge_h"]
                for c in range(KC):
                    act.wait_ge(unit_done, g0 + 3 * (c // 2) + c % 2 + 1 + RING)
                    if c >= 2:
                        act.wait_ge(merge_out, c - 1)
                    for r in range(2):
                        b = OB_IN + 56 + 8 * r + c
                        ins = act.activation(sg_t[:, c % 2, r * NX:(r + 1) * NX], bank(2 * (c % 2) + r), ACT.Sigmoid,
                                             bias=vec2[:, b:b + 1])
                    ins.then_inc(merge_sig, 1)
                squares(RMS + 1, res, res_sq, NX, lambda c: act.wait_ge(centred, KC + c + 1))
                root(RMS + 1, sg_t[:, 0, 0:NX], NX, eps[:, 1:2])
                modulate(RMS + 1, res, fin, False, lambda c, s: vec2[:, OLG + c:OLG + c + 1],
                         lambda c, s: vec2[:, OLB + c:OLB + c + 1])

            act.wait_ge(consts_in, N_CONSTS)
            act.wait_ge(setup_done, 1)
            act.activation(cv[:, :, 0:2], cv[:, :, 0:2], ACT.Silu).then_inc(silu_c, 1)
            for l in range(DEPTH):
                def gain_of(k):
                    return lambda c, s: gainv[:, k, c, s:s + 1]

                def shift_of(k):
                    return lambda c, s: mod[l][:, 3 * k, c, s:s + 1]
                if on(f"ffn1_{l}"):
                    act.wait_ge(mod_ready, l + 1)
                    rms(3 * l, T, gain_of(0), shift_of(0))
                    ffn_gate(f"up1_{l}", 2 * l, True)
                if on(f"mix{l}"):
                    rms(3 * l + 1, T, gain_of(1), shift_of(1))
                    mix(l)
                if on(f"ffn2_{l}"):
                    rms(3 * l + 2, T if both_in[l] else NX, gain_of(2), shift_of(2))
                    ffn_gate(f"up2_{l}", 2 * l + 1, both_in[l])
            if on("final"):
                n = RMS - 1
                squares(n, h, a, NX, lambda c: act.wait_ge(res_done, FREE + KC * (n - 1) + c + 1))
                root(n, rstd, NX, eps[:, 0:1])
                modulate(n, x2, x2, False, lambda c, s: final_g[:, c:c + 1], lambda c, s: 0.0)
            if on("qkv_h"):
                squares(RMS, h2, sq2, NX, lambda c: act.wait_ge(centred, c + 1))
                root(RMS, rstd2, NX, eps[:, 1:2])
                modulate(RMS, h2, h2, False, lambda c, s: gain2[:, c:c + 1], lambda c, s: mod2[:, c:c + 1])
                for c in range(24):
                    act.wait_ge(unit_done, first["q_h"] + c // 2 + 1 + RING)
                    dst = (qh if c < 12 else kh)[:, c % 12, :].rearrange("p (r u) -> p u r", r=RES)
                    src = bank(c % 4).rearrange("p (u r) -> p u r", r=RES)
                    if c < 12:
                        act.activation(dst, src, ACT.Identity, scale=SCORE_SCALE,
                                       bias=bq[:, c:c + 1]).then_inc(qk2_out, 1)
                    else:
                        act.activation(dst, src, ACT.Identity,
                                       bias=vec2[:, OB_IN + c:OB_IN + c + 1]).then_inc(qk2_out, 1)
            if on("att_h"):

                def head_dst(i, j, rows):
                    by_residue = y_attn[rows, j // 2, :].rearrange("p (u r) -> p r u", r=RES)
                    return by_residue[:, ds(i, 1), :].rearrange("p a u -> p (a u)")
                attention(att_h, probs_2, keysT_2, lambda j: True, head_dst)
                gates("gattn_h", 0, OB_IN + 36)
            if on("hyena"):
                hyena()
            if on("merge"):
                merge()

        @block.vector
        def _(dve):
            own = Chain(dve, dve_own)

            def modulation(l):
                dve.wait_ge(unit_done, after[f"ada{l}"] + RING)
                n = NMOD * KC * 2
                own.link(dve.tensor_tensor(mods[l][:], psum[:, 3584:3584 + n], b_ada[:, l * n:(l + 1) * n], ALU.add))
                for k in range(3):
                    own.mark(dve.scalar_tensor_tensor(gainv[:, k, :, :], mod[l][:, 3 * k + 1, :, :], 1.0, ngv[:, l, k, :, :],
                                                      ALU.add, ALU.mult))
                for k, m in ((0, 2), (1, 8)):
                    ins = dve.tensor_scalar(hgate[:, k, :, :], mod[l][:, m, :, :], 0.5, None, ALU.mult)
                    if k == 0:
                        own.mark(ins)
                ins.then_inc(mod_ready, 1)

            def scale_rows(n, src, dst, root_ap, width):
                dve.wait_ge(root_done, n + 1)
                own.link(dve.reciprocal(root_ap[:, 0:width], root_ap[:, 0:width]))
                for c in range(KC):
                    dve.tensor_tensor(dst[:, c, 0:width], src[:, c, 0:width], root_ap[:, 0:width], ALU.mult)\
                       .then_inc(scaled_done, 1)

            def ffn_product(name, n, both):
                g0 = first[name]

                def unit(u, g, slot, turn):
                    s = (slot - g0) % 2
                    dve.wait_ge(silu_done, u + (FC * n + 1))
                    out_x = hid[:, ds(u, 1), 0:NX].rearrange("p a n -> p (a n)")
                    ins = dve.tensor_tensor(out_x, sil[:, s, 0:NX], bank(3 * s + 1), ALU.mult)
                    if both:
                        out_c = hid[:, ds(u, 1), NX:T].rearrange("p a n -> p (a n)")
                        at = (3 * s + 2) * 512 + NCTX
                        ins = dve.tensor_tensor(out_c, sil[:, s, NX:T], psum[:, at:at + NCTX], ALU.mult)
                    ins.then_inc(hid_done, 1)
                for_units(dve, plan, name, unit)

            def add_residual(name, n, per_unit, gate_at, both):
                g0 = first[name]

                def unit(u, g, slot, turn):
                    dve.wait_ge(unit_done, g + 1 + RING)
                    for j in range(per_unit):
                        s = (slot - g0) % 2 * per_unit + j
                        m = u * per_unit + j
                        hx = h[:, ds(m, 1), 0:NX].rearrange("p a n -> p (a n)")
                        ins = dve.scalar_tensor_tensor(hx, bank(2 * s), gate_at(m, 0), hx, ALU.mult, ALU.add)
                        if both:
                            hc = h[:, ds(m, 1), NX:T].rearrange("p a n -> p (a n)")
                            ins = dve.scalar_tensor_tensor(hc, bank(2 * s + 1, NCTX), gate_at(m, 1), hc, ALU.mult, ALU.add)
                        ins.then_inc(res_done, 1)
                for_units(dve, plan, name, unit)

            def attention(att, staged, probs, keysT, bias):
                NJ, NP = att.jobs, att.pieces
                with dve.Fori(0, att.tiles) as i:
                    own.enter(i, att.own_steps)

                    def row_max(j):
                        dve.wait_ge(scores_done, i * NJ + (att.job0 + j + 1))
                        if bias(i, j):
                            src = probs[:, j % 3, 0:att.width]
                            own.wait()
                        else:
                            at = att.scores_at(j)
                            src = psum[:, at:at + att.width]
                        dve.tensor_reduce(nmax[:, j % 4:j % 4 + 1], src, AX.X, ALU.max, negate=True).then_inc(max_done, 1)

                    def normalise(j):
                        dve.wait_ge(exp_done, i * NJ + (att.job0 + j + 1))
                        own.link(dve.reciprocal(rinv[:, j % 4:j % 4 + 1], rsum[:, j % 4:j % 4 + 1]))
                        p = probs[:, j % 3, 0:att.width]
                        dve.tensor_scalar(p, p, rinv[:, j % 4:j % 4 + 1], None, ALU.mult).then_inc(probs_ready, 1)

                    def take(j):
                        for p in att.on_dve:
                            dve.wait_ge(turned, i * (NJ * NP) + (att.piece0 + j * NP + p + 1))
                            lo, hi = att.keys_of(p)
                            dve.tensor_copy(keysT[:, j % 2, lo:hi], psum[:, 2048 + lo:2048 + hi]).then_inc(turned_dve, 1)

                    copies = staged(i)
                    for n, (dst, src) in enumerate(copies):
                        ins = dve.tensor_copy(dst, src)
                        if n < len(copies) - 1:
                            own.mark(ins)
                    ins.then_inc(q_staged, 1)
                    row_max(0)
                    row_max(1)
                    normalise(0)
                    row_max(2)
                    take(0)
                    for j in range(NJ):
                        if j + 1 < NJ:
                            normalise(j + 1)
                        if j + AHEAD < NJ:
                            row_max(j + AHEAD)
                        if j + 1 < NJ:
                            take(j + 1)
                    dve.wait_ge(heads_done, i * NJ + (att.job0 + NJ))
                    own.leave(att.tiles)

            def turned_before(att, i, j):
                if j >= 3:
                    dve.wait_ge(turned, i * (att.jobs * att.pieces) + (att.piece0 + (j - 2) * att.pieces))

            def block1_attention(att, l, t0, latent):
                def staged(i):
                    return [(qst_1[:, 0:2, :], proj[:, QA:QA + 2, ds(i * P + t0, P)]),
                            (qst_1[:, 2:6, :], proj[:, QG:QG + 4, ds(i * P + t0, P)])]

                def bias(i, j):
                    if not latent or j >= 4:
                        return False
                    turned_before(att, i, j)
                    at = att.scores_at(j)
                    own.mark(dve.tensor_tensor(probs_1[:, j % 3, 0:NX], psum[:, at:at + NX],
                                               rpb[:, j, ds(i * (-2 * GRID) + 7 * GRID, NX)], ALU.add))
                    own.mark(dve.tensor_copy(probs_1[:, j % 3, NX:T], psum[:, at + NX:at + T]))
                    return True
                attention(att, staged, probs_1, keysT_1, bias)

            def qk_norm(l):
                for n in range(5):
                    c = QG + n
                    w = T if keeps_ctx(l, c) else NX
                    gain_col = qkg[:, 2 * l + (c == KG):2 * l + (c == KG) + 1]
                    dve.wait_ge(qk_root_done, 5 * l + n + 1)
                    own.link(dve.reciprocal(qk_rs[:, n % 2, 0:w], qk_rs[:, n % 2, 0:w]))
                    dve.scalar_tensor_tensor(proj[:, c, 0:w], proj[:, c, 0:w], gain_col, qk_rs[:, n % 2, 0:w],
                                             ALU.mult, ALU.mult).then_inc(qk_normed, 1)
                    dve.wait_ge(qk_normed, 5 * l + n + 1)
                    dve.wait_ge(qk_rotated, 5 * l + n + 1)
                    own.mark(dve.tensor_tensor(rope_t[:, 0, :], proj[:, c, 0:NX], cos_t, ALU.mult))
                    own.link(dve.tensor_tensor(rope_t[:, 1, :], bank(6 + n % 2), sin_t, ALU.mult))
                    dve.tensor_tensor(proj[:, c, 0:NX], rope_t[:, 0, :], rope_t[:, 1, :], ALU.add).then_inc(qk_roped, 1)
                    if n == 4:
                        dve.wait_ge(qk_roped, 5 * (l + 1))

            def pooling(l):
                w = POOL_W if both_in[l] else PAD + NX + PAD
                add = ALU.add
                own.link(dve.tensor_tensor(win2[:, :, 1:w], upad[:, :, 1:w], upad[:, :, 0:w - 1], add))
                own.link(dve.tensor_tensor(win4[:, :, 2:w - 1], win2[:, :, 1:w - 2], win2[:, :, 3:w], add))
                own.link(dve.tensor_tensor(win8[:, 4:w - 3], win4[:, 1, 2:w - 5], win4[:, 1, 6:w - 1], add))
                own.link(dve.tensor_tensor(win16[:, 8:w - 7], win8[:, 4:w - 11], win8[:, 12:w - 3], add))
                lo, hi = PAD, w - PAD
                for k, half, win in ((0, 0, win2[:, 0, :]), (0, 1, win4[:, 0, :]), (1, 0, win8), (1, 1, win16)):
                    q = slice(64 * half, 64 * half + 64)
                    own.link(dve.tensor_tensor(pool_y[q, k, lo:hi], win[q, lo:hi], pool_inv[q, k, lo:hi], ALU.mult))
                    ins = dve.tensor_tensor(pool_y[q, k, lo:hi], pool_y[q, k, lo:hi], upad[q, k, lo:hi], ALU.subtract)
                    if half == 0:
                        own.mark(ins)
                    else:
                        ins.then_inc(pool_ready, 1)

            def mix(l):
                dve.wait_ge(scaled_done, KC * (3 * l + 2))
                dve.memset(upad, 0.0).then_inc(upad_ready, 1)
                dve.wait_ge(table_in, TAB_MIX[l])
                qk_norm(l)
                pooling(l)
                dve.wait_ge(proj_done, PER_PROJ * (l + 1))
                dve.wait_ge(pool_done, 2 * l + 2)
                block1_attention(att_x[l], l, 0, True)
                if both_in[l]:
                    block1_attention(att_c0, l, NX, False)

            def gates(n0, dst):
                for c in range(4):
                    dve.wait_ge(gate_act, n0 + c + 1)
                    dve.tensor_tensor(dst[:, c, :], dst[:, c, :], gate_t[:, c % 2, :], ALU.mult).then_inc(gate_mul, 1)

            def hyena():
                freq = fw[0:HD, 3 * HD:3 * HD + 1]
                for n in range(3):
                    dve.wait_ge(f_mm, n + 1)
                    arg, turns, rest = (f_tmp[0:HD, k, :] for k in range(3))
                    own.link(dve.tensor_scalar(rest, psum[0:HD, 0:NX], fw[0:HD, 3 * HD + 1 + n:3 * HD + 2 + n], freq,
                                               ALU.add, ALU.mult))
                    own.link(dve.tensor_scalar(turns, rest, 1 / (2 * math.pi), ROUND_MAGIC, ALU.mult, ALU.add))
                    own.link(dve.tensor_scalar(turns, turns, -ROUND_MAGIC, None, ALU.add))
                    own.link(dve.scalar_tensor_tensor(rest, turns, -TWO_PI_HI, rest, ALU.mult, ALU.add))
                    own.link(dve.scalar_tensor_tensor(rest, turns, -TWO_PI_LO, rest, ALU.mult, ALU.add))
                    dve.tensor_scalar(arg, rest, PI_BELOW, -PI_BELOW, ALU.min, ALU.max).then_inc(f_arg, 1)
                dve.wait_ge(f_sin, 3)
                own.mark(dve.memset(cpad[:, :, 0:1], 0.0))
                dve.memset(cpad[:, :, NX + 1:NX + 2], 0.0).then_inc(cpad_zero, 1)
                for c in range(12):
                    dve.wait_ge(conv_in, c + 1)

                    def tap(k):
                        return vec2[:, OCW + 12 * k + c:OCW + 12 * k + c + 1]
                    own.link(dve.tensor_scalar(vxx[:, c, :], cpad[:, c % 2, 0:NX], tap(0), vec2[:, OCB + c:OCB + c + 1],
                                               ALU.mult, ALU.add))
                    own.link(dve.scalar_tensor_tensor(vxx[:, c, :], cpad[:, c % 2, 1:NX + 1], tap(1), vxx[:, c, :],
                                                      ALU.mult, ALU.add))
                    dve.scalar_tensor_tensor(vxx[:, c, :], cpad[:, c % 2, 2:NX + 2], tap(2), vxx[:, c, :],
                                             ALU.mult, ALU.add).then_inc(conv_out, 1)
                dve.wait_ge(conv_out, 12)
                dve.wait_ge(table_in, TAB_W4[0])
                for o in range(2):
                    for t in range(QC):
                        for r, dst in enumerate((hf, hb)):
                            n = 8 * o + 2 * t + r
                            dve.wait_ge(fh_mm, n + 1)
                            if o == 1:
                                dve.wait_ge(zi_mm, 4)
                            dve.tensor_tensor(dst[:, t, :], bank(n % 4), decay[:, t, :], ALU.mult).then_inc(fh_out, 1)
                        dve.wait_ge(fh_out, 8 * o + 2 * t + 2)
                        if t == 0:
                            own.link(dve.memset(hb[0:1, 0, :], 0.0))
                        own.link(dve.tensor_tensor(mul_t[:, 0, :], hb[:, t, :], hf[:, t, :], ALU.subtract))
                        own.link(dve.tensor_tensor(hf[:, t, :], hf[:, t, :], hb[:, t, :], ALU.add))
                        dve.tensor_copy(hb[:, t, :], mul_t[:, 0, :]).then_inc(fh_ready, 1)
                    for q in range(4):
                        if q > 0:
                            dve.wait_ge(zf_out, 4 * o + q)
                        dve.wait_ge(zf_mm, 4 * o + q + 1)
                        dve.wait_ge(ft_out, 4 * o + q + 1)
                        A, B = bank(2 * (q % 2)), bank(2 * (q % 2) + 1)
                        own.mark(dve.tensor_tensor(mul_t[:, 0, :], H_re[:, q, :], A, ALU.mult))
                        own.link(dve.tensor_tensor(mul_t[:, 1, :], H_im[:, q, :], B, ALU.mult))
                        own.link(dve.tensor_tensor(y_re[:, q, :], mul_t[:, 0, :], mul_t[:, 1, :], ALU.add))
                        own.mark(dve.tensor_tensor(mul_t[:, 0, :], H_re[:, q, :], B, ALU.mult))
                        own.link(dve.tensor_tensor(mul_t[:, 1, :], H_im[:, q, :], A, ALU.mult))
                        dve.tensor_tensor(y_im[:, q, :], mul_t[:, 0, :], mul_t[:, 1, :], ALU.subtract).then_inc(zf_out, 1)
                    dve.wait_ge(zf_out, 4 * (o + 1))
                    for c in range(4):
                        dve.wait_ge(zi_mm, 4 * o + c + 1)
                        fb = vec2[:, OFB + 4 * o + c:OFB + 4 * o + c + 1]
                        own.link(dve.scalar_tensor_tensor(mul_t[:, c % 2, :], vxx[:, c, :], fb, bank(4 + c % 2),
                                                          ALU.mult, ALU.add))
                        dve.tensor_tensor(vxx[:, c, :], mul_t[:, c % 2, :], vxx[:, 4 + 4 * o + c, :], ALU.mult)\
                           .then_inc(zi_out, 1)
                    dve.wait_ge(zi_out, 4 * (o + 1))
                gates(4, vxx)

            def merge():
                g0 = first["merge_h"]
                for c in range(KC):
                    dve.wait_ge(merge_sig, c + 1)
                    dve.wait_ge(unit_done, g0 + 3 * (c // 2) + 3 + RING)
                    if c > 0:
                        dve.wait_ge(merge_out, c)
                    for r in range(2):
                        own.mark(dve.tensor_tensor(mt_t[:, r, :], sg_t[:, c % 2, r * NX:(r + 1) * NX],
                                                   bank(4 + 2 * (c % 2) + r), ALU.mult))
                    own.wait()
                    dve.tensor_tensor(merged[:, c, :], mt_t[:, 0, :], mt_t[:, 1, :], ALU.add).then_inc(merge_out, 1)
                g0 = first["out_h"]
                for c in range(KC):
                    dve.wait_ge(unit_done, g0 + c // 2 + 1 + RING)
                    own.link(dve.tensor_scalar(mt_t[:, c % 2, :], bank(c % 4), vec2[:, OBO + c:OBO + c + 1],
                                               mod2[:, 2 * KC + c:2 * KC + c + 1], ALU.add, ALU.mult))
                    dve.scalar_tensor_tensor(res[:, c, :], x2[:, c, :], ALPHA, mt_t[:, c % 2, :], ALU.mult, ALU.add)\
                       .then_inc(out2_done, 1)
                dve.wait_ge(out2_done, KC)
                dve.wait_ge(mean_done, 1)
                centre(res, res)
                scale_rows(RMS + 1, res, res, sg_t[:, 0, :], NX)

            def centre(src, dst):
                for c in range(KC):
                    dve.scalar_tensor_tensor(dst[:, c, :], bank(4), -1.0 / D, src[:, c, :], ALU.mult, ALU.add)\
                       .then_inc(centred, 1)

            own.mark(dve.memset(eps[:, 0:1], EPS))
            own.mark(dve.memset(eps[:, 1:2], LN_EPS))
            own.mark(dve.memset(ones[:, 0:1], 1.0))
            dve.memset(ones[:, 1:2], 1.0).then_inc(hid_done, FREE_HID)
            dve.memset(ones[:, 2:3], 1.0).then_inc(res_done, FREE)
            dve.wait_ge(consts_in, N_CONSTS)
            for l in range(DEPTH):
                own.mark(dve.tensor_scalar(qkg[:, 2 * l:2 * l + 1], small[:, 4 * l + 2:4 * l + 3], SCORE_SCALE, None, ALU.mult))
                own.mark(dve.tensor_copy(qkg[:, 2 * l + 1:2 * l + 2], small[:, 4 * l + 3:4 * l + 4]))
            own.mark(dve.tensor_scalar(bq[:], vec2[:, OB_IN:OB_IN + 12], SCORE_SCALE, None, ALU.mult))
            own.wait()
            dve.memset(ones[:], 1.0).then_inc(setup_done, 1)
            for l in range(DEPTH):
                if on(f"ada{l}"):
                    modulation(l)
                gate = mod[l][:, 5, :, :]

                def half_of(k):
                    return lambda m, s: hgate[:, k, ds(m, 1), s:s + 1].rearrange("p a b -> p (a b)")

                if on(f"ffn1_{l}"):
                    dve.wait_ge(mod_ready, l + 1)
                    scale_rows(3 * l, h, a, rstd, T)
                    ffn_product(f"up1_{l}", 2 * l, True)
                    add_residual(f"down1_{l}", 3 * l, 1, half_of(0), True)
                if on(f"mix{l}"):
                    dve.wait_ge(res_done, FREE + KC * (3 * l + 1))
                    scale_rows(3 * l + 1, h, a, rstd, T)
                    mix(l)
                    add_residual(f"out{l}", 3 * l + 1, 2,
                                 lambda m, s: gate[:, ds(m, 1), s:s + 1].rearrange("p a b -> p (a b)"), both_in[l])
                if on(f"ffn2_{l}"):
                    dve.wait_ge(res_done, FREE + KC * (3 * l + 2))
                    scale_rows(3 * l + 2, h, a, rstd, T if both_in[l] else NX)
                    ffn_product(f"up2_{l}", 2 * l + 1, both_in[l])
                    add_residual(f"down2_{l}", 3 * l + 2, 1, half_of(1), both_in[l])
                    dve.wait_ge(res_done, FREE + KC * (3 * l + 3))
            if on("final"):
                scale_rows(RMS - 1, h, x2, rstd, NX)
            if on("qkv_h"):
                dve.wait_ge(unit_done, after["ada_h"] + RING)
                own.link(dve.tensor_tensor(mod2[:], psum[:, 3584:3608], vec2[:, OB_ADA:OB_ADA + 24], ALU.add))
                own.link(dve.tensor_scalar(gain2[:], mod2[:, KC:2 * KC], 1.0, None, ALU.add))
                dve.wait_ge(mean_done_0, 1)
                centre(x2, h2)
                dve.wait_ge(centred, KC)
                scale_rows(RMS, h2, h2, rstd2, NX)
                dve.wait_ge(table_in, TAB_QKV)
                for u in range(6):
                    dve.wait_ge(unit_done, first["v_h"] + u + 1 + RING)
                    for t in range(QC):
                        dve.tensor_tensor(vh[:, t, 256 * u:256 * (u + 1)], bank(4 + t, 256), vbias[:, 256 * u:256 * (u + 1)],
                                          ALU.add).then_inc(v2_out, 1)
            if on("att_h"):
                dve.wait_ge(qk2_out, 24)
                dve.wait_ge(v2_out, 24)

                def staged(i):
                    return [(qst_2, qh[:, :, ds(i * P, P)]), (kst, kh[:, 4:12, ds(i * P, P)]),
                            (vst, vh[:, ds(i, 1), 512:1536].rearrange("p a (g n) -> p (a g) n", g=2))]

                def bias(i, j):
                    turned_before(att_h, i, j)
                    at, p = att_h.scores_at(j), probs_2[:, j % 3, :]
                    slope = 2.0 ** -(j + 1)
                    own.mark(dve.scalar_tensor_tensor(p[:, 0:NX], alibi[:, ds(i * (-P) + 3 * P, NX)], slope,
                                                      psum[:, at:at + NX], ALU.mult, ALU.add))
                    own.mark(dve.scalar_tensor_tensor(p[:, NX:KEYS2], alibi[:, 7 * P:9 * P], slope,
                                                      psum[:, at + NX:at + KEYS2], ALU.mult, ALU.add))
                    return True
                attention(att_h, staged, probs_2, keysT_2, bias)
                gates(0, y_attn)
            if on("hyena"):
                hyena()
            if on("merge"):
                merge()


def constants():
    t = np.arange(NX)
    inv = (10000.0 ** (-np.arange(0, HD // 2, 2, dtype=np.float32) / np.float32(HD // 2))).astype(np.float32)
    ang = np.stack([(t // GRID).astype(np.float32)[:, None] * inv, (t % GRID).astype(np.float32)[:, None] * inv])
    c64 = np.concatenate([np.cos(ang[0]), np.cos(ang[0]), np.cos(ang[1]), np.cos(ang[1])], 1).T
    s64 = np.concatenate([-np.sin(ang[0]), np.sin(ang[0]), -np.sin(ang[1]), np.sin(ang[1])], 1).T
    cos_t, sin_t = (np.concatenate([x, x]).astype(np.float32) for x in (c64, s64))
    rot = np.zeros((P, P), np.float32)
    for i in range(P):
        rot[i ^ 16, i] = 1.0
    pairs = np.kron(np.eye(2), np.ones((HD, HD))).astype(np.float32)
    cst = np.concatenate([np.eye(P, dtype=np.float32), rot, pairs], 1)
    inv_count = np.zeros((P, 2, POOL_W), np.float32)
    for n, at in ((NX, POOL_X), (NCTX, POOL_C)):
        s = np.arange(n)
        for g, w in enumerate((2, 4, 8, 16)):
            count = np.clip(s - w // 2 + w, 0, n) - np.clip(s - w // 2, 0, n)
            inv_count[64 * (g % 2):64 * (g % 2) + 64, g // 2, at:at + n] = 1.0 / count
    alibi = np.full((P, 9, P), NEG, np.float32)
    step = np.arange(P)[None, :] - np.arange(P)[:, None]
    for k in range(7):
        dist = np.abs(RES * step + k - 3)
        alibi[:, k][dist <= 64] = -dist[dist <= 64]
    for k, dil in ((7, 4), (8, 16)):
        dist = np.abs(RES * step)
        valid = (dist % dil == 0) & (dist <= 64 * dil)
        alibi[:, k][valid] = -dist[valid]
    alibi = alibi.reshape(P, 9 * P)
    tl = np.linspace(0.0, 1.0, NX, dtype=np.float32)[:, None]
    w = (np.float32(2.0 * math.pi) * np.arange(NX, dtype=np.float32)[:, None] / np.float32(NX)).astype(np.float32)
    f = np.linspace(1e-4, 15, 16, dtype=np.float32)[None, :]
    fw_ = (f * w).astype(np.float32)
    feats = np.concatenate([tl, np.cos(fw_), -np.sin(fw_)], 1).T.astype(np.float32)
    deltas = np.linspace(math.log(1e-2) / 1.5, math.log(1e-2) / 0.3, NX, dtype=np.float32)
    decay = np.exp(-tl * np.abs(deltas)[None, :]).astype(np.float32)
    th = np.pi * (2 * np.arange(NX)[None, :] + 1) * np.arange(NX)[:, None] / (2 * NX)
    def tiles(m):
        return m.reshape(4, P, NX).transpose(1, 0, 2).astype(np.float32)
    dft = np.concatenate([tiles(np.cos(th)), tiles(np.sin(th)), tiles(np.cos(th.T) / NX), tiles(np.sin(th.T) / NX)], 1)
    return dict(cos_t=cos_t, sin_t=sin_t, cst=cst, pool_inv=inv_count, alibi=alibi, feats=np.ascontiguousarray(feats),
                decay=tiles(decay), dft=np.ascontiguousarray(dft))


def blocked(w, cols_per_unit):
    k, m = w.shape
    v = w.reshape(k // P, P, m // P // cols_per_unit, cols_per_unit, P)
    return np.ascontiguousarray(v.transpose(2, 1, 3, 0, 4)).reshape(m // P // cols_per_unit, P, -1)


def as_rhs(w, cols):
    k, m = w.shape
    v = w.reshape(k // P, P, m // cols, cols)
    return np.ascontiguousarray(v.transpose(2, 1, 0, 3)).reshape(m // cols, P, -1)


def columns(v):
    return v.reshape(-1, P).T


def layout(inputs):
    x = {k: np.asarray(v) for k, v in inputs.items()}
    d = dict(constants())
    d["xT"] = x["x"][0].T.reshape(KC, P, NX).transpose(1, 0, 2)
    d["ctxT"] = x["ctx"][0].T.reshape(KC, P, NCTX).transpose(1, 0, 2)
    d["cvec"] = np.stack([columns(x["c"][0]), columns(x["c_ctx"]), columns(x["c_2"][0])], 2).reshape(P, -1)
    d["b_ada"] = np.repeat(np.concatenate([columns(x["b_ada"][l]) for l in range(DEPTH)], 1), 2, axis=1)
    d["ng"] = np.concatenate([np.repeat(np.concatenate([columns(x["norm_g"][l, k]) for l in range(DEPTH) for k in range(3)], 1),
                                        2, axis=1), columns(x["final_g"])], 1)
    small = []
    for l in range(DEPTH):
        small += [columns(x["pool_scale"][l]), np.tile(x["q_norm_g"][l], 2)[:, None], np.tile(x["k_norm_g"][l], 2)[:, None]]
    d["small"] = np.concatenate(small, 1)
    poolw = np.zeros((P, DEPTH, 2, P), np.float32)
    for l in range(DEPTH):
        for g in range(4):
            r = 64 * (g % 2)
            poolw[r:r + 64, l, g // 2, r:r + 64] = x["pool_w"][l, g]
    d["poolw"] = poolw.reshape(P, -1)
    d["vec2"] = np.concatenate(
        [columns(x["b_ada_2"][0]), columns(x["b_in_2"][0])] + [columns(x["conv_w_2"][0, k]) for k in range(3)]
        + [columns(x["conv_b_2"][0])] + [columns(x["filt_bias_2"][0, o]) for o in range(2)]
        + [columns(x["b_out_2"][0]), columns(x["ln_g_2"][0]), columns(x["ln_b_2"][0])], 1)
    fw = np.zeros((HD, 3 * HD + 4), np.float32)
    fw[0:33, 0:HD] = x["filt_w1_2"][0]
    fw[:, HD:2 * HD], fw[:, 2 * HD:3 * HD] = x["filt_w2_2"][0], x["filt_w3_2"][0]
    for k, name in enumerate(("filt_freq_2", "filt_b1_2", "filt_b2_2", "filt_b3_2")):
        fw[:, 3 * HD + k] = x[name][0]
    d["fw"] = fw
    d["w4_0"], d["w4_1"] = x["filt_w4_2"][0][:, 0:2 * NX], x["filt_w4_2"][0][:, 2 * NX:4 * NX]
    order = np.concatenate([np.arange(HD) + HD * n for i in range(4) for n in (i, 4 + i)])
    col = np.arange(GRID)
    c0 = np.clip(col - 8, 0, GRID - 16)
    seen = (col[None, :] >= c0[:, None]) & (col[None, :] < c0[:, None] + 16)
    dx = np.clip(col[None, :] - col[:, None], -15, 15) + 15
    for l in range(DEPTH):
        wi = x["w_in"][l]
        d[f"ada{l}"] = blocked(x["w_ada"][l], 2)
        for k in (1, 2):
            up = x[f"ffn{k}_up"][l]
            pairs = np.stack([up[:, :FF].reshape(D, FC, P), up[:, FF:].reshape(D, FC, P)], 2).reshape(D, 2 * FF)
            d[f"up{k}_{l}"] = blocked(pairs, 2)
            d[f"down{k}_{l}"] = blocked(x[f"ffn{k}_down"][l], 1)
        u = np.zeros((8, P, 2 * D), np.float32)
        u[0:5] = blocked(np.concatenate([wi[:, 0:512], wi[:, 768:1024], wi[:, 1024:1536][:, order]], 1), 2)
        u[5, :, 0:D] = blocked(wi[:, 1536:1664], 1)[0]
        u[6] = as_rhs(wi[:, 512:768], 256)[0]
        u[7, :, 0:D] = as_rhs(wi[:, 1664:1792], 128)[0]
        d[f"in{l}"] = u
        wo = x["w_out"][l]
        d[f"out{l}"] = blocked(np.concatenate([wo[0:512], wo[512:1024][order]], 0), 2)
        table = np.where(seen[None, None], x["na_rpb"][l][:, :, dx], np.float32(NEG)).transpose(2, 0, 1, 3)
        rpb = np.zeros((P, 4, 15, GRID), np.float32)
        rpb[0:64] = table
        rpb[64:128, :, 1:15] = table[:, :, 0:14]
        d[f"rpb{l}"] = rpb.reshape(P, 4, 15 * GRID)
    w2 = x["w_in_2"][0]
    d["ada_h"] = blocked(x["w_ada_2"][0], 2)
    d["q_h"], d["k_h"] = blocked(w2[:, 0:1536], 2), blocked(w2[:, 1536:3072], 2)
    d["v_h"] = as_rhs(w2[:, 3072:4608], 256)
    d["vbias"] = np.broadcast_to(x["b_in_2"][0][3072:4608], (P, 1536))
    d["gattn_h"] = blocked(w2[:, 4608:5120], 2)
    d["conv_h"] = blocked(w2[:, 5120:6656], 2)
    d["ghy_h"] = blocked(w2[:, 6656:7168], 2)
    r = np.stack([w2[:, 7168:8192].reshape(D, KC, P), w2[:, 8192:9216].reshape(D, KC, P)], 2).reshape(D, 2 * D)
    r = blocked(r, 2)
    pj = np.stack([x["w_proj_attn_2"][0].reshape(512, KC, P), x["w_proj_hyena_2"][0].reshape(512, KC, P)], 2).reshape(512, 2 * D)
    pj = blocked(pj, 4)
    m = np.zeros((12, P, 2 * D), np.float32)
    for q in range(4):
        m[3 * q], m[3 * q + 1], m[3 * q + 2] = r[2 * q], r[2 * q + 1], pj[q]
    d["merge_h"] = m
    d["out_h"] = blocked(x["w_out_2"][0], 2)
    return {k: np.ascontiguousarray(v) for k, v in d.items()}


def kernel(**inputs):
    import concourse.bacc as bacc
    from concourse.bass_utils import run_bass_kernel_spmd

    arrays = layout(inputs)
    nc = bacc.Bacc("TRN2", target_bir_lowering=False, num_devices=1)
    io = {k: nc.dram_tensor(f"in_{k}", v.shape, mybir.dt.from_np(v.dtype), kind="ExternalInput").ap()
          for k, v in arrays.items()}
    out = nc.dram_tensor("out_T", (KC, P, NX), F32, kind="ExternalOutput").ap()
    hybrid_kernel(nc, io, out)
    r = run_bass_kernel_spmd(nc, [{f"in_{k}": v for k, v in arrays.items()}], core_ids=[0])
    return r.results[0]["out_T"].reshape(D, NX).T.reshape(1, NX, D)
```

```python
import math
from contextlib import ExitStack

import numpy as np

import concourse.bass as bass
from concourse import mybir

F32 = mybir.dt.float32
F32R = mybir.dt.float32r
ALU = mybir.AluOpType
ACT = mybir.ActivationFunctionType
AX = mybir.AxisListType
ds = bass.ds

P = 128
D = 1024
KC = D // P
NX, NCTX = 512, 256
T = NX + NCTX
DEPTH = 2
FF = 2816
FC = FF // P
NMOD = 9
HD = 64
EPS, LN_EPS = 1e-6, 1e-5
GRID = 64
NEG = -1e30
SCORE_SCALE = HD ** -0.5
PAD = 16
POOL_X, POOL_C, POOL_W = PAD, 2 * PAD + NX, 3 * PAD + T
ALPHA = 2 ** 0.25
NG, NH2 = 3, 8
RES = 4
KEYS2 = NX + 2 * P
AHEAD = 3
RING, SLOT = 4, 2 * D
FREE = 4
HB, DOWN = 8, KC // 2
LAST_HB = FC - 2 * HB
ADA_GROUPS = NMOD * KC // 4
GROUPS_FIRST = ADA_GROUPS // 3
FFN_GROUPS = ((6, 2), (6, 4), (0, 4), (0, 2))
PART_CHUNKS = (3 * KC, KC, 3 * KC)
QC = NX // P
TWO_PI_HI = 6.28125
TWO_PI_LO = 2 * math.pi - TWO_PI_HI
ROUND_MAGIC = 12582912.0
PI_BELOW = 3.1415925

QG, KG, UU, QA, KA, NPROJ = 0, 4, 5, 7, 9, 11


def weight_plan():
    plan, at = {}, 0

    def add(name, n):
        nonlocal at
        plan[name] = (at, n)
        at += n

    for l in range(DEPTH):
        if l == 0:
            add("ada0", 2 * GROUPS_FIRST)
        add(f"ffn1_{l}", ffn_units(2 * l))
        add(f"in{l}", 8)
        add(f"out{l}", KC // 2)
        add(f"ffn2_{l}", ffn_units(2 * l + 1))
    add("q_h", 6)
    add("k_h", 6)
    add("v_h", 6)
    add("gattn_h", 2)
    add("conv_h", 6)
    add("ghy_h", 2)
    add("merge_h", 3 * KC // 2)
    add("out_h", KC // 2)
    return plan


class Chain:

    def __init__(self, eng, sem):
        self.eng, self.sem, self.n, self.i = eng, sem, 0, None

    def mark(self, ins):
        ins.then_inc(self.sem, 1)
        self.n += 1

    def wait(self):
        self.eng.wait_ge(self.sem, self.n if self.i is None else self.i * self.per + self.n)

    def link(self, ins):
        self.mark(ins)
        self.wait()

    def enter(self, i, per):
        self.i, self.per, self.n0 = i, per, self.n

    def leave(self, trips):
        assert self.n - self.n0 == self.per, (self.n - self.n0, self.per)
        self.n, self.i = self.n0 + trips * self.per, None


def for_units(eng, plan, name, body):
    g0, n = plan[name]
    trips = n // RING if n >= 2 * RING else 0
    if trips:
        with eng.Fori(0, trips) as i:
            for j in range(RING):
                k = g0 + j
                body(i * RING + j, i * RING + k, k % RING, i + k // RING)
    for u in range(trips * RING, n):
        body(u, g0 + u, (g0 + u) % RING, (g0 + u) // RING)


def added_before(n):
    return n // 3 * sum(PART_CHUNKS) + sum(PART_CHUNKS[:n % 3])


def groups_before(n):
    return GROUPS_FIRST + sum(2 * a + b for a, b in FFN_GROUPS[:n])


def block_schedule(n_hid, groups):
    units, pending = [], None
    for j in range(n_hid):
        units.append(("up", j, pending))
        pending = None
        if 2 <= j < 2 + groups:
            pending = j - 2
            units += [("ada", pending, 0), ("ada", pending, 1)]
    for j in range(DOWN):
        units.append(("down", j, pending))
        pending = None
    return units


def ffn_schedules(n):
    return block_schedule(HB, FFN_GROUPS[n][0]), block_schedule(LAST_HB, FFN_GROUPS[n][1])


def ffn_units(n):
    first_two, last = ffn_schedules(n)
    return 2 * len(first_two) + len(last)


LEAD = RING - 1
SPLIT_BEFORE = [2 * GROUPS_FIRST + sum(ffn_units(m) for m in range(n)) for n in range(2 * DEPTH)]


def for_ffn_units(eng, plan, name, n, up, down, ada, loop=None, loop_marks=0, ahead=None):
    g0, _ = plan[name]
    first_two, last = ffn_schedules(n)
    size = len(first_two)
    assert size % RING == 0

    def block(b, units, n_hid, ends):
        for i, (kind, j, more) in enumerate(units):
            u, g, slot = b * size + i, b * size + (g0 + i), (g0 + i) % RING

            def go_ahead():
                if ahead and (not ends or i + LEAD < len(units)):
                    k = g0 + i + LEAD
                    ahead(u + LEAD, k % RING, b * (size // RING) + k // RING)
            if kind == "ada":
                ada(b, j, more, u, g, slot)
                go_ahead()
            elif kind == "up":
                go_ahead()
                up(b, j, u, g, slot, more)
            else:
                go_ahead()
                down(b, j, u, g, slot, more, n_hid)

    with eng.Fori(0, 2) as b:
        if loop:
            loop.enter(b, loop_marks)
        block(b, first_two, HB, False)
    if loop:
        loop.leave(2)
    block(2, last, LAST_HB, True)


class Attention:

    def __init__(self, tiles, jobs, width, own_steps, before):
        self.own_steps, self.tiles, self.jobs, self.width = own_steps, tiles, jobs, width
        self.pieces = -(-width // 512)
        self.on_act = [p for p in range(self.pieces) if p % 2 == 0]
        self.on_dve = [p for p in range(self.pieces) if p % 2 == 1]
        b = before
        self.tile0 = b.tile0 + b.tiles if b else 0
        self.job0 = b.job0 + b.tiles * b.jobs if b else 0
        self.job_end = self.job0 + tiles * jobs
        self.piece0 = b.piece0 + b.tiles * b.jobs * b.pieces if b else 0
        self.act0 = b.act0 + b.tiles * b.jobs * len(b.on_act) if b else 0
        self.dve0 = b.dve0 + b.tiles * b.jobs * len(b.on_dve) if b else 0

    def scores_at(self, j):
        return 1024 * (j % 2)

    def keys_of(self, p):
        return 512 * p, min(512 * (p + 1), self.width)

    def evacuated(self, i, j, p):
        mine = self.on_act if p % 2 == 0 else self.on_dve
        first = self.act0 if p % 2 == 0 else self.dve0
        return i * (self.jobs * len(mine)) + (first + j * len(mine) + mine.index(p) + 1)


def hybrid_kernel(nc, io, out, stop=None):
    plan = weight_plan()
    first = {k: v[0] for k, v in plan.items()}
    after = {k: v[0] + v[1] for k, v in plan.items()}
    att_x0 = Attention(QC, 12, T, 1 + 2 * 4 + 12, None)
    att_c0 = Attention(NCTX // P, 12, NCTX, 1 + 12, att_x0)
    att_x1 = Attention(QC, 12, T, 1 + 2 * 4 + 12, att_c0)
    att_h = Attention(QC, NH2, KEYS2, 2 + 2 * NH2 + NH2, att_x1)
    att_x = [att_x0, att_x1]
    TAB_MIX, TAB_QKV = (64, 128), 160
    TAB_FEATS, TAB_DFT, TAB_W4 = 224, 240, (224, 256)

    ctx = ExitStack()
    with ctx:
        def sb(name, shape):
            return ctx.enter_context(nc.sbuf_tensor(name, shape, F32))

        def sem(name):
            return ctx.enter_context(nc.semaphore(name))

        with nc.sbuf_tensor("ring", [P, RING * SLOT], F32) as ring_t:
            pass
        ring_r = ctx.enter_context(nc.sbuf_tensor("ring_r", [P, RING * SLOT], F32R))
        ring = [ring_t[:, i * SLOT:(i + 1) * SLOT] for i in range(RING)]
        w_lo = [ring_r[:, i * SLOT:(i + 1) * SLOT] for i in range(RING)]
        ARENA = 41216
        rooms = (("h_room", KC * T, F32), ("a_lo", KC * T, F32R), ("a_hi", KC * T, F32R), ("hid_hi", HB * T, F32R),
                 ("hid_lo", HB * T, F32R), ("w_hi", RING * SLOT, F32R), ("sil", 2 * T, F32), ("rstd", T, F32))
        assert sum(n for _, n, _ in rooms) == ARENA
        with ExitStack() as under:
            room = {name: under.enter_context(nc.sbuf_tensor(name, [P, n], t)) for name, n, t in rooms}
        with ExitStack() as under:
            under.enter_context(nc.sbuf_tensor("h_room2", [P, KC * T], F32))
            a_plain = under.enter_context(nc.sbuf_tensor("a_plain", [P, KC * T], F32))
        arena = sb("arena", [P, ARENA])

        def view(at, *dims):
            n = int(np.prod(dims))
            assert at + n <= ARENA, (at, dims)
            v = arena[:, at:at + n]
            if len(dims) == 2:
                return v.rearrange("p (a b) -> p a b", a=dims[0])
            if len(dims) == 3:
                return v.rearrange("p (a b c) -> p a b c", a=dims[0], b=dims[1])
            return v

        A0 = KC * T
        G0 = 2 * KC * T
        W0 = G0 + FC * T
        h = view(0, KC, T)
        a = view(A0, KC, T)
        sq_g = view(G0, KC, T)
        def chunks(t):
            return t[:].rearrange("p (c n) -> p c n", n=T)

        a_f = chunks(a_plain)
        a_lo, a_hi, hid_hi, hid_lo = (chunks(room[k]) for k in ("a_lo", "a_hi", "hid_hi", "hid_lo"))
        w_hi = [room["w_hi"][:, SLOT * s:SLOT * (s + 1)] for s in range(RING)]
        sil = chunks(room["sil"])
        rstd = room["rstd"][:]
        proj = view(G0, NPROJ, T)
        v_tok = view(G0 + NPROJ * T, T // P, 384)
        rpb = view(G0 + NPROJ * T + T // P * 384, 4, 15 * GRID)
        cos_t = view(W0 - 2 * NX, NX)
        sin_t = view(W0 - NX, NX)
        upad = view(W0, 2, POOL_W)
        qk_sq = view(W0 + 2 * POOL_W, 2, T)
        qk_rs = view(W0 + 2 * POOL_W + 2 * T, 2, T)
        rope_t = view(W0 + 2 * POOL_W + 4 * T, 2, NX)
        win2 = view(W0 + 2 * POOL_W, 2, POOL_W)
        win4 = view(W0 + 4 * POOL_W, 2, POOL_W)
        win8 = view(W0 + 6 * POOL_W, POOL_W)
        win16 = view(W0 + 7 * POOL_W, POOL_W)
        pool_y = view(W0 + 8 * POOL_W, 2, POOL_W)
        pool_inv = view(W0 + 10 * POOL_W, 2, POOL_W)
        probs_1 = view(W0, 3, T)
        keysT_1 = view(W0 + 3 * T, 2, T)
        qst_1 = view(W0 + 5 * T, 6, P)

        h2 = view(0, KC, NX)
        h2r = h2.rearrange("p c (u r) -> p c r u", r=RES)
        y_attn = view(4096, 4, NX)
        x2 = view(A0, KC, NX)
        B0 = A0 + KC * NX
        qh = view(B0, 12, NX)
        kh = view(B0 + 12 * NX, 12, NX)
        vh = view(B0 + 24 * NX, QC, 1536)
        alibi = view(B0 + 24 * NX + QC * 1536, 9 * P)
        H0 = B0 + 24 * NX + QC * 1536 + 9 * P
        probs_2 = view(H0, 3, KEYS2)
        keysT_2 = view(H0 + 3 * KEYS2, 2, KEYS2)
        qst_2 = view(H0 + 5 * KEYS2, 12, P)
        kst = view(H0 + 5 * KEYS2 + 12 * P, 8, P)
        vst = view(H0 + 5 * KEYS2 + 20 * P, 2, NX)
        vbias = view(H0, 1536)
        sq2 = view(B0, KC, NX)
        rstd2 = view(B0 + KC * NX, NX)
        dft = view(B0, 16, NX)
        vxx = view(B0 + 8192, 12, NX)
        hf = view(B0 + 8192 + 6144, 4, NX)
        hb = view(B0 + 8192 + 8192, 4, NX)
        y_re, y_im = hf, hb
        decay = view(B0 + 18432, 4, NX)
        H_re = view(B0 + 20480, 4, NX)
        H_im = view(B0 + 22528, 4, NX)
        z_tok = view(B0 + 24576, 4, NX)
        cpad = view(B0 + 26624, 2, 520)
        gate_t = view(B0 + 26624, 2, NX)
        mul_t = view(B0 + 26624 + 1040, 2, NX)
        f_hid = view(B0 + 28688, NX)
        f_tmp = view(B0 + 26624, 3, NX)
        w4 = view(B0 + 24576, 2 * NX)
        merged = view(B0, KC, NX)
        res = view(B0 + 4096, KC, NX)
        res_sq = view(B0, KC, NX)
        sg_t = view(B0 + 14336, 2, 2 * NX)
        mt_t = view(B0 + 16384, 2, NX)
        fin = view(B0 + 18432, KC, NX)

        cst = sb("cst", [P, 3 * P + 3])
        fold = cst[0:6, 3 * P:]
        c_parts_t = ctx.enter_context(nc.sbuf_tensor("c_parts", [P, KC * P], F32R))
        c_parts = c_parts_t[:].rearrange("p (k m) -> p k m", k=KC)
        ada_rows = sb("ada_rows", [6, 512])
        ident, rot, pairs = (cst[:, k * P:(k + 1) * P] for k in range(3))
        ones = sb("ones", [P, P])
        cvec = sb("cvec", [P, KC * 3])
        cv = cvec[:].rearrange("p (k s) -> p k s", s=3)
        b_ada = sb("b_ada", [P, DEPTH * NMOD * KC * 2])
        mods = [sb(f"mods{l}", [P, NMOD * KC * 2]) for l in range(DEPTH)]
        mod = [m[:].rearrange("p (n c s) -> p n c s", n=NMOD, s=2) for m in mods]
        ng = sb("ng", [P, DEPTH * 3 * KC * 2 + KC])
        ngv = ng[:, 0:DEPTH * 3 * KC * 2].rearrange("p (l k c s) -> p l k c s", l=DEPTH, k=3, s=2)
        final_g = ng[:, DEPTH * 3 * KC * 2:]
        gain = sb("gain", [P, 3 * KC * 2])
        gainv = gain[:].rearrange("p (k c s) -> p k c s", k=3, s=2)
        half_gate = sb("half_gate", [P, 2 * KC * 2])
        hgate = half_gate[:].rearrange("p (k c s) -> p k c s", k=2, s=2)
        small = sb("small", [P, 4 * DEPTH])
        qkg = sb("qkg", [P, 2 * DEPTH])
        poolw = sb("poolw", [P, DEPTH * 2 * P])
        pw = poolw[:].rearrange("p (l k m) -> p l k m", l=DEPTH, k=2)
        nmax = sb("nmax", [P, 4])
        rsum = sb("rsum", [P, 4])
        rinv = sb("rinv", [P, 4])
        vec2 = sb("vec2", [P, 176])
        OB_ADA, OB_IN, OCW, OCB, OFB, OBO, OLG, OLB = 0, 24, 96, 132, 144, 152, 160, 168
        mod2 = sb("mod2", [P, 3 * KC])
        gain2 = sb("gain2", [P, KC])
        bq = sb("bq", [P, 12])
        eps = sb("eps", [P, 2])
        feats = view(B0, NX)
        fw = view(B0 + 28688 + NX, 3 * HD + 4)

        psum = ctx.enter_context(nc.psum_tensor("psum", [P, 4096], F32))

        def bank(b, n=512):
            return psum[:, 512 * b:512 * b + n]

        w_landed = [sem(f"w_landed{i}") for i in range(RING)]
        unit_done = sem("unit_done")
        consts_in = sem("consts_in")
        table_in = sem("table_in")
        act_own, dve_own = sem("act_own"), sem("dve_own")
        setup_done = sem("setup_done")
        silu_c = sem("silu_c")
        c_ready = sem("c_ready")
        rows_out, rows_turned, mods_done = sem("rows_out"), sem("rows_turned"), sem("mods_done")
        mod_ready = sem("mod_ready")
        mean_done, mean_done_0, centred = sem("mean_done"), sem("mean_done_0"), sem("centred")
        sq_done, ss_done, root_done = sem("sq_done"), sem("ss_done"), sem("root_done")
        scaled_done, normed = sem("scaled_done"), sem("normed")
        silu_done = sem("silu_done")
        hi_done, w_split = sem("hi_done"), sem("w_split")
        a_hi_done, a_split = sem("a_hi_done"), sem("a_split")
        hid_done = sem("hid_done")
        res_done = sem("res_done")
        upad_ready = sem("upad_ready")
        even_proj = sem("even_proj")
        proj_done = sem("proj_done")
        qk_sq_done, qk_ss_done, qk_root_done = sem("qk_sq_done"), sem("qk_ss_done"), sem("qk_root_done")
        qk_normed, qk_rotated, qk_roped = sem("qk_normed"), sem("qk_rotated"), sem("qk_roped")
        pool_ready, pool_done, pool_out = sem("pool_ready"), sem("pool_done"), sem("pool_out")
        q_staged = sem("q_staged")
        scores_done, max_done, exp_done = sem("scores_done"), sem("max_done"), sem("exp_done")
        turned, turned_act, turned_dve = sem("turned"), sem("turned_act"), sem("turned_dve")
        probs_ready = sem("probs_ready")
        heads_done, heads_out = sem("heads_done"), sem("heads_out")
        qk2_out, v2_out = sem("qk2_out"), sem("v2_out")
        f_mm, f_arg, f_sin = sem("f_mm"), sem("f_arg"), sem("f_sin")
        cpad_zero, conv_in, conv_out = sem("cpad_zero"), sem("conv_in"), sem("conv_out")
        fh_mm, fh_out, fh_ready = sem("fh_mm"), sem("fh_out"), sem("fh_ready")
        ft_mm, ft_out = sem("ft_mm"), sem("ft_out")
        zt_mm, zt_out = sem("zt_mm"), sem("zt_out")
        zf_mm, zf_out = sem("zf_mm"), sem("zf_out")
        zi_mm, zi_out = sem("zi_mm"), sem("zi_out")
        gate_act, gate_mul = sem("gate_act"), sem("gate_mul")
        merge_sig, merge_out, out2_done = sem("merge_sig"), sem("merge_out"), sem("out2_done")
        stored = sem("stored")

        N_CONSTS = 16 * 9
        PER_PROJ = NPROJ + 2 * (T // P)
        RMS = 3 * DEPTH + 1
        both_in = [l < DEPTH - 1 for l in range(DEPTH)]

        def keeps_ctx(l, c):
            return both_in[l] or c in (KA, KA + 1, KG)

        def blocks_of(slot, n, k):
            return ring[slot][:, 0:n * k * P].rearrange("p (n k m) -> p n k m", n=n, k=k)

        phases = ["ada0", "ffn1_0", "mix0", "ffn2_0", "ada1", "ffn1_1", "mix1", "ffn2_1", "final",
                  "qkv_h", "att_h", "hyena", "merge"]

        def on(name):
            return stop is None or phases.index(name) <= phases.index(stop)

        block = ctx.enter_context(nc.Block())

        @block.sync
        def _(sp):
            def stream(name, floats):
                def load(u, g, slot, turn):
                    sp.wait_ge(unit_done, g + 1)
                    sp.dma_start(ring[slot][:, 0:floats],
                                 io[name][ds(u, 1), :, :].rearrange("u p n -> (u p) n")).then_inc(w_landed[slot], 16)
                for_units(sp, plan, name, load)

            for l in range(DEPTH):
                if l == 0:
                    stream("ada0", 2 * D)
                if on(f"ffn1_{l}"):
                    stream(f"ffn1_{l}", 2 * D)
                if on(f"mix{l}"):
                    stream(f"in{l}", 2 * D)
                    stream(f"out{l}", 2 * D)
                if on(f"ffn2_{l}"):
                    stream(f"ffn2_{l}", 2 * D)
            if on("qkv_h"):
                for name in ("q_h", "k_h", "v_h"):
                    stream(name, 2 * D)
            if on("att_h"):
                stream("gattn_h", 2 * D)
            if on("hyena"):
                stream("conv_h", 2 * D)
                stream("ghy_h", 2 * D)
            if on("merge"):
                stream("merge_h", 2 * D)
                stream("out_h", 2 * D)

        @block.gpsimd
        def _(gp):
            def load(dst, src, s=consts_in):
                gp.dma_start(dst, src).then_inc(s, 16)

            load(cvec[:], io["cvec"])
            load(b_ada[:], io["b_ada"])
            load(ng[:], io["ng"])
            load(h[:, :, 0:NX], io["xT"])
            load(h[:, :, NX:T], io["ctxT"])
            load(cst[:], io["cst"])
            load(small[:], io["small"])
            load(poolw[:], io["poolw"])
            load(vec2[:], io["vec2"])
            for l in range(DEPTH):
                if on(f"mix{l}"):
                    gp.wait_ge(unit_done, after[f"ffn1_{l}"] + RING)
                    load(cos_t, io["cos_t"], table_in)
                    load(sin_t, io["sin_t"], table_in)
                    load(rpb, io[f"rpb{l}"], table_in)
                    load(pool_inv, io["pool_inv"], table_in)
            if on("qkv_h"):
                gp.wait_ge(normed, KC * RMS)
                load(alibi, io["alibi"], table_in)
                load(vbias, io["vbias"], table_in)
            if on("hyena"):
                gp.wait_ge(heads_out, att_h.job_end)
                load(feats[0:33, :], io["feats"], table_in)
                load(fw[0:HD, :], io["fw"], table_in)
                load(decay, io["decay"], table_in)
                load(w4[0:HD, :], io["w4_0"], table_in)
                gp.wait_ge(f_mm, 1)
                load(dft, io["dft"], table_in)
                gp.wait_ge(zf_mm, 4)
                load(w4[0:HD, :], io["w4_1"], table_in)
            if on("merge"):
                for c in range(KC):
                    gp.wait_ge(normed, KC * (RMS + 1) + c + 1)
                    gp.dma_start(out[c], fin[:, c, :]).then_inc(stored, 16)
                gp.wait_ge(stored, 16 * KC)

        @block.tensor
        def _(pe):
            def landed(slot, turn):
                pe.wait_ge(w_landed[slot], 16 * turn + 16)

            def accumulate(out_ap, pairs_):
                for k, (w, x) in enumerate(pairs_):
                    mm = pe.matmul(out_ap, w, x, start=(k == 0), stop=(k == len(pairs_) - 1))
                return mm

            def ada_unit(group, half, split_count, slot, bank_no=7):
                pe.wait_ge(w_split, split_count)
                if half == 0 and not isinstance(group, int):
                    pe.wait_ge(mods_done, group)
                elif half == 0 and group >= 2:
                    pe.wait_ge(mods_done, group - 1 if group < GROUPS_FIRST else group)
                at = 512 * bank_no + 256 * half
                for part, w in enumerate((w_hi[slot], w_lo[slot])):
                    for k in range(KC):
                        mm = pe.matmul(psum[:, at:at + 256], c_parts[:, k, :], w[:, 256 * k:256 * (k + 1)],
                                       start=(part == 0 and k == 0), stop=(part == 1 and k == KC - 1))
                mm.then_inc(unit_done, 1)

            def turn_rows(group, second_block, bank_no=7):
                pe.wait_ge(rows_out, group + 1)
                cols = slice(2, 3) if second_block else slice(0, 2)
                n = cols.stop - cols.start
                for c in range(4):
                    at = 512 * bank_no + n * c
                    mm = pe.matmul(psum[:, at:at + n], ada_rows[:, c * P:(c + 1) * P], fold[:, cols],
                                   start=True, stop=True)
                mm.then_inc(rows_turned, 1)

            def sum_chunks(n, src, width, at, s_in, s_out):
                for c in range(KC):
                    pe.wait_ge(s_in, n + c + 1)
                    mm = pe.matmul(psum[:, at:at + NX], ones[:], src[:, c, 0:NX], start=(c == 0), stop=(c == KC - 1))
                    if width > NX:
                        mm = pe.matmul(psum[:, at + NX:at + T], ones[:], src[:, c, NX:T], start=(c == 0), stop=(c == KC - 1))
                mm.then_inc(s_out, 1)

            def stream_sums(n, src, width):
                pe.wait_ge(res_done, FREE + added_before(n) - 2)
                sum_chunks(KC * n, src, width, 0, sq_done, ss_done)

            def split_product(out_x, out_c, hi, lo, src_hi, src_lo, k, n):
                outs = [(out_x, slice(0, NX))] + ([(out_c, slice(NX, T))] if out_c is not None else [])
                for w, src, part in ((hi, src_hi, 0), (hi, src_lo, 1), (lo, src_hi, 2)):
                    for out_ap, cols in outs:
                        mm = pe.matmul(out_ap, w, src[:, k, cols], start=(k == 0 and part == 0),
                                       stop=(k == n - 1 and part == 2))
                return mm

            def ffn(name, n, part, both):
                before = added_before(part)

                group0, later = groups_before(n), groups_before(n) >= 2 * ADA_GROUPS

                def group_of(b, j):
                    return b * FFN_GROUPS[n][0] + (group0 + j)

                def weights(slot, chunks, blocks):
                    return [w[slot][:, 0:chunks * blocks * P].rearrange("p (n k m) -> p n k m", n=chunks, k=blocks)
                            for w in (w_hi, w_lo)]

                def up(b, j, u, g, slot, pending):
                    s = j % 2
                    pe.wait_ge(w_split, u + (SPLIT_BEFORE[n] + 1))
                    if j >= 2:
                        pe.wait_ge(hid_done, b * HB + (FC * n + j - 1))
                    else:
                        pe.wait_ge(res_done, b * KC + (before + FREE - (2 if j == 0 else 0)))
                    hi, lo = weights(slot, 2, KC)
                    for r in range(2):
                        at_c = (3 * s + 2) * 512 + r * NCTX
                        for k in range(KC):
                            if j == 0 and r == 0:
                                pe.wait_ge(a_split, KC * n + k + 1)
                            mm = split_product(bank(3 * s + r), psum[:, at_c:at_c + NCTX] if both else None,
                                               hi[:, r, k, :], lo[:, r, k, :], a_hi, a_lo, k, KC)
                        if r == 0 and pending is not None:
                            turn_rows(group_of(b, pending), later)
                    mm.then_inc(unit_done, 1)

                def down(b, j, u, g, slot, pending, n_hid):
                    s = j % 2
                    pe.wait_ge(w_split, u + (SPLIT_BEFORE[n] + 1))
                    if j >= 2:
                        pe.wait_ge(res_done, b * KC + (before + FREE + 2 * (j - 1)))
                    groups = FFN_GROUPS[n][n_hid != HB]
                    if j == 1 and groups:
                        pe.wait_ge(mods_done, group_of(b, groups))
                    hi, lo = weights(slot, 2, n_hid)
                    steps = [(r, k) for r in range(2) for k in range(n_hid)]
                    if j == 0:
                        steps.sort(key=lambda rk: rk[1] == n_hid - 1)
                        pe.wait_ge(hid_done, b * HB + (FC * n + n_hid - 1))
                    for at, (r, k) in enumerate(steps):
                        if at == n_hid and pending is not None:
                            turn_rows(group_of(b, pending), later)
                        if j == 0 and at == len(steps) - 2:
                            pe.wait_ge(hid_done, b * HB + (FC * n + n_hid))
                        out_x, out_c = (bank(3 * s), bank(3 * s + 1, NCTX)) if r == 0 else (bank(3 * s + 2), bank(6 + s, NCTX))
                        mm = split_product(out_x, out_c if both else None, hi[:, r, k, :], lo[:, r, k, :],
                                           hid_hi, hid_lo, k, n_hid)
                    mm.then_inc(unit_done, 1)

                def ada(b, j, half, u, g, slot):
                    ada_unit(group_of(b, j), half, u + (SPLIT_BEFORE[n] + 1), slot)
                for_ffn_units(pe, plan, name, n, up, down, ada)

            def residual(name, n, src, blocks, per_unit, both):
                g0 = first[name]

                def unit(u, g, slot, turn):
                    landed(slot, turn)
                    w = blocks_of(slot, per_unit, blocks)
                    pe.wait_ge(res_done, u * per_unit + (added_before(n) + FREE - per_unit))
                    for j in range(per_unit):
                        s = (slot - g0) % 2 * per_unit + j
                        for k in range(blocks):
                            mm = pe.matmul(bank(2 * s), w[:, j, k, :], src[:, k, 0:NX], start=(k == 0), stop=(k == blocks - 1))
                            if both:
                                mm = pe.matmul(bank(2 * s + 1, NCTX), w[:, j, k, :], src[:, k, NX:T],
                                               start=(k == 0), stop=(k == blocks - 1))
                    mm.then_inc(unit_done, 1)
                for_units(pe, plan, name, unit)

            def attention(att, jobs, qst, probs, keysT):
                NJ, NP = att.jobs, att.pieces
                with pe.Fori(0, att.tiles) as i:
                    def scores(j):
                        if j >= 2:
                            pe.wait_ge(exp_done, i * NJ + (att.job0 + j - 1))
                        base = att.scores_at(j)
                        for q, half, keys, lo, hi in jobs[j][0]:
                            mm = pe.matmul(psum[:, base + lo:base + hi], qst[64 * half:64 * half + 64, q, :], keys,
                                           start=True, stop=True)
                        mm.then_inc(scores_done, 1)

                    def turn(j):
                        pe.wait_ge(probs_ready, i * NJ + (att.job0 + j + 1))
                        for p in range(NP):
                            if j >= 1:
                                pe.wait_ge(turned_act if p % 2 == 0 else turned_dve, att.evacuated(i, j - 1, p))
                            lo, hi = att.keys_of(p)
                            for k in range(lo, hi, P):
                                mm = pe.transpose(psum[:, 2048 + k:2048 + k + P], probs[:, j % 3, k:k + P], ident)
                            mm.then_inc(turned, 1)

                    def values(j):
                        if j == NJ - 1:
                            for p in range(NP):
                                pe.wait_ge(turned_act if p % 2 == 0 else turned_dve, att.evacuated(i, j, p))
                        if j >= 2:
                            pe.wait_ge(heads_out, i * NJ + (att.job0 + j - 1))
                        half = j % 2
                        out_ = psum[64 * half:64 * half + 64, 3072 + 512 * (j % 2):3072 + 512 * (j % 2) + P]
                        for k in range(0, att.width, P):
                            mm = pe.matmul(out_, jobs[j][1][k // P], keysT[:, j % 2, k:k + P],
                                           start=(k == 0), stop=(k + P == att.width))
                        mm.then_inc(heads_done, 1)

                    pe.wait_ge(q_staged, i + (att.tile0 + 1))
                    for j in range(AHEAD):
                        scores(j)
                    turn(0)
                    for j in range(NJ):
                        if j + AHEAD < NJ:
                            scores(j + AHEAD)
                        if j + 1 < NJ:
                            turn(j + 1)
                        values(j)
                    pe.wait_ge(heads_out, i * NJ + (att.job0 + NJ))

            def block1_jobs(k0):
                jobs = []
                for n in range(12):
                    if n < 4:
                        q, half, kc, vcol = n // 2, n % 2, KA + n // 2, n * HD
                    else:
                        q, half, kc, vcol = 2 + (n - 4) // 2, n % 2, KG, 256 + n % 2 * HD
                    pieces = [(q, half, proj[64 * half:64 * half + 64, kc, lo:hi], lo - k0, hi - k0)
                              for lo, hi in ((k0, NX), (NX, T)) if hi > lo]
                    jobs.append((pieces, [v_tok[:, t, vcol:vcol + HD] for t in range(k0 // P, T // P)]))
                return jobs

            def mix(l):
                g0 = first[f"in{l}"]
                both = both_in[l]

                def head_sums(n):
                    pe.wait_ge(qk_sq_done, 5 * l + n + 1)
                    if n > 0:
                        pe.wait_ge(qk_root_done, 5 * l + n)
                    mm = pe.matmul(bank(4), pairs, qk_sq[:, n % 2, 0:NX], start=True, stop=True)
                    if keeps_ctx(l, QG + n):
                        mm = pe.matmul(bank(5, NCTX), pairs, qk_sq[:, n % 2, NX:T], start=True, stop=True)
                    mm.then_inc(qk_ss_done, 1)

                def rotation(n):
                    pe.wait_ge(qk_normed, 5 * l + n + 1)
                    if n >= 2:
                        pe.wait_ge(qk_roped, 5 * l + n - 1)
                    pe.matmul(bank(6 + n % 2), rot, proj[:, QG + n, 0:NX], start=True, stop=True).then_inc(qk_rotated, 1)

                for c in range(NPROJ):
                    slot = (g0 + c // 2) % RING
                    if c % 2 == 0:
                        landed(slot, (g0 + c // 2) // RING)
                    if c >= 2:
                        pe.wait_ge(proj_done, PER_PROJ * l + c - 1)
                    w = blocks_of(slot, 2, KC)
                    for k in range(KC):
                        if c == 0:
                            pe.wait_ge(normed, KC * (3 * l + 1) + k + 1)
                        mm = pe.matmul(bank(2 * (c % 2)), w[:, c % 2, k, :], a[:, k, 0:NX], start=(k == 0), stop=(k == KC - 1))
                        if keeps_ctx(l, c):
                            mm = pe.matmul(bank(2 * (c % 2) + 1, NCTX), w[:, c % 2, k, :], a[:, k, NX:T],
                                           start=(k == 0), stop=(k == KC - 1))
                    mm.then_inc(unit_done if c % 2 == 1 or c == NPROJ - 1 else even_proj, 1)
                    if 1 <= c <= 5:
                        head_sums(c - 1)
                    if 2 <= c <= 6:
                        rotation(c - 2)
                pe.wait_ge(qk_root_done, 5 * (l + 1))
                for n, cols in ((0, 256), (1, 128)):
                    slot = (g0 + 6 + n) % RING
                    landed(slot, (g0 + 6 + n) // RING)
                    w = ring[slot][:, 0:KC * cols].rearrange("p (k n) -> p k n", k=KC)
                    for t in range(T // P):
                        pe.wait_ge(proj_done, PER_PROJ * l + NPROJ + (t + 1 if n else 0))
                        mm = accumulate(bank(t, cols), [(a[:, k, t * P:(t + 1) * P], w[:, k, :]) for k in range(KC)])
                    mm.then_inc(unit_done, 1)
                for k in range(2):
                    pe.wait_ge(pool_ready, 2 * l + k + 1)
                    if k == 0:
                        pe.wait_ge(proj_done, PER_PROJ * (l + 1))
                    mm = pe.matmul(bank(2 * k), pw[:, l, k, :], pool_y[:, k, POOL_X:POOL_X + NX], start=True, stop=True)
                    if both:
                        mm = pe.matmul(bank(2 * k + 1, NCTX), pw[:, l, k, :], pool_y[:, k, POOL_C:POOL_C + NCTX],
                                       start=True, stop=True)
                    mm.then_inc(pool_done, 1)
                pe.wait_ge(pool_out, 2 * l + 2)
                attention(att_x[l], block1_jobs(0), qst_1, probs_1, keysT_1)
                if both:
                    attention(att_c0, block1_jobs(NX), qst_1, probs_1, keysT_1)
                residual(f"out{l}", 3 * l + 1, a, KC, 2, both)

            def wide(name, c0, n_chunks, s_read, read0, epilogue_banks=4):
                g0 = first[name]
                for c in range(n_chunks):
                    slot = (g0 + c // 2) % RING
                    if c % 2 == 0:
                        landed(slot, (g0 + c // 2) // RING)
                    if c0 + c >= 4:
                        pe.wait_ge(s_read, read0 + c0 + c - 3)
                    w = blocks_of(slot, 2, KC)
                    for k in range(KC):
                        if name == "q_h" and c == 0:
                            pe.wait_ge(normed, KC * RMS + k + 1)
                        mm = pe.matmul(bank(c % 4), w[:, c % 2, k, :], h2[:, k, :], start=(k == 0), stop=(k == KC - 1))
                    if c % 2 == 1:
                        mm.then_inc(unit_done, 1)

            def hyena():
                for n in range(3):
                    if n == 0:
                        pe.wait_ge(table_in, TAB_FEATS)
                        pe.wait_ge(gate_act, 4)
                        pe.matmul(psum[0:HD, 0:NX], fw[0:33, 0:HD], feats[0:33, :], start=True, stop=True).then_inc(f_mm, 1)
                    else:
                        pe.wait_ge(f_sin, n)
                        pe.matmul(psum[0:HD, 0:NX], fw[0:HD, n * HD:(n + 1) * HD], f_hid[0:HD, :],
                                  start=True, stop=True).then_inc(f_mm, 1)
                pe.wait_ge(f_sin, 3)
                wide("conv_h", 0, 12, conv_in, 0)
                for o in range(2):
                    pe.wait_ge(table_in, TAB_W4[o])
                    if o == 0:
                        pe.wait_ge(conv_in, 12)
                    for t in range(QC):
                        for r in range(2):
                            n = 8 * o + 2 * t + r
                            if n % 8 >= 4:
                                pe.wait_ge(fh_out, n - 3)
                            pe.matmul(bank(n % 4), f_hid[0:HD, t * P:(t + 1) * P], w4[0:HD, r * NX:(r + 1) * NX],
                                      start=True, stop=True).then_inc(fh_mm, 1)
                    pe.wait_ge(table_in, TAB_DFT)
                    pe.wait_ge(fh_ready, 4 * (o + 1))
                    for q in range(4):
                        n = 4 * o + q
                        if q >= 2:
                            pe.wait_ge(ft_out, n - 1)
                        accumulate(bank(2 * (q % 2)), [(dft[:, t, q * P:(q + 1) * P], hf[:, t, :]) for t in range(QC)])
                        accumulate(bank(2 * (q % 2) + 1), [(dft[:, 4 + t, q * P:(q + 1) * P], hb[:, t, :])
                                                           for t in range(QC)]).then_inc(ft_mm, 1)
                    if o == 0:
                        pe.wait_ge(conv_out, 12)
                    else:
                        pe.wait_ge(zi_out, 4)
                    for c in range(4):
                        n = 4 * o + c
                        if c >= 2:
                            pe.wait_ge(zt_out, n - 1)
                        for t in range(QC):
                            mm = pe.transpose(psum[:, 2048 + 512 * (c % 2) + t * P:2048 + 512 * (c % 2) + (t + 1) * P],
                                              vxx[:, c, t * P:(t + 1) * P], ident)
                        mm.then_inc(zt_mm, 1)
                    pe.wait_ge(zt_out, 4 * (o + 1))
                    pe.wait_ge(ft_out, 4 * (o + 1))
                    for q in range(4):
                        n = 4 * o + q
                        if q >= 2:
                            pe.wait_ge(zf_out, n - 1)
                        accumulate(bank(2 * (q % 2)), [(dft[:, t, q * P:(q + 1) * P], z_tok[:, t, :]) for t in range(QC)])
                        accumulate(bank(2 * (q % 2) + 1), [(dft[:, 4 + t, q * P:(q + 1) * P], z_tok[:, t, :])
                                                           for t in range(QC)]).then_inc(zf_mm, 1)
                    pe.wait_ge(zf_out, 4 * (o + 1))
                    for c in range(4):
                        n = 4 * o + c
                        if c >= 2:
                            pe.wait_ge(zi_out, n - 1)
                        accumulate(bank(4 + c % 2),
                                   [(y_re[:, q, c * P:(c + 1) * P], dft[:, 8 + q, :]) for q in range(4)]
                                   + [(y_im[:, q, c * P:(c + 1) * P], dft[:, 12 + q, :]) for q in range(4)]).then_inc(zi_mm, 1)
                wide("ghy_h", 4, 4, gate_mul, 0)

            def merge():
                g0 = first["merge_h"]
                pe.wait_ge(gate_mul, 8)
                for q in range(KC // 2):
                    for j in range(2):
                        c, g = 2 * q + j, g0 + 3 * q + j
                        landed(g % RING, g // RING)
                        if c >= 2:
                            pe.wait_ge(merge_sig, c - 1)
                        w = blocks_of(g % RING, 2, KC)
                        for r in range(2):
                            mm = accumulate(bank(2 * j + r), [(w[:, r, k, :], h2[:, k, :]) for k in range(KC)])
                        mm.then_inc(unit_done, 1)
                    g = g0 + 3 * q + 2
                    landed(g % RING, g // RING)
                    if q >= 1:
                        pe.wait_ge(merge_out, 2 * q)
                    w = blocks_of(g % RING, 4, 4)
                    for j in range(2):
                        for r, y in enumerate((y_attn, vxx)):
                            mm = accumulate(bank(4 + 2 * j + r), [(w[:, 2 * j + r, k, :], y[:, k, :]) for k in range(4)])
                    mm.then_inc(unit_done, 1)
                pe.wait_ge(merge_out, KC)
                g0 = first["out_h"]
                for c in range(KC):
                    g = g0 + c // 2
                    if c % 2 == 0:
                        landed(g % RING, g // RING)
                    if c >= 4:
                        pe.wait_ge(out2_done, c - 3)
                    w = blocks_of(g % RING, 2, KC)
                    mm = accumulate(bank(c % 4), [(w[:, c % 2, k, :], merged[:, k, :]) for k in range(KC)])
                    if c % 2 == 1:
                        mm.then_inc(unit_done, 1)
                sum_chunks(0, res, NX, 2048, out2_done, mean_done)
                sum_chunks(KC * (RMS + 1), res_sq, NX, 3072, sq_done, ss_done)

            pe.nop().then_inc(unit_done, RING)
            pe.wait_ge(consts_in, N_CONSTS)
            pe.wait_ge(setup_done, 1)
            pe.wait_ge(c_ready, 1)
            for t in range(GROUPS_FIRST):
                for half in range(2):
                    u = 2 * t + half
                    ada_unit(t, half, u + 1, u % RING, 7 - t % 2)
                if t > 0:
                    turn_rows(t - 1, False, 7 - (t - 1) % 2)
            turn_rows(GROUPS_FIRST - 1, False, 7 - (GROUPS_FIRST - 1) % 2)
            for l in range(DEPTH):
                if on(f"ffn1_{l}"):
                    stream_sums(3 * l, a, T)
                    ffn(f"ffn1_{l}", 2 * l, 3 * l, True)
                if on(f"mix{l}"):
                    stream_sums(3 * l + 1, a, T)
                    mix(l)
                if on(f"ffn2_{l}"):
                    stream_sums(3 * l + 2, sq_g, T if both_in[l] else NX)
                    ffn(f"ffn2_{l}", 2 * l + 1, 3 * l + 2, both_in[l])
            if on("final"):
                stream_sums(RMS - 1, a, NX)
            if on("qkv_h"):
                pe.wait_ge(root_done, RMS)
                sum_chunks(KC * (RMS - 1), x2, NX, 2048, normed, mean_done_0)
                sum_chunks(KC * RMS, sq2, NX, 3072, sq_done, ss_done)
                wide("q_h", 0, 12, qk2_out, 0)
                wide("k_h", 12, 12, qk2_out, 0)
                for u in range(6):
                    g = first["v_h"] + u
                    landed(g % RING, g // RING)
                    w = ring[g % RING][:, 0:KC * 256].rearrange("p (k n) -> p k n", k=KC)
                    for t in range(QC):
                        if u >= 1:
                            pe.wait_ge(v2_out, 4 * (u - 1) + t + 1)
                        mm = accumulate(bank(4 + t, 256), [(h2r[:, k, t, :], w[:, k, :]) for k in range(KC)])
                    mm.then_inc(unit_done, 1)
            if on("att_h"):
                pe.wait_ge(qk2_out, 24)
                pe.wait_ge(v2_out, 24)
                jobs = []
                for n in range(NH2):
                    c, rows, cols = n // 2, slice(64 * (n % 2), 64 * (n % 2) + 64), slice(n * HD, (n + 1) * HD)
                    jobs.append((
                        [(c, n % 2, kh[rows, c, :], 0, NX)]
                        + [(4 * g + c, n % 2, kst[rows, 4 * (g - 1) + c, :], NX + (g - 1) * P, NX + g * P) for g in (1, 2)],
                        [vh[:, r, cols] for r in range(RES)] + [vst[:, g, cols] for g in range(2)]))
                attention(att_h, jobs, qst_2, probs_2, keysT_2)
                wide("gattn_h", 0, 4, gate_mul, 0)
            if on("hyena"):
                hyena()
            if on("merge"):
                merge()

        @block.scalar
        def _(act):
            def squares(n, src, dst, width, ready):
                for c in range(KC):
                    ready(c)
                    act.activation(dst[:, c, 0:width], src[:, c, 0:width], ACT.Square).then_inc(sq_done, 1)

            def root(n, dst, width, eps_col, at=3072):
                act.wait_ge(ss_done, n + 1)
                act.activation(dst[:, 0:width], psum[:, at:at + width], ACT.Sqrt, scale=1.0 / D,
                               bias=eps_col).then_inc(root_done, 1)

            def modulate(n, src, dst, both, gain_of, shift_of, split=False):
                for c in range(KC):
                    act.wait_ge(scaled_done, KC * n + c + 1)
                    ins = act.activation(dst[:, c, 0:NX], src[:, c, 0:NX], ACT.Identity, scale=gain_of(c, 0), bias=shift_of(c, 0))
                    if both:
                        ins = act.activation(dst[:, c, NX:T], src[:, c, NX:T], ACT.Identity, scale=gain_of(c, 1), bias=shift_of(c, 1))
                    ins.then_inc(normed, 1)
                    if split:
                        act.wait_ge(normed, KC * n + c + 1)
                        w = T if both else NX
                        act.activation(a_hi[:, c, 0:w], a_f[:, c, 0:w], ACT.Copy).then_inc(a_hi_done, 1)

            def rms(n, width, gain_of, shift_of, ffn_name=None):
                def ready(c):
                    if n == 0:
                        return
                    act.wait_ge(res_done, FREE + added_before(n) - KC + c + 1)
                squares(n, h, sq_g if n % 3 == 2 else a, width, ready)
                if ffn_name:
                    for k in range(first[ffn_name], first[ffn_name] + LEAD):
                        first_parts(k % RING, k // RING)
                root(n, rstd, width, eps[:, 0:1], 0)
                act.wait_ge(mod_ready, n + 1)
                x = a_f if ffn_name else a
                modulate(n, x, x, width > NX, gain_of, shift_of, bool(ffn_name))

            def first_parts(slot, turn):
                act.wait_ge(w_landed[slot], turn * 16 + 16)
                act.activation(w_hi[slot], ring[slot], ACT.Copy).then_inc(hi_done, 1)

            def take_rows(group, g, bank_no=7):
                act.wait_ge(unit_done, g + (1 + RING))
                if not isinstance(group, int) or group > 0:
                    act.wait_ge(rows_turned, group)
                act.activation(ada_rows[:], psum[0:6, 512 * bank_no:512 * bank_no + 512], ACT.Copy).then_inc(rows_out, 1)

            def ffn_gate(name, n, both):

                def up(b, j, u, g, slot, pending):
                    s = j % 2
                    act.wait_ge(unit_done, g + (1 + RING))
                    ins = act.activation(sil[:, s, 0:NX], bank(3 * s), ACT.Silu)
                    if both:
                        ins = act.activation(sil[:, s, NX:T], bank(3 * s + 2, NCTX), ACT.Silu)
                    ins.then_inc(silu_done, 1)

                def down(b, j, u, g, slot, pending, n_hid):
                    pass

                def ada(b, j, half, u, g, slot):
                    if half == 1:
                        take_rows(b * FFN_GROUPS[n][0] + (groups_before(n) + j), g)
                for_ffn_units(act, plan, name, n, up, down, ada,
                              ahead=lambda u, slot, turn: first_parts(slot, turn))

            def attention(att, probs, keysT, biased, head_dst):
                NJ, NP = att.jobs, att.pieces
                with act.Fori(0, att.tiles) as i:
                    def exp(j):
                        act.wait_ge(max_done, i * NJ + (att.job0 + j + 1))
                        if j >= 3:
                            act.wait_ge(turned, i * (NJ * NP) + (att.piece0 + (j - 2) * NP))
                        at = att.scores_at(j)
                        src = probs[:, j % 3, 0:att.width] if biased(j) else psum[:, at:at + att.width]
                        act.activation(probs[:, j % 3, 0:att.width], src, ACT.Exp, bias=nmax[:, j % 4:j % 4 + 1],
                                       accum_out=rsum[:, j % 4:j % 4 + 1]).then_inc(exp_done, 1)

                    def take(j):
                        for p in att.on_act:
                            act.wait_ge(turned, i * (NJ * NP) + (att.piece0 + j * NP + p + 1))
                            lo, hi = att.keys_of(p)
                            act.activation(keysT[:, j % 2, lo:hi], psum[:, 2048 + lo:2048 + hi], ACT.Copy).then_inc(turned_act, 1)

                    for j in range(AHEAD):
                        exp(j)
                    take(0)
                    for j in range(NJ):
                        if j + AHEAD < NJ:
                            exp(j + AHEAD)
                        if j + 1 < NJ:
                            take(j + 1)
                        act.wait_ge(heads_done, i * NJ + (att.job0 + j + 1))
                        rows, at = slice(64 * (j % 2), 64 * (j % 2) + 64), 3072 + 512 * (j % 2)
                        act.activation(head_dst(i, j, rows), psum[rows, at:at + P], ACT.Copy).then_inc(heads_out, 1)

            def block1_attention(att, t0, latent):
                def head_dst(i, j, rows):
                    c = j // 2 if j < 4 else 2 + j // 2
                    return a[rows, c, ds(i * P + t0, P)]
                attention(att, probs_1, keysT_1, lambda j: latent and j < 4, head_dst)

            def mix(l):
                g0 = first[f"in{l}"]

                def square(n):
                    c = QG + n
                    w = T if keeps_ctx(l, c) else NX
                    act.wait_ge(proj_done, PER_PROJ * l + c + 1)
                    if n >= 2:
                        act.wait_ge(qk_ss_done, 5 * l + n - 1)
                    act.activation(qk_sq[:, n % 2, 0:w], proj[:, c, 0:w], ACT.Square).then_inc(qk_sq_done, 1)

                def head_root(n):
                    w = T if keeps_ctx(l, QG + n) else NX
                    act.wait_ge(qk_ss_done, 5 * l + n + 1)
                    if n >= 2:
                        act.wait_ge(qk_normed, 5 * l + n - 1)
                    act.activation(qk_rs[:, n % 2, 0:w], psum[:, 2048:2048 + w], ACT.Sqrt, scale=1.0 / HD,
                                   bias=eps[:, 0:1]).then_inc(qk_root_done, 1)

                for c in range(NPROJ):
                    if c % 2 == 1 or c == NPROJ - 1:
                        act.wait_ge(unit_done, g0 + c // 2 + 1 + RING)
                    else:
                        act.wait_ge(even_proj, NPROJ // 2 * l + c // 2 + 1)
                    b0 = 1024 * (c % 2)
                    if c in (UU, UU + 1):
                        act.wait_ge(upad_ready, l + 1)
                        ins = act.activation(upad[:, c - UU, POOL_X:POOL_X + NX], psum[:, b0:b0 + NX], ACT.Copy)
                        if both_in[l]:
                            ins = act.activation(upad[:, c - UU, POOL_C:POOL_C + NCTX], psum[:, b0 + NX:b0 + T], ACT.Copy)
                    else:
                        w = T if keeps_ctx(l, c) else NX
                        ins = act.activation(proj[:, c, 0:w], psum[:, b0:b0 + w], ACT.Copy,
                                             scale=SCORE_SCALE if c in (QA, QA + 1) else 1.0)
                    ins.then_inc(proj_done, 1)
                    if c < 5:
                        square(c)
                    if 1 <= c <= 5:
                        head_root(c - 1)
                for n, lo, cols in ((0, 0, 256), (1, 256, 128)):
                    act.wait_ge(unit_done, g0 + 6 + n + 1 + RING)
                    for t in range(T // P):
                        act.activation(v_tok[:, t, lo:lo + cols], bank(t, cols), ACT.Copy).then_inc(proj_done, 1)
                for k in range(2):
                    act.wait_ge(pool_done, 2 * l + k + 1)
                    scale = small[:, 4 * l + k:4 * l + k + 1]
                    ins = act.activation(a[:, 2 + k, 0:NX], bank(2 * k), ACT.Copy, scale=scale)
                    if both_in[l]:
                        ins = act.activation(a[:, 2 + k, NX:T], bank(2 * k + 1, NCTX), ACT.Copy, scale=scale)
                    ins.then_inc(pool_out, 1)
                block1_attention(att_x[l], 0, True)
                if both_in[l]:
                    block1_attention(att_c0, NX, False)

            def gates(name, n0, bias0):
                g0 = first[name]
                for c in range(4):
                    act.wait_ge(unit_done, g0 + c // 2 + 1 + RING)
                    if n0 + c >= 2:
                        act.wait_ge(gate_mul, n0 + c - 1)
                    act.activation(gate_t[:, c % 2, :], bank(c % 4), ACT.Silu,
                                   bias=vec2[:, bias0 + c:bias0 + c + 1]).then_inc(gate_act, 1)

            def hyena():
                for n in range(3):
                    act.wait_ge(f_arg, n + 1)
                    act.activation(f_hid[0:HD, :], f_tmp[0:HD, 0, :], ACT.Sin).then_inc(f_sin, 1)
                act.wait_ge(cpad_zero, 1)
                g0 = first["conv_h"]
                for c in range(12):
                    act.wait_ge(unit_done, g0 + c // 2 + 1 + RING)
                    if c >= 2:
                        act.wait_ge(conv_out, c - 1)
                    act.activation(cpad[:, c % 2, 1:NX + 1], bank(c % 4), ACT.Identity,
                                   bias=vec2[:, OB_IN + 40 + c:OB_IN + 41 + c]).then_inc(conv_in, 1)
                for o in range(2):
                    for q in range(4):
                        act.wait_ge(ft_mm, 4 * o + q + 1)
                        if o == 1 and q == 0:
                            act.wait_ge(zf_out, 4)
                        act.activation(H_re[:, q, :], bank(2 * (q % 2)), ACT.Copy)
                        act.activation(H_im[:, q, :], bank(2 * (q % 2) + 1), ACT.Copy).then_inc(ft_out, 1)
                    for c in range(4):
                        act.wait_ge(zt_mm, 4 * o + c + 1)
                        act.activation(z_tok[:, :, c * P:(c + 1) * P],
                                       bank(4 + c % 2).rearrange("p (t m) -> p t m", t=4), ACT.Copy).then_inc(zt_out, 1)
                gates("ghy_h", 4, OB_IN + 52)

            def merge():
                g0 = first["merge_h"]
                for c in range(KC):
                    act.wait_ge(unit_done, g0 + 3 * (c // 2) + c % 2 + 1 + RING)
                    if c >= 2:
                        act.wait_ge(merge_out, c - 1)
                    for r in range(2):
                        b = OB_IN + 56 + 8 * r + c
                        ins = act.activation(sg_t[:, c % 2, r * NX:(r + 1) * NX], bank(2 * (c % 2) + r), ACT.Sigmoid,
                                             bias=vec2[:, b:b + 1])
                    ins.then_inc(merge_sig, 1)
                squares(RMS + 1, res, res_sq, NX, lambda c: act.wait_ge(centred, KC + c + 1))
                root(RMS + 1, sg_t[:, 0, 0:NX], NX, eps[:, 1:2])
                modulate(RMS + 1, res, fin, False, lambda c, s: vec2[:, OLG + c:OLG + c + 1],
                         lambda c, s: vec2[:, OLB + c:OLB + c + 1])

            act.wait_ge(consts_in, N_CONSTS)
            act.wait_ge(setup_done, 1)
            act.activation(cv[:, :, 0:2], cv[:, :, 0:2], ACT.Silu).then_inc(silu_c, 1)
            for t in range(GROUPS_FIRST + 1):
                if t < GROUPS_FIRST:
                    for u in (2 * t, 2 * t + 1):
                        first_parts(u % RING, u // RING)
                if t > 0:
                    take_rows(t - 1, 2 * t - 1, 7 - (t - 1) % 2)
            for l in range(DEPTH):
                def gain_of(k):
                    return lambda c, s: gainv[:, k, c, s:s + 1]

                def shift_of(k):
                    return lambda c, s: mod[l][:, 3 * k, c, s:s + 1]
                if on(f"ffn1_{l}"):
                    rms(3 * l, T, gain_of(0), shift_of(0), f"ffn1_{l}")
                    ffn_gate(f"ffn1_{l}", 2 * l, True)
                if on(f"mix{l}"):
                    rms(3 * l + 1, T, gain_of(1), shift_of(1))
                    mix(l)
                if on(f"ffn2_{l}"):
                    rms(3 * l + 2, T if both_in[l] else NX, gain_of(2), shift_of(2), f"ffn2_{l}")
                    ffn_gate(f"ffn2_{l}", 2 * l + 1, both_in[l])
            if on("final"):
                n = RMS - 1
                squares(n, h, a, NX, lambda c: act.wait_ge(res_done, FREE + added_before(n) - KC + c + 1))
                root(n, rstd, NX, eps[:, 0:1], 0)
                modulate(n, x2, x2, False, lambda c, s: final_g[:, c:c + 1], lambda c, s: 0.0)
            if on("qkv_h"):
                squares(RMS, h2, sq2, NX, lambda c: act.wait_ge(centred, c + 1))
                root(RMS, rstd2, NX, eps[:, 1:2])
                modulate(RMS, h2, h2, False, lambda c, s: gain2[:, c:c + 1], lambda c, s: mod2[:, c:c + 1])
                for c in range(24):
                    act.wait_ge(unit_done, first["q_h"] + c // 2 + 1 + RING)
                    dst = (qh if c < 12 else kh)[:, c % 12, :].rearrange("p (r u) -> p u r", r=RES)
                    src = bank(c % 4).rearrange("p (u r) -> p u r", r=RES)
                    if c < 12:
                        act.activation(dst, src, ACT.Identity, scale=SCORE_SCALE,
                                       bias=bq[:, c:c + 1]).then_inc(qk2_out, 1)
                    else:
                        act.activation(dst, src, ACT.Identity,
                                       bias=vec2[:, OB_IN + c:OB_IN + c + 1]).then_inc(qk2_out, 1)
            if on("att_h"):

                def head_dst(i, j, rows):
                    by_residue = y_attn[rows, j // 2, :].rearrange("p (u r) -> p r u", r=RES)
                    return by_residue[:, ds(i, 1), :].rearrange("p a u -> p (a u)")
                attention(att_h, probs_2, keysT_2, lambda j: True, head_dst)
                gates("gattn_h", 0, OB_IN + 36)
            if on("hyena"):
                hyena()
            if on("merge"):
                merge()

        @block.vector
        def _(dve):
            own = Chain(dve, dve_own)

            def modulation(l, k):
                dve.wait_ge(mods_done, (GROUPS_FIRST, ADA_GROUPS)[k > 0] if l == 0 else 2 * ADA_GROUPS)
                ins = dve.scalar_tensor_tensor(gainv[:, k, :, :], mod[l][:, 3 * k + 1, :, :], 1.0, ngv[:, l, k, :, :],
                                               ALU.add, ALU.mult)
                if k != 1:
                    own.mark(ins)
                    ins = dve.tensor_scalar(hgate[:, k // 2, :, :], mod[l][:, 3 * k + 2, :, :], 0.5, None, ALU.mult)
                ins.then_inc(mod_ready, 1)
                dve.wait_ge(mod_ready, 3 * l + k + 1)

            def take_vectors(group, b, step, bank_no=7):
                dve.wait_ge(rows_turned, b * step + (group + 1))
                l, at = group // ADA_GROUPS, group % ADA_GROUPS
                if l < DEPTH:
                    cols, bias_cols = ds(b * (8 * step) + 8 * at, 8), ds(b * (8 * step) + (l * NMOD * KC * 2 + 8 * at), 8)
                    dve.tensor_tensor(mods[l][:, cols], psum[:, 512 * bank_no:512 * bank_no + 8], b_ada[:, bias_cols],
                                      ALU.add).then_inc(mods_done, 1)
                else:
                    cols, bias_cols = ds(b * (4 * step) + 4 * at, 4), ds(b * (4 * step) + (OB_ADA + 4 * at), 4)
                    dve.tensor_tensor(mod2[:, cols], psum[:, 512 * bank_no:512 * bank_no + 4], vec2[:, bias_cols],
                                      ALU.add).then_inc(mods_done, 1)

            def scale_rows(n, src, dst, root_ap, width):
                dve.wait_ge(root_done, n + 1)
                own.link(dve.reciprocal(root_ap[:, 0:width], root_ap[:, 0:width]))
                for c in range(KC):
                    dve.tensor_tensor(dst[:, c, 0:width], src[:, c, 0:width], root_ap[:, 0:width], ALU.mult)\
                       .then_inc(scaled_done, 1)

            def rest_parts(count, slot):
                dve.wait_ge(hi_done, count)
                dve.tensor_tensor(w_lo[slot], ring[slot], w_hi[slot].bitcast(F32), ALU.subtract).then_inc(w_split, 1)

            def first_rests(name, n):
                for k in range(LEAD):
                    rest_parts(SPLIT_BEFORE[n] + k + 1, (first[name] + k) % RING)

            def scale_and_split(n, n_ffn, width):
                dve.wait_ge(root_done, n + 1)
                own.link(dve.reciprocal(rstd[:, 0:width], rstd[:, 0:width]))
                for c in range(KC + 2):
                    if c < KC:
                        dve.tensor_tensor(a_f[:, c, 0:width], h[:, c, 0:width], rstd[:, 0:width], ALU.mult)\
                           .then_inc(scaled_done, 1)
                    if c >= 2:
                        dve.wait_ge(a_hi_done, KC * n_ffn + c - 1)
                        dve.tensor_tensor(a_lo[:, c - 2, 0:width], a_f[:, c - 2, 0:width],
                                          a_hi[:, c - 2, 0:width].bitcast(F32), ALU.subtract).then_inc(a_split, 1)

            def ffn(name, n, part, gate_at, both):
                width = T if both else NX

                def pending_vectors(b, pending):
                    if pending is not None:
                        step = FFN_GROUPS[n][0]
                        if isinstance(b, int):
                            take_vectors(groups_before(n) + b * step + pending, 0, 0)
                        else:
                            take_vectors(groups_before(n) + pending, b, step)

                def up(b, j, u, g, slot, pending):
                    s = j % 2
                    pending_vectors(b, pending)
                    dve.wait_ge(silu_done, b * HB + (FC * n + j + 1))
                    p = sil[:, s, 0:width]
                    ins = dve.tensor_tensor(sil[:, s, 0:NX], sil[:, s, 0:NX], bank(3 * s + 1), ALU.mult)
                    if both:
                        at = (3 * s + 2) * 512 + NCTX
                        ins = dve.tensor_tensor(sil[:, s, NX:T], sil[:, s, NX:T], psum[:, at:at + NCTX], ALU.mult)
                    own.link(ins)
                    own.link(dve.tensor_copy(hid_hi[:, j, 0:width], p))
                    dve.tensor_tensor(hid_lo[:, j, 0:width], p, hid_hi[:, j, 0:width].bitcast(F32), ALU.subtract)\
                       .then_inc(hid_done, 1)

                def down(b, j, u, g, slot, pending, n_hid):
                    s = j % 2
                    pending_vectors(b, pending)
                    dve.wait_ge(unit_done, g + (1 + RING))
                    for r in range(2):
                        m = 2 * j + r
                        at_x, at_c = (3 * s, 3 * s + 1) if r == 0 else (3 * s + 2, 6 + s)
                        if j == 0 and r == 0:
                            dve.wait_ge(res_done, b * KC + (added_before(part) + FREE))
                        ins = dve.scalar_tensor_tensor(h[:, m, 0:NX], bank(at_x), gate_at(m, 0), h[:, m, 0:NX],
                                                       ALU.mult, ALU.add)
                        if both:
                            ins = dve.scalar_tensor_tensor(h[:, m, NX:T], bank(at_c, NCTX), gate_at(m, 1), h[:, m, NX:T],
                                                           ALU.mult, ALU.add)
                        ins.then_inc(res_done, 1)
                for_ffn_units(dve, plan, name, n, up, down, lambda *unit: None, own, 2 * HB,
                              lambda u, slot, turn: rest_parts(u + (SPLIT_BEFORE[n] + 1), slot))

            def add_residual(name, n, per_unit, gate_at, both):
                g0 = first[name]

                def unit(u, g, slot, turn):
                    dve.wait_ge(unit_done, g + 1 + RING)
                    for j in range(per_unit):
                        s = (slot - g0) % 2 * per_unit + j
                        m = u * per_unit + j
                        hx = h[:, ds(m, 1), 0:NX].rearrange("p a n -> p (a n)")
                        ins = dve.scalar_tensor_tensor(hx, bank(2 * s), gate_at(m, 0), hx, ALU.mult, ALU.add)
                        if both:
                            hc = h[:, ds(m, 1), NX:T].rearrange("p a n -> p (a n)")
                            ins = dve.scalar_tensor_tensor(hc, bank(2 * s + 1, NCTX), gate_at(m, 1), hc, ALU.mult, ALU.add)
                        ins.then_inc(res_done, 1)
                for_units(dve, plan, name, unit)

            def attention(att, staged, probs, keysT, bias):
                NJ, NP = att.jobs, att.pieces
                with dve.Fori(0, att.tiles) as i:
                    own.enter(i, att.own_steps)

                    def row_max(j):
                        dve.wait_ge(scores_done, i * NJ + (att.job0 + j + 1))
                        if bias(i, j):
                            src = probs[:, j % 3, 0:att.width]
                            own.wait()
                        else:
                            at = att.scores_at(j)
                            src = psum[:, at:at + att.width]
                        dve.tensor_reduce(nmax[:, j % 4:j % 4 + 1], src, AX.X, ALU.max, negate=True).then_inc(max_done, 1)

                    def normalise(j):
                        dve.wait_ge(exp_done, i * NJ + (att.job0 + j + 1))
                        own.link(dve.reciprocal(rinv[:, j % 4:j % 4 + 1], rsum[:, j % 4:j % 4 + 1]))
                        p = probs[:, j % 3, 0:att.width]
                        dve.tensor_scalar(p, p, rinv[:, j % 4:j % 4 + 1], None, ALU.mult).then_inc(probs_ready, 1)

                    def take(j):
                        for p in att.on_dve:
                            dve.wait_ge(turned, i * (NJ * NP) + (att.piece0 + j * NP + p + 1))
                            lo, hi = att.keys_of(p)
                            dve.tensor_copy(keysT[:, j % 2, lo:hi], psum[:, 2048 + lo:2048 + hi]).then_inc(turned_dve, 1)

                    copies = staged(i)
                    for n, (dst, src) in enumerate(copies):
                        ins = dve.tensor_copy(dst, src)
                        if n < len(copies) - 1:
                            own.mark(ins)
                    ins.then_inc(q_staged, 1)
                    row_max(0)
                    row_max(1)
                    normalise(0)
                    row_max(2)
                    take(0)
                    for j in range(NJ):
                        if j + 1 < NJ:
                            normalise(j + 1)
                        if j + AHEAD < NJ:
                            row_max(j + AHEAD)
                        if j + 1 < NJ:
                            take(j + 1)
                    dve.wait_ge(heads_done, i * NJ + (att.job0 + NJ))
                    own.leave(att.tiles)

            def turned_before(att, i, j):
                if j >= 3:
                    dve.wait_ge(turned, i * (att.jobs * att.pieces) + (att.piece0 + (j - 2) * att.pieces))

            def block1_attention(att, l, t0, latent):
                def staged(i):
                    return [(qst_1[:, 0:2, :], proj[:, QA:QA + 2, ds(i * P + t0, P)]),
                            (qst_1[:, 2:6, :], proj[:, QG:QG + 4, ds(i * P + t0, P)])]

                def bias(i, j):
                    if not latent or j >= 4:
                        return False
                    turned_before(att, i, j)
                    at = att.scores_at(j)
                    own.mark(dve.tensor_tensor(probs_1[:, j % 3, 0:NX], psum[:, at:at + NX],
                                               rpb[:, j, ds(i * (-2 * GRID) + 7 * GRID, NX)], ALU.add))
                    own.mark(dve.tensor_copy(probs_1[:, j % 3, NX:T], psum[:, at + NX:at + T]))
                    return True
                attention(att, staged, probs_1, keysT_1, bias)

            def qk_norm(l):
                for n in range(5):
                    c = QG + n
                    w = T if keeps_ctx(l, c) else NX
                    gain_col = qkg[:, 2 * l + (c == KG):2 * l + (c == KG) + 1]
                    dve.wait_ge(qk_root_done, 5 * l + n + 1)
                    own.link(dve.reciprocal(qk_rs[:, n % 2, 0:w], qk_rs[:, n % 2, 0:w]))
                    dve.scalar_tensor_tensor(proj[:, c, 0:w], proj[:, c, 0:w], gain_col, qk_rs[:, n % 2, 0:w],
                                             ALU.mult, ALU.mult).then_inc(qk_normed, 1)
                    dve.wait_ge(qk_normed, 5 * l + n + 1)
                    dve.wait_ge(qk_rotated, 5 * l + n + 1)
                    own.mark(dve.tensor_tensor(rope_t[:, 0, :], proj[:, c, 0:NX], cos_t, ALU.mult))
                    own.link(dve.tensor_tensor(rope_t[:, 1, :], bank(6 + n % 2), sin_t, ALU.mult))
                    dve.tensor_tensor(proj[:, c, 0:NX], rope_t[:, 0, :], rope_t[:, 1, :], ALU.add).then_inc(qk_roped, 1)
                    if n == 4:
                        dve.wait_ge(qk_roped, 5 * (l + 1))

            def pooling(l):
                w = POOL_W if both_in[l] else PAD + NX + PAD
                add = ALU.add
                dve.wait_ge(proj_done, PER_PROJ * l + UU + 2)
                own.link(dve.tensor_tensor(win2[:, :, 1:w], upad[:, :, 1:w], upad[:, :, 0:w - 1], add))
                own.link(dve.tensor_tensor(win4[:, :, 2:w - 1], win2[:, :, 1:w - 2], win2[:, :, 3:w], add))
                own.link(dve.tensor_tensor(win8[:, 4:w - 3], win4[:, 1, 2:w - 5], win4[:, 1, 6:w - 1], add))
                own.link(dve.tensor_tensor(win16[:, 8:w - 7], win8[:, 4:w - 11], win8[:, 12:w - 3], add))
                lo, hi = PAD, w - PAD
                for k, half, win in ((0, 0, win2[:, 0, :]), (0, 1, win4[:, 0, :]), (1, 0, win8), (1, 1, win16)):
                    q = slice(64 * half, 64 * half + 64)
                    own.link(dve.tensor_tensor(pool_y[q, k, lo:hi], win[q, lo:hi], pool_inv[q, k, lo:hi], ALU.mult))
                    ins = dve.tensor_tensor(pool_y[q, k, lo:hi], pool_y[q, k, lo:hi], upad[q, k, lo:hi], ALU.subtract)
                    if half == 0:
                        own.mark(ins)
                    else:
                        ins.then_inc(pool_ready, 1)

            def mix(l):
                dve.wait_ge(scaled_done, KC * (3 * l + 2))
                dve.memset(upad, 0.0).then_inc(upad_ready, 1)
                dve.wait_ge(table_in, TAB_MIX[l])
                qk_norm(l)
                pooling(l)
                dve.wait_ge(proj_done, PER_PROJ * (l + 1))
                dve.wait_ge(pool_done, 2 * l + 2)
                block1_attention(att_x[l], l, 0, True)
                if both_in[l]:
                    block1_attention(att_c0, l, NX, False)

            def gates(n0, dst):
                for c in range(4):
                    dve.wait_ge(gate_act, n0 + c + 1)
                    dve.tensor_tensor(dst[:, c, :], dst[:, c, :], gate_t[:, c % 2, :], ALU.mult).then_inc(gate_mul, 1)

            def hyena():
                freq = fw[0:HD, 3 * HD:3 * HD + 1]
                for n in range(3):
                    dve.wait_ge(f_mm, n + 1)
                    arg, turns, rest = (f_tmp[0:HD, k, :] for k in range(3))
                    own.link(dve.tensor_scalar(rest, psum[0:HD, 0:NX], fw[0:HD, 3 * HD + 1 + n:3 * HD + 2 + n], freq,
                                               ALU.add, ALU.mult))
                    own.link(dve.tensor_scalar(turns, rest, 1 / (2 * math.pi), ROUND_MAGIC, ALU.mult, ALU.add))
                    own.link(dve.tensor_scalar(turns, turns, -ROUND_MAGIC, None, ALU.add))
                    own.link(dve.scalar_tensor_tensor(rest, turns, -TWO_PI_HI, rest, ALU.mult, ALU.add))
                    own.link(dve.scalar_tensor_tensor(rest, turns, -TWO_PI_LO, rest, ALU.mult, ALU.add))
                    dve.tensor_scalar(arg, rest, PI_BELOW, -PI_BELOW, ALU.min, ALU.max).then_inc(f_arg, 1)
                dve.wait_ge(f_sin, 3)
                own.mark(dve.memset(cpad[:, :, 0:1], 0.0))
                dve.memset(cpad[:, :, NX + 1:NX + 2], 0.0).then_inc(cpad_zero, 1)
                for c in range(12):
                    dve.wait_ge(conv_in, c + 1)

                    def tap(k):
                        return vec2[:, OCW + 12 * k + c:OCW + 12 * k + c + 1]
                    own.link(dve.tensor_scalar(vxx[:, c, :], cpad[:, c % 2, 0:NX], tap(0), vec2[:, OCB + c:OCB + c + 1],
                                               ALU.mult, ALU.add))
                    own.link(dve.scalar_tensor_tensor(vxx[:, c, :], cpad[:, c % 2, 1:NX + 1], tap(1), vxx[:, c, :],
                                                      ALU.mult, ALU.add))
                    dve.scalar_tensor_tensor(vxx[:, c, :], cpad[:, c % 2, 2:NX + 2], tap(2), vxx[:, c, :],
                                             ALU.mult, ALU.add).then_inc(conv_out, 1)
                dve.wait_ge(conv_out, 12)
                dve.wait_ge(table_in, TAB_W4[0])
                for o in range(2):
                    for t in range(QC):
                        for r, dst in enumerate((hf, hb)):
                            n = 8 * o + 2 * t + r
                            dve.wait_ge(fh_mm, n + 1)
                            if o == 1:
                                dve.wait_ge(zi_mm, 4)
                            dve.tensor_tensor(dst[:, t, :], bank(n % 4), decay[:, t, :], ALU.mult).then_inc(fh_out, 1)
                        dve.wait_ge(fh_out, 8 * o + 2 * t + 2)
                        if t == 0:
                            own.link(dve.memset(hb[0:1, 0, :], 0.0))
                        own.link(dve.tensor_tensor(mul_t[:, 0, :], hb[:, t, :], hf[:, t, :], ALU.subtract))
                        own.link(dve.tensor_tensor(hf[:, t, :], hf[:, t, :], hb[:, t, :], ALU.add))
                        dve.tensor_copy(hb[:, t, :], mul_t[:, 0, :]).then_inc(fh_ready, 1)
                    for q in range(4):
                        if q > 0:
                            dve.wait_ge(zf_out, 4 * o + q)
                        dve.wait_ge(zf_mm, 4 * o + q + 1)
                        dve.wait_ge(ft_out, 4 * o + q + 1)
                        A, B = bank(2 * (q % 2)), bank(2 * (q % 2) + 1)
                        own.mark(dve.tensor_tensor(mul_t[:, 0, :], H_re[:, q, :], A, ALU.mult))
                        own.link(dve.tensor_tensor(mul_t[:, 1, :], H_im[:, q, :], B, ALU.mult))
                        own.link(dve.tensor_tensor(y_re[:, q, :], mul_t[:, 0, :], mul_t[:, 1, :], ALU.add))
                        own.mark(dve.tensor_tensor(mul_t[:, 0, :], H_re[:, q, :], B, ALU.mult))
                        own.link(dve.tensor_tensor(mul_t[:, 1, :], H_im[:, q, :], A, ALU.mult))
                        dve.tensor_tensor(y_im[:, q, :], mul_t[:, 0, :], mul_t[:, 1, :], ALU.subtract).then_inc(zf_out, 1)
                    dve.wait_ge(zf_out, 4 * (o + 1))
                    for c in range(4):
                        dve.wait_ge(zi_mm, 4 * o + c + 1)
                        fb = vec2[:, OFB + 4 * o + c:OFB + 4 * o + c + 1]
                        own.link(dve.scalar_tensor_tensor(mul_t[:, c % 2, :], vxx[:, c, :], fb, bank(4 + c % 2),
                                                          ALU.mult, ALU.add))
                        dve.tensor_tensor(vxx[:, c, :], mul_t[:, c % 2, :], vxx[:, 4 + 4 * o + c, :], ALU.mult)\
                           .then_inc(zi_out, 1)
                    dve.wait_ge(zi_out, 4 * (o + 1))
                gates(4, vxx)

            def merge():
                g0 = first["merge_h"]
                for c in range(KC):
                    dve.wait_ge(merge_sig, c + 1)
                    dve.wait_ge(unit_done, g0 + 3 * (c // 2) + 3 + RING)
                    if c > 0:
                        dve.wait_ge(merge_out, c)
                    for r in range(2):
                        own.mark(dve.tensor_tensor(mt_t[:, r, :], sg_t[:, c % 2, r * NX:(r + 1) * NX],
                                                   bank(4 + 2 * (c % 2) + r), ALU.mult))
                    own.wait()
                    dve.tensor_tensor(merged[:, c, :], mt_t[:, 0, :], mt_t[:, 1, :], ALU.add).then_inc(merge_out, 1)
                g0 = first["out_h"]
                for c in range(KC):
                    dve.wait_ge(unit_done, g0 + c // 2 + 1 + RING)
                    own.link(dve.tensor_scalar(mt_t[:, c % 2, :], bank(c % 4), vec2[:, OBO + c:OBO + c + 1],
                                               mod2[:, 2 * KC + c:2 * KC + c + 1], ALU.add, ALU.mult))
                    dve.scalar_tensor_tensor(res[:, c, :], x2[:, c, :], ALPHA, mt_t[:, c % 2, :], ALU.mult, ALU.add)\
                       .then_inc(out2_done, 1)
                dve.wait_ge(out2_done, KC)
                dve.wait_ge(mean_done, 1)
                centre(res, res)
                scale_rows(RMS + 1, res, res, sg_t[:, 0, :], NX)

            def centre(src, dst):
                for c in range(KC):
                    dve.scalar_tensor_tensor(dst[:, c, :], bank(4), -1.0 / D, src[:, c, :], ALU.mult, ALU.add)\
                       .then_inc(centred, 1)

            own.mark(dve.memset(eps[:, 0:1], EPS))
            own.mark(dve.memset(eps[:, 1:2], LN_EPS))
            own.mark(dve.memset(ones[:, 0:1], 1.0))
            dve.memset(ones[:, 2:3], 1.0).then_inc(res_done, FREE)
            dve.wait_ge(consts_in, N_CONSTS)
            for l in range(DEPTH):
                own.mark(dve.tensor_scalar(qkg[:, 2 * l:2 * l + 1], small[:, 4 * l + 2:4 * l + 3], SCORE_SCALE, None, ALU.mult))
                own.mark(dve.tensor_copy(qkg[:, 2 * l + 1:2 * l + 2], small[:, 4 * l + 3:4 * l + 4]))
            own.mark(dve.tensor_scalar(bq[:], vec2[:, OB_IN:OB_IN + 12], SCORE_SCALE, None, ALU.mult))
            own.wait()
            dve.memset(ones[:], 1.0).then_inc(setup_done, 1)
            own.link(dve.memset(c_parts_t[:].bitcast(F32), 0.0))
            dve.wait_ge(silu_c, 1)
            own.link(dve.tensor_copy(c_parts[:, :, 0:3], cv))
            dve.tensor_tensor(c_parts[:, :, 3:6], cv, c_parts[:, :, 0:3].bitcast(F32), ALU.subtract).then_inc(c_ready, 1)
            for t in range(GROUPS_FIRST + 1):
                if t < GROUPS_FIRST:
                    for u in (2 * t, 2 * t + 1):
                        rest_parts(u + 1, u % RING)
                if t > 0:
                    take_vectors(t - 1, 0, 0, 7 - (t - 1) % 2)
            for l in range(DEPTH):
                gate = mod[l][:, 5, :, :]

                def half_of(k):
                    return lambda m, s: hgate[:, k, m, s:s + 1]

                if on(f"ffn1_{l}"):
                    first_rests(f"ffn1_{l}", 2 * l)
                    modulation(l, 0)
                    scale_and_split(3 * l, 2 * l, T)
                    ffn(f"ffn1_{l}", 2 * l, 3 * l, half_of(0), True)
                if on(f"mix{l}"):
                    dve.wait_ge(res_done, FREE + added_before(3 * l + 1))
                    modulation(l, 1)
                    scale_rows(3 * l + 1, h, a, rstd, T)
                    mix(l)
                    add_residual(f"out{l}", 3 * l + 1, 2,
                                 lambda m, s: gate[:, ds(m, 1), s:s + 1].rearrange("p a b -> p (a b)"), both_in[l])
                if on(f"ffn2_{l}"):
                    dve.wait_ge(res_done, FREE + added_before(3 * l + 2))
                    first_rests(f"ffn2_{l}", 2 * l + 1)
                    modulation(l, 2)
                    scale_and_split(3 * l + 2, 2 * l + 1, T if both_in[l] else NX)
                    ffn(f"ffn2_{l}", 2 * l + 1, 3 * l + 2, half_of(1), both_in[l])
                    dve.wait_ge(res_done, FREE + added_before(3 * l + 3))
            if on("final"):
                scale_rows(RMS - 1, h, x2, rstd, NX)
            if on("qkv_h"):
                dve.wait_ge(mods_done, 2 * ADA_GROUPS + 3 * KC // 4)
                own.link(dve.tensor_scalar(gain2[:], mod2[:, KC:2 * KC], 1.0, None, ALU.add))
                dve.wait_ge(mean_done_0, 1)
                centre(x2, h2)
                dve.wait_ge(centred, KC)
                scale_rows(RMS, h2, h2, rstd2, NX)
                dve.wait_ge(table_in, TAB_QKV)
                for u in range(6):
                    dve.wait_ge(unit_done, first["v_h"] + u + 1 + RING)
                    for t in range(QC):
                        dve.tensor_tensor(vh[:, t, 256 * u:256 * (u + 1)], bank(4 + t, 256), vbias[:, 256 * u:256 * (u + 1)],
                                          ALU.add).then_inc(v2_out, 1)
            if on("att_h"):
                dve.wait_ge(qk2_out, 24)
                dve.wait_ge(v2_out, 24)

                def staged(i):
                    return [(qst_2, qh[:, :, ds(i * P, P)]), (kst, kh[:, 4:12, ds(i * P, P)]),
                            (vst, vh[:, ds(i, 1), 512:1536].rearrange("p a (g n) -> p (a g) n", g=2))]

                def bias(i, j):
                    turned_before(att_h, i, j)
                    at, p = att_h.scores_at(j), probs_2[:, j % 3, :]
                    slope = 2.0 ** -(j + 1)
                    own.mark(dve.scalar_tensor_tensor(p[:, 0:NX], alibi[:, ds(i * (-P) + 3 * P, NX)], slope,
                                                      psum[:, at:at + NX], ALU.mult, ALU.add))
                    own.mark(dve.scalar_tensor_tensor(p[:, NX:KEYS2], alibi[:, 7 * P:9 * P], slope,
                                                      psum[:, at + NX:at + KEYS2], ALU.mult, ALU.add))
                    return True
                attention(att_h, staged, probs_2, keysT_2, bias)
                gates(0, y_attn)
            if on("hyena"):
                hyena()
            if on("merge"):
                merge()


def constants():
    t = np.arange(NX)
    inv = (10000.0 ** (-np.arange(0, HD // 2, 2, dtype=np.float32) / np.float32(HD // 2))).astype(np.float32)
    ang = np.stack([(t // GRID).astype(np.float32)[:, None] * inv, (t % GRID).astype(np.float32)[:, None] * inv])
    c64 = np.concatenate([np.cos(ang[0]), np.cos(ang[0]), np.cos(ang[1]), np.cos(ang[1])], 1).T
    s64 = np.concatenate([-np.sin(ang[0]), np.sin(ang[0]), -np.sin(ang[1]), np.sin(ang[1])], 1).T
    cos_t, sin_t = (np.concatenate([x, x]).astype(np.float32) for x in (c64, s64))
    rot = np.zeros((P, P), np.float32)
    for i in range(P):
        rot[i ^ 16, i] = 1.0
    pairs = np.kron(np.eye(2), np.ones((HD, HD))).astype(np.float32)
    fold = np.zeros((P, 3), np.float32)
    fold[0:3], fold[3:6] = np.eye(3), np.eye(3)
    cst = np.concatenate([np.eye(P, dtype=np.float32), rot, pairs, fold], 1)
    inv_count = np.zeros((P, 2, POOL_W), np.float32)
    for n, at in ((NX, POOL_X), (NCTX, POOL_C)):
        s = np.arange(n)
        for g, w in enumerate((2, 4, 8, 16)):
            count = np.clip(s - w // 2 + w, 0, n) - np.clip(s - w // 2, 0, n)
            inv_count[64 * (g % 2):64 * (g % 2) + 64, g // 2, at:at + n] = 1.0 / count
    alibi = np.full((P, 9, P), NEG, np.float32)
    step = np.arange(P)[None, :] - np.arange(P)[:, None]
    for k in range(7):
        dist = np.abs(RES * step + k - 3)
        alibi[:, k][dist <= 64] = -dist[dist <= 64]
    for k, dil in ((7, 4), (8, 16)):
        dist = np.abs(RES * step)
        valid = (dist % dil == 0) & (dist <= 64 * dil)
        alibi[:, k][valid] = -dist[valid]
    alibi = alibi.reshape(P, 9 * P)
    tl = np.linspace(0.0, 1.0, NX, dtype=np.float32)[:, None]
    w = (np.float32(2.0 * math.pi) * np.arange(NX, dtype=np.float32)[:, None] / np.float32(NX)).astype(np.float32)
    f = np.linspace(1e-4, 15, 16, dtype=np.float32)[None, :]
    fw_ = (f * w).astype(np.float32)
    feats = np.concatenate([tl, np.cos(fw_), -np.sin(fw_)], 1).T.astype(np.float32)
    deltas = np.linspace(math.log(1e-2) / 1.5, math.log(1e-2) / 0.3, NX, dtype=np.float32)
    decay = np.exp(-tl * np.abs(deltas)[None, :]).astype(np.float32)
    th = np.pi * (2 * np.arange(NX)[None, :] + 1) * np.arange(NX)[:, None] / (2 * NX)
    def tiles(m):
        return m.reshape(4, P, NX).transpose(1, 0, 2).astype(np.float32)
    dft = np.concatenate([tiles(np.cos(th)), tiles(np.sin(th)), tiles(np.cos(th.T) / NX), tiles(np.sin(th.T) / NX)], 1)
    return dict(cos_t=cos_t, sin_t=sin_t, cst=cst, pool_inv=inv_count, alibi=alibi, feats=np.ascontiguousarray(feats),
                decay=tiles(decay), dft=np.ascontiguousarray(dft))


def blocked(w, cols_per_unit):
    k, m = w.shape
    v = w.reshape(k // P, P, m // P // cols_per_unit, cols_per_unit, P)
    return np.ascontiguousarray(v.transpose(2, 1, 3, 0, 4)).reshape(m // P // cols_per_unit, P, -1)


def as_rhs(w, cols):
    k, m = w.shape
    v = w.reshape(k // P, P, m // cols, cols)
    return np.ascontiguousarray(v.transpose(2, 1, 0, 3)).reshape(m // cols, P, -1)


def columns(v):
    return v.reshape(-1, P).T


def layout(inputs):
    x = {k: np.asarray(v) for k, v in inputs.items()}
    d = dict(constants())
    d["xT"] = x["x"][0].T.reshape(KC, P, NX).transpose(1, 0, 2)
    d["ctxT"] = x["ctx"][0].T.reshape(KC, P, NCTX).transpose(1, 0, 2)
    d["cvec"] = np.stack([columns(x["c"][0]), columns(x["c_ctx"]), columns(x["c_2"][0])], 2).reshape(P, -1)
    d["b_ada"] = np.repeat(np.concatenate([columns(x["b_ada"][l]) for l in range(DEPTH)], 1), 2, axis=1)
    d["ng"] = np.concatenate([np.repeat(np.concatenate([columns(x["norm_g"][l, k]) for l in range(DEPTH) for k in range(3)], 1),
                                        2, axis=1), columns(x["final_g"])], 1)
    small = []
    for l in range(DEPTH):
        small += [columns(x["pool_scale"][l]), np.tile(x["q_norm_g"][l], 2)[:, None], np.tile(x["k_norm_g"][l], 2)[:, None]]
    d["small"] = np.concatenate(small, 1)
    poolw = np.zeros((P, DEPTH, 2, P), np.float32)
    for l in range(DEPTH):
        for g in range(4):
            r = 64 * (g % 2)
            poolw[r:r + 64, l, g // 2, r:r + 64] = x["pool_w"][l, g]
    d["poolw"] = poolw.reshape(P, -1)
    d["vec2"] = np.concatenate(
        [columns(x["b_ada_2"][0]), columns(x["b_in_2"][0])] + [columns(x["conv_w_2"][0, k]) for k in range(3)]
        + [columns(x["conv_b_2"][0])] + [columns(x["filt_bias_2"][0, o]) for o in range(2)]
        + [columns(x["b_out_2"][0]), columns(x["ln_g_2"][0]), columns(x["ln_b_2"][0])], 1)
    fw = np.zeros((HD, 3 * HD + 4), np.float32)
    fw[0:33, 0:HD] = x["filt_w1_2"][0]
    fw[:, HD:2 * HD], fw[:, 2 * HD:3 * HD] = x["filt_w2_2"][0], x["filt_w3_2"][0]
    for k, name in enumerate(("filt_freq_2", "filt_b1_2", "filt_b2_2", "filt_b3_2")):
        fw[:, 3 * HD + k] = x[name][0]
    d["fw"] = fw
    d["w4_0"], d["w4_1"] = x["filt_w4_2"][0][:, 0:2 * NX], x["filt_w4_2"][0][:, 2 * NX:4 * NX]
    order = np.concatenate([np.arange(HD) + HD * n for i in range(4) for n in (i, 4 + i)])
    col = np.arange(GRID)
    c0 = np.clip(col - 8, 0, GRID - 16)
    seen = (col[None, :] >= c0[:, None]) & (col[None, :] < c0[:, None] + 16)
    dx = np.clip(col[None, :] - col[:, None], -15, 15) + 15
    ada = np.concatenate([as_rhs(w, 256) for w in (x["w_ada"][0], x["w_ada"][1], x["w_ada_2"][0])])
    d["ada0"] = ada[0:2 * GROUPS_FIRST]
    for l in range(DEPTH):
        wi = x["w_in"][l]
        for k in (1, 2):
            up = x[f"ffn{k}_up"][l]
            pairs = np.stack([up[:, :FF].reshape(D, FC, P), up[:, FF:].reshape(D, FC, P)], 2).reshape(D, 2 * FF)
            ups, down = blocked(pairs, 2), x[f"ffn{k}_down"][l]
            n = 2 * l + k - 1
            (first_two, last), group = ffn_schedules(n), groups_before(n)
            units, at = np.zeros((ffn_units(n), P, SLOT), np.float32), 0
            for b, schedule in enumerate((first_two, first_two, last)):
                lo, hi = b * HB, min((b + 1) * HB, FC)
                downs = blocked(down[lo * P:hi * P], 2)
                for kind, j, half in schedule:
                    if kind == "up":
                        units[at] = ups[lo + j]
                    elif kind == "down":
                        units[at, :, 0:2 * (hi - lo) * P] = downs[j]
                    else:
                        units[at] = ada[2 * group + half]
                        group += half
                    at += 1
            d[f"ffn{k}_{l}"] = units
        u = np.zeros((8, P, 2 * D), np.float32)
        cols = np.concatenate([wi[:, 1024:1536][:, order], wi[:, 1536:1664], wi[:, 768:1024], wi[:, 0:512]], 1)
        u[0:5] = blocked(cols[:, 0:10 * P], 2)
        u[5, :, 0:D] = blocked(cols[:, 10 * P:], 1)[0]
        u[6] = as_rhs(wi[:, 512:768], 256)[0]
        u[7, :, 0:D] = as_rhs(wi[:, 1664:1792], 128)[0]
        d[f"in{l}"] = u
        wo = x["w_out"][l]
        d[f"out{l}"] = blocked(np.concatenate([wo[0:512], wo[512:1024][order]], 0), 2)
        table = np.where(seen[None, None], x["na_rpb"][l][:, :, dx], np.float32(NEG)).transpose(2, 0, 1, 3)
        rpb = np.zeros((P, 4, 15, GRID), np.float32)
        rpb[0:64] = table
        rpb[64:128, :, 1:15] = table[:, :, 0:14]
        d[f"rpb{l}"] = rpb.reshape(P, 4, 15 * GRID)
    w2 = x["w_in_2"][0]
    d["q_h"], d["k_h"] = blocked(w2[:, 0:1536], 2), blocked(w2[:, 1536:3072], 2)
    d["v_h"] = as_rhs(w2[:, 3072:4608], 256)
    d["vbias"] = np.broadcast_to(x["b_in_2"][0][3072:4608], (P, 1536))
    d["gattn_h"] = blocked(w2[:, 4608:5120], 2)
    d["conv_h"] = blocked(w2[:, 5120:6656], 2)
    d["ghy_h"] = blocked(w2[:, 6656:7168], 2)
    r = np.stack([w2[:, 7168:8192].reshape(D, KC, P), w2[:, 8192:9216].reshape(D, KC, P)], 2).reshape(D, 2 * D)
    r = blocked(r, 2)
    pj = np.stack([x["w_proj_attn_2"][0].reshape(512, KC, P), x["w_proj_hyena_2"][0].reshape(512, KC, P)], 2).reshape(512, 2 * D)
    pj = blocked(pj, 4)
    m = np.zeros((12, P, 2 * D), np.float32)
    for q in range(4):
        m[3 * q], m[3 * q + 1], m[3 * q + 2] = r[2 * q], r[2 * q + 1], pj[q]
    d["merge_h"] = m
    d["out_h"] = blocked(x["w_out_2"][0], 2)
    return {k: np.ascontiguousarray(v) for k, v in d.items()}


def kernel(**inputs):
    import concourse.bacc as bacc
    from concourse.bass_utils import run_bass_kernel_spmd

    arrays = layout(inputs)
    nc = bacc.Bacc("TRN2", target_bir_lowering=False, num_devices=1)
    io = {k: nc.dram_tensor(f"in_{k}", v.shape, mybir.dt.from_np(v.dtype), kind="ExternalInput").ap()
          for k, v in arrays.items()}
    out = nc.dram_tensor("out_T", (KC, P, NX), F32, kind="ExternalOutput").ap()
    hybrid_kernel(nc, io, out)
    r = run_bass_kernel_spmd(nc, [{f"in_{k}": v for k, v in arrays.items()}], core_ids=[0])
    return r.results[0]["out_T"].reshape(D, NX).T.reshape(1, NX, D)
```

```python
import math
from contextlib import ExitStack

import numpy as np

import concourse.bass as bass
from concourse import mybir

F32 = mybir.dt.float32
F32R = mybir.dt.float32r
ALU = mybir.AluOpType
ACT = mybir.ActivationFunctionType
AX = mybir.AxisListType
ds = bass.ds

P = 128
D = 1024
KC = D // P
NX, NCTX = 512, 256
T = NX + NCTX
DEPTH = 2
FF = 2816
FC = FF // P
NMOD = 9
HD = 64
EPS, LN_EPS = 1e-6, 1e-5
GRID = 64
NEG = -1e30
SCORE_SCALE = HD ** -0.5
PAD = 16
POOL_X, POOL_C, POOL_W = PAD, 2 * PAD + NX, 3 * PAD + T
ALPHA = 2 ** 0.25
NH2 = 8
RES = 4
KEYS2 = NX + 2 * P
AHEAD, PROBS = 3, 4
FREE_HEADS = 2
RING, SLOT = 4, 2 * D
FREE = 4
HB, DOWN = 8, KC // 2
LAST_HB = FC - 2 * HB
ADA_GROUPS = NMOD * KC // 4
GROUPS_FIRST = ADA_GROUPS // 3
FFN_GROUPS = ((6, 2), (6, 4), (0, 4), (0, 2))
PART_CHUNKS = (3 * KC, KC, 3 * KC)
QC = NX // P
TWO_PI_HI = 6.28125
TWO_PI_LO = 2 * math.pi - TWO_PI_HI
ROUND_MAGIC = 12582912.0
PI_BELOW = 3.1415925

NET_AFTER, NET_ARGUMENT_AFTER = [3, 7, 9], [1, 5, 7]

QG, KG, UU, QA, KA, NPROJ = 0, 4, 5, 7, 9, 11


def weight_plan():
    plan, at = {}, 0

    def add(name, n):
        nonlocal at
        plan[name] = (at, n)
        at += n

    for l in range(DEPTH):
        if l == 0:
            add("ada0", 2 * GROUPS_FIRST)
        add(f"ffn1_{l}", ffn_units(2 * l))
        add(f"in{l}", 8)
        add(f"out{l}", KC // 2)
        add(f"ffn2_{l}", ffn_units(2 * l + 1))
    add("q_h", 6)
    add("k_h", 6)
    add("v_h", 6)
    add("gattn_h", 2)
    add("conv_h", 6)
    add("ghy_h", 2)
    add("merge_h", 3 * KC // 2)
    add("out_h", KC // 2)
    return plan


class Chain:

    def __init__(self, eng, sem):
        self.eng, self.sem, self.n, self.i = eng, sem, 0, None

    def mark(self, ins):
        ins.then_inc(self.sem, 1)
        self.n += 1

    def wait(self):
        self.eng.wait_ge(self.sem, self.n if self.i is None else self.i * self.per + self.n)

    def link(self, ins):
        self.mark(ins)
        self.wait()

    def enter(self, i, per):
        self.i, self.per, self.n0 = i, per, self.n

    def leave(self, trips):
        assert self.n - self.n0 == self.per, (self.n - self.n0, self.per)
        self.n, self.i = self.n0 + trips * self.per, None


def for_units(eng, plan, name, body):
    g0, n = plan[name]
    trips = n // RING if n >= 2 * RING else 0
    if trips:
        with eng.Fori(0, trips) as i:
            for j in range(RING):
                k = g0 + j
                body(i * RING + j, i * RING + k, k % RING, i + k // RING)
    for u in range(trips * RING, n):
        body(u, g0 + u, (g0 + u) % RING, (g0 + u) // RING)


def added_before(n):
    return n // 3 * sum(PART_CHUNKS) + sum(PART_CHUNKS[:n % 3])


def groups_before(n):
    return GROUPS_FIRST + sum(2 * a + b for a, b in FFN_GROUPS[:n])


def block_schedule(n_hid, groups):
    units, pending = [], None
    for j in range(n_hid):
        units.append(("up", j, pending))
        pending = None
        if 2 <= j < 2 + groups:
            pending = j - 2
            units += [("ada", pending, 0), ("ada", pending, 1)]
    for j in range(DOWN):
        units.append(("down", j, pending))
        pending = None
    return units


def ffn_schedules(n):
    return block_schedule(HB, FFN_GROUPS[n][0]), block_schedule(LAST_HB, FFN_GROUPS[n][1])


def ffn_units(n):
    first_two, last = ffn_schedules(n)
    return 2 * len(first_two) + len(last)


LEAD = RING - 1
SPLIT_BEFORE = [2 * GROUPS_FIRST + sum(ffn_units(m) for m in range(n)) for n in range(2 * DEPTH + 1)]


def for_ffn_units(eng, plan, name, n, up, down, ada, loop=None, loop_marks=0, ahead=None):
    g0, _ = plan[name]
    first_two, last = ffn_schedules(n)
    size = len(first_two)
    assert size % RING == 0

    def block(b, units, n_hid, ends):
        for i, (kind, j, more) in enumerate(units):
            u, g, slot = b * size + i, b * size + (g0 + i), (g0 + i) % RING

            def go_ahead():
                if ahead and (not ends or i + LEAD < len(units)):
                    k = g0 + i + LEAD
                    ahead(u + LEAD, k % RING, b * (size // RING) + k // RING)
            if kind == "ada":
                ada(b, j, more, u, g, slot)
                go_ahead()
            elif kind == "up":
                go_ahead()
                up(b, j, u, g, slot, more)
            else:
                go_ahead()
                down(b, j, u, g, slot, more, n_hid)

    with eng.Fori(0, 2) as b:
        if loop:
            loop.enter(b, loop_marks)
        block(b, first_two, HB, False)
    if loop:
        loop.leave(2)
    block(2, last, LAST_HB, True)


def for_tiles(eng, att, tile, loop=None):
    n = att.tiles - 1
    if n >= 2:
        with eng.Fori(0, n) as i:
            if loop:
                loop.enter(i, att.own_steps)
            tile(i, False)
        if loop:
            loop.leave(n)
    else:
        for i in range(n):
            tile(i, False)
    tile(n, True)


class Attention:

    def __init__(self, tiles, jobs, width, own_steps, before):
        self.own_steps, self.tiles, self.jobs, self.width = own_steps, tiles, jobs, width
        self.pieces = -(-width // 512)
        self.on_act = [p for p in range(self.pieces) if p % 2 == 0]
        self.on_dve = [p for p in range(self.pieces) if p % 2 == 1]
        b = before
        self.tile0 = b.tile0 + b.tiles if b else 0
        self.job0 = b.job0 + b.tiles * b.jobs if b else 0
        self.job_end = self.job0 + tiles * jobs
        self.piece0 = b.piece0 + b.tiles * b.jobs * b.pieces if b else 0
        self.act0 = b.act0 + b.tiles * b.jobs * len(b.on_act) if b else 0
        self.dve0 = b.dve0 + b.tiles * b.jobs * len(b.on_dve) if b else 0

    def scores_at(self, j):
        return 1024 * (j % 2)

    def keys_of(self, p):
        return 512 * p, min(512 * (p + 1), self.width)

    def evacuated(self, i, j, p):
        mine = self.on_act if p % 2 == 0 else self.on_dve
        first = self.act0 if p % 2 == 0 else self.dve0
        return i * (self.jobs * len(mine)) + (first + j * len(mine) + mine.index(p) + 1)


def hybrid_kernel(nc, io, out):
    plan = weight_plan()
    first = {k: v[0] for k, v in plan.items()}
    after = {k: v[0] + v[1] for k, v in plan.items()}
    att_x0 = Attention(QC, 12, T, 1 + 2 * 4 + 12, None)
    att_c0 = Attention(NCTX // P, 12, NCTX, 1 + 12, att_x0)
    att_x1 = Attention(QC, 12, T, 1 + 2 * 4 + 12, att_c0)
    att_h = Attention(QC, NH2, KEYS2, 1 + 2 * NH2 + NH2, att_x1)
    att_x = [att_x0, att_x1]
    TAB_MIX, TAB_QKV = (64, 128), 160
    TAB_FEATS, TAB_DFT, TAB_W4 = 224, 240, (224, 256)

    ctx = ExitStack()
    with ctx:
        def sb(name, shape):
            return ctx.enter_context(nc.sbuf_tensor(name, shape, F32))

        def sem(name):
            return ctx.enter_context(nc.semaphore(name))

        with nc.sbuf_tensor("ring", [P, RING * SLOT], F32) as ring_t:
            pass
        ring_r = ctx.enter_context(nc.sbuf_tensor("ring_r", [P, RING * SLOT], F32R))
        ring = [ring_t[:, i * SLOT:(i + 1) * SLOT] for i in range(RING)]
        w_lo = [ring_r[:, i * SLOT:(i + 1) * SLOT] for i in range(RING)]
        ARENA = 41216
        rooms = (("h_room", KC * T, F32), ("a_lo", KC * T, F32R), ("a_hi", KC * T, F32R), ("hid_hi", HB * T, F32R),
                 ("hid_lo", HB * T, F32R), ("w_hi", RING * SLOT, F32R), ("sil", 2 * T, F32), ("rstd", T, F32))
        assert sum(n for _, n, _ in rooms) == ARENA
        with ExitStack() as under:
            room = {name: under.enter_context(nc.sbuf_tensor(name, [P, n], t)) for name, n, t in rooms}
        with ExitStack() as under:
            under.enter_context(nc.sbuf_tensor("h_room2", [P, KC * T], F32))
            a_plain = under.enter_context(nc.sbuf_tensor("a_plain", [P, KC * T], F32))
        B0 = KC * (T + NX)
        with ExitStack() as under:
            under.enter_context(nc.sbuf_tensor("low_room", [P, B0 + 24 * NX], F32))
            h2_hi_t = under.enter_context(nc.sbuf_tensor("h2_hi", [P, KC * NX], F32R))
            h2_lo_t = under.enter_context(nc.sbuf_tensor("h2_lo", [P, KC * NX], F32R))
        arena = sb("arena", [P, ARENA])

        def view(at, *dims):
            n = int(np.prod(dims))
            assert at + n <= ARENA, (at, dims)
            v = arena[:, at:at + n]
            if len(dims) == 2:
                return v.rearrange("p (a b) -> p a b", a=dims[0])
            if len(dims) == 3:
                return v.rearrange("p (a b c) -> p a b c", a=dims[0], b=dims[1])
            return v

        A0 = KC * T
        G0 = 2 * KC * T
        W0 = G0 + FC * T
        h = view(0, KC, T)
        a = view(A0, KC, T)
        sq_g = view(G0, KC, T)
        def chunks(t):
            return t[:].rearrange("p (c n) -> p c n", n=T)

        a_f = chunks(a_plain)
        a_lo, a_hi, hid_hi, hid_lo = (chunks(room[k]) for k in ("a_lo", "a_hi", "hid_hi", "hid_lo"))
        w_hi = [room["w_hi"][:, SLOT * s:SLOT * (s + 1)] for s in range(RING)]
        sil = chunks(room["sil"])
        rstd = room["rstd"][:]
        proj = view(G0, NPROJ, T)
        v_tok = view(G0 + NPROJ * T, T // P, 384)
        rpb = view(G0 + NPROJ * T + T // P * 384, 4, 15 * GRID)
        cos_t = view(W0 - 2 * NX, NX)
        sin_t = view(W0 - NX, NX)
        upad = view(W0, 2, POOL_W)
        qk_sq = view(W0 + 2 * POOL_W, 2, T)
        qk_rs = view(W0 + 2 * POOL_W + 2 * T, 2, T)
        rope_t = view(W0 + 2 * POOL_W + 4 * T, 2, NX)
        win2 = view(W0 + 2 * POOL_W, 2, POOL_W)
        win4 = view(W0 + 4 * POOL_W, 2, POOL_W)
        win8 = view(W0 + 6 * POOL_W, POOL_W)
        win16 = view(W0 + 7 * POOL_W, POOL_W)
        pool_y = view(W0 + 8 * POOL_W, 2, POOL_W)
        pool_inv = view(W0 + 10 * POOL_W, 2, POOL_W)
        probs_1 = view(W0, PROBS, T)
        keysT_1 = view(W0 + PROBS * T, 2, T)
        qst_1 = view(W0 + (PROBS + 2) * T, 6, P)

        h2 = view(0, KC, NX)
        h2_hi, h2_lo = (t[:].rearrange("p (c n) -> p c n", n=NX) for t in (h2_hi_t, h2_lo_t))
        h2r = h2.rearrange("p c (u r) -> p c r u", r=RES)
        y_attn = view(4096, 4, NX)
        x2 = view(A0, KC, NX)
        qh = view(B0, 12, NX)
        kh = view(B0 + 12 * NX, 12, NX)
        vh = view(B0 + 24 * NX, QC, 1536)
        alibi = view(B0 + 24 * NX + QC * 1536, 9 * P)
        H0 = B0 + 24 * NX + QC * 1536 + 9 * P
        probs_2 = view(H0, PROBS, KEYS2)
        keysT_2 = view(H0 + PROBS * KEYS2, 2, KEYS2)
        Q0 = H0 + (PROBS + 2) * KEYS2
        qst_2 = view(Q0, 12, P)
        kst = view(Q0 + 12 * P, 8, P)
        vst = view(Q0 + 20 * P, 2, NX)
        vbias = view(H0, 1536)
        sq2 = view(B0, KC, NX)
        rstd2 = view(B0 + KC * NX, NX)
        dft = view(B0, 16, NX)
        vxx = view(B0 + 8192, 12, NX)
        hf = view(B0 + 8192 + 6144, 4, NX)
        hb = view(B0 + 8192 + 8192, 4, NX)
        y_re, y_im = hf, hb
        decay = view(B0 + 18432, 4, NX)
        H_re = view(B0 + 20480, 4, NX)
        H_im = view(B0 + 22528, 4, NX)
        z_tok = view(B0 + 24576, 4, NX)
        cpad = view(B0 + 26624, 2, 520)
        gate_t = view(B0 + 26624, 2, NX)
        mul_t = view(B0 + 26624 + 1040, 2, NX)
        f_hid = view(B0 + 28688, NX)
        f_tmp = view(B0 + 8192 + 6144, 3, NX)
        w4 = view(B0 + 24576, 2 * NX)
        merged = view(B0, KC, NX)
        res = view(B0 + 4096, KC, NX)
        res_sq = view(B0, KC, NX)
        sg_t = view(B0 + 14336, 2, 2 * NX)
        mt_t = view(B0 + 16384, 2, NX)
        fin = view(B0 + 18432, KC, NX)

        cst = sb("cst", [P, 3 * P + 3])
        fold = cst[0:6, 3 * P:]
        c_parts_t = ctx.enter_context(nc.sbuf_tensor("c_parts", [P, KC * P], F32R))
        c_parts = c_parts_t[:].rearrange("p (k m) -> p k m", k=KC)
        ada_rows = sb("ada_rows", [6, 512])
        ident, rot, pairs = (cst[:, k * P:(k + 1) * P] for k in range(3))
        ones = sb("ones", [P, P])
        cvec = sb("cvec", [P, KC * 3])
        cv = cvec[:].rearrange("p (k s) -> p k s", s=3)
        b_ada = sb("b_ada", [P, DEPTH * NMOD * KC * 2])
        mods = [sb(f"mods{l}", [P, NMOD * KC * 2]) for l in range(DEPTH)]
        mod = [m[:].rearrange("p (n c s) -> p n c s", n=NMOD, s=2) for m in mods]
        ng = sb("ng", [P, DEPTH * 3 * KC * 2 + KC])
        ngv = ng[:, 0:DEPTH * 3 * KC * 2].rearrange("p (l k c s) -> p l k c s", l=DEPTH, k=3, s=2)
        final_g = ng[:, DEPTH * 3 * KC * 2:]
        gain = sb("gain", [P, 3 * KC * 2])
        gainv = gain[:].rearrange("p (k c s) -> p k c s", k=3, s=2)
        half_gate = sb("half_gate", [P, 2 * KC * 2])
        hgate = half_gate[:].rearrange("p (k c s) -> p k c s", k=2, s=2)
        small = sb("small", [P, 4 * DEPTH])
        qkg = sb("qkg", [P, 2 * DEPTH])
        poolw = sb("poolw", [P, DEPTH * 2 * P])
        pw = poolw[:].rearrange("p (l k m) -> p l k m", l=DEPTH, k=2)
        nmax = sb("nmax", [P, 4])
        rsum = sb("rsum", [P, 4])
        rinv = sb("rinv", [P, 4])
        vec2 = sb("vec2", [P, 176])
        OB_ADA, OB_IN, OCW, OCB, OFB, OBO, OLG, OLB = 0, 24, 96, 132, 144, 152, 160, 168
        mod2 = sb("mod2", [P, 3 * KC])
        gain2 = sb("gain2", [P, KC])
        bq = sb("bq", [P, 12])
        eps = sb("eps", [P, 2])
        feats = view(B0, NX)
        fw = view(B0 + 28688 + NX, 3 * HD + 4)

        psum = ctx.enter_context(nc.psum_tensor("psum", [P, 4096], F32))

        def bank(b, n=512):
            return psum[:, 512 * b:512 * b + n]

        w_landed = [sem(f"w_landed{i}") for i in range(RING)]
        unit_done = sem("unit_done")
        cvec_in, consts_in = sem("cvec_in"), sem("consts_in")
        table_in = sem("table_in")
        act_own, dve_own = sem("act_own"), sem("dve_own")
        setup_done = sem("setup_done")
        silu_c = sem("silu_c")
        c_ready = sem("c_ready")
        rows_out, rows_turned, mods_done = sem("rows_out"), sem("rows_turned"), sem("mods_done")
        mod_ready = sem("mod_ready")
        mean_done, mean_done_0, centred = sem("mean_done"), sem("mean_done_0"), sem("centred")
        sq_done, ss_done, root_done = sem("sq_done"), sem("ss_done"), sem("root_done")
        scaled_done, normed = sem("scaled_done"), sem("normed")
        silu_done = sem("silu_done")
        hi_done, w_split = sem("hi_done"), sem("w_split")
        a_hi_done, a_split = sem("a_hi_done"), sem("a_split")
        h2_hi_done, h2_split = sem("h2_hi_done"), sem("h2_split")
        hid_done = sem("hid_done")
        res_done = sem("res_done")
        upad_ready = sem("upad_ready")
        even_proj = sem("even_proj")
        proj_done = sem("proj_done")
        qk_sq_done, qk_ss_done, qk_root_done = sem("qk_sq_done"), sem("qk_ss_done"), sem("qk_root_done")
        qk_normed, qk_rotated, qk_roped = sem("qk_normed"), sem("qk_rotated"), sem("qk_roped")
        pool_ready, pool_done, pool_out = sem("pool_ready"), sem("pool_done"), sem("pool_out")
        q_staged, v_staged = sem("q_staged"), sem("v_staged")
        scores_done, max_done, exp_done = sem("scores_done"), sem("max_done"), sem("exp_done")
        turned, turned_act, turned_dve = sem("turned"), sem("turned_act"), sem("turned_dve")
        probs_ready = sem("probs_ready")
        heads_done, heads_out = sem("heads_done"), sem("heads_out")
        qk2_out, v2_out = sem("qk2_out"), sem("v2_out")
        f_mm, f_arg, f_sin = sem("f_mm"), sem("f_arg"), sem("f_sin")
        cpad_zero, conv_in, conv_out = sem("cpad_zero"), sem("conv_in"), sem("conv_out")
        fh_mm, fh_out, fh_ready = sem("fh_mm"), sem("fh_out"), sem("fh_ready")
        ft_mm, ft_out = sem("ft_mm"), sem("ft_out")
        zt_mm, zt_out = sem("zt_mm"), sem("zt_out")
        zf_mm, zf_out = sem("zf_mm"), sem("zf_out")
        zi_mm, zi_out = sem("zi_mm"), sem("zi_out")
        gate_act, gate_mul = sem("gate_act"), sem("gate_mul")
        merge_sig, merge_out, out2_done = sem("merge_sig"), sem("merge_out"), sem("out2_done")
        stored = sem("stored")

        N_CONSTS = 16 * 8
        PER_PROJ = NPROJ + 2 * (T // P)
        RMS = 3 * DEPTH + 1
        both_in = [l < DEPTH - 1 for l in range(DEPTH)]

        def keeps_ctx(l, c):
            return both_in[l] or c in (KA, KA + 1, KG)

        def blocks_of(slot, n, k):
            return ring[slot][:, 0:n * k * P].rearrange("p (n k m) -> p n k m", n=n, k=k)

        block = ctx.enter_context(nc.Block())

        @block.sync
        def _(sp):
            def stream(name):
                def load(u, g, slot, turn):
                    sp.wait_ge(unit_done, g + 1)
                    sp.dma_start(ring[slot],
                                 io[name][ds(u, 1), :, :].rearrange("u p n -> (u p) n")).then_inc(w_landed[slot], 16)
                for_units(sp, plan, name, load)

            for name in plan:
                stream(name)

        @block.gpsimd
        def _(gp):
            def load(dst, src, s=consts_in):
                gp.dma_start(dst, src).then_inc(s, 16)

            load(cvec[:], io["cvec"], cvec_in)
            load(cst[:], io["cst"])
            load(b_ada[:], io["b_ada"])
            load(ng[:], io["ng"])
            load(h[:, :, 0:NX], io["xT"])
            load(h[:, :, NX:T], io["ctxT"])
            load(small[:], io["small"])
            load(poolw[:], io["poolw"])
            load(vec2[:], io["vec2"])
            for l in range(DEPTH):
                gp.wait_ge(unit_done, after[f"ffn1_{l}"] + RING)
                load(cos_t, io["cos_t"], table_in)
                load(sin_t, io["sin_t"], table_in)
                load(rpb, io[f"rpb{l}"], table_in)
                load(pool_inv, io["pool_inv"], table_in)
            gp.wait_ge(normed, KC * RMS)
            gp.wait_ge(unit_done, after["k_h"] + RING)
            load(alibi, io["alibi"], table_in)
            load(vbias, io["vbias"], table_in)
            gp.wait_ge(heads_out, att_h.job_end + FREE_HEADS)
            load(feats[0:33, :], io["feats"], table_in)
            load(fw[0:HD, :], io["fw"], table_in)
            load(decay, io["decay"], table_in)
            load(w4[0:HD, :], io["w4_0"], table_in)
            gp.wait_ge(f_mm, 1)
            load(dft, io["dft"], table_in)
            gp.wait_ge(zf_mm, 4)
            load(w4[0:HD, :], io["w4_1"], table_in)
            for c in range(KC):
                gp.wait_ge(normed, KC * (RMS + 1) + c + 1)
                gp.dma_start(out[c], fin[:, c, :]).then_inc(stored, 16)
            gp.wait_ge(stored, 16 * KC)

        @block.tensor
        def _(pe):
            def landed(slot, turn):
                pe.wait_ge(w_landed[slot], 16 * turn + 16)

            def accumulate(out_ap, pairs_):
                for k, (w, x) in enumerate(pairs_):
                    mm = pe.matmul(out_ap, w, x, start=(k == 0), stop=(k == len(pairs_) - 1))
                return mm

            def ada_unit(group, half, split_count, slot, bank_no=7):
                pe.wait_ge(w_split, split_count)
                if half == 0 and not isinstance(group, int):
                    pe.wait_ge(mods_done, group)
                elif half == 0 and group >= 2:
                    pe.wait_ge(mods_done, group - 1 if group < GROUPS_FIRST else group)
                at = 512 * bank_no + 256 * half
                for part, w in enumerate((w_hi[slot], w_lo[slot])):
                    for k in range(KC):
                        mm = pe.matmul(psum[:, at:at + 256], c_parts[:, k, :], w[:, 256 * k:256 * (k + 1)],
                                       start=(part == 0 and k == 0), stop=(part == 1 and k == KC - 1))
                mm.then_inc(unit_done, 1)

            def turn_rows(group, second_block, bank_no=7):
                pe.wait_ge(rows_out, group + 1)
                cols = slice(2, 3) if second_block else slice(0, 2)
                n = cols.stop - cols.start
                for c in range(4):
                    at = 512 * bank_no + n * c
                    mm = pe.matmul(psum[:, at:at + n], ada_rows[:, c * P:(c + 1) * P], fold[:, cols],
                                   start=True, stop=True)
                mm.then_inc(rows_turned, 1)

            def sum_chunks(n, src, width, at, s_in, s_out):
                for c in range(KC):
                    pe.wait_ge(s_in, n + c + 1)
                    mm = pe.matmul(psum[:, at:at + NX], ones[:], src[:, c, 0:NX], start=(c == 0), stop=(c == KC - 1))
                    if width > NX:
                        mm = pe.matmul(psum[:, at + NX:at + T], ones[:], src[:, c, NX:T], start=(c == 0), stop=(c == KC - 1))
                mm.then_inc(s_out, 1)

            def stream_sums(n, src, width):
                pe.wait_ge(res_done, FREE + added_before(n) - 2)
                sum_chunks(KC * n, src, width, 0, sq_done, ss_done)

            def split_product(out_x, out_c, hi, lo, src_hi, src_lo, k, n):
                outs = [(out_x, slice(0, NX))] + ([(out_c, slice(NX, T))] if out_c is not None else [])
                for w, src, part in ((hi, src_hi, 0), (hi, src_lo, 1), (lo, src_hi, 2)):
                    for out_ap, cols in outs:
                        mm = pe.matmul(out_ap, w, src[:, k, cols], start=(k == 0 and part == 0),
                                       stop=(k == n - 1 and part == 2))
                return mm

            def ffn(name, n, part, both):
                before = added_before(part)

                group0, later = groups_before(n), groups_before(n) >= 2 * ADA_GROUPS

                def group_of(b, j):
                    return b * FFN_GROUPS[n][0] + (group0 + j)

                def weights(slot, chunks, blocks):
                    return [w[slot][:, 0:chunks * blocks * P].rearrange("p (n k m) -> p n k m", n=chunks, k=blocks)
                            for w in (w_hi, w_lo)]

                def up(b, j, u, g, slot, pending):
                    s = j % 2
                    pe.wait_ge(w_split, u + (SPLIT_BEFORE[n] + 1))
                    if j >= 2:
                        pe.wait_ge(hid_done, b * HB + (FC * n + j - 1))
                    else:
                        pe.wait_ge(res_done, b * KC + (before + FREE - (2 if j == 0 else 0)))
                    hi, lo = weights(slot, 2, KC)
                    for r in range(2):
                        at_c = (3 * s + 2) * 512 + r * NCTX
                        for k in range(KC):
                            if j == 0 and r == 0:
                                pe.wait_ge(a_split, KC * n + k + 1)
                            mm = split_product(bank(3 * s + r), psum[:, at_c:at_c + NCTX] if both else None,
                                               hi[:, r, k, :], lo[:, r, k, :], a_hi, a_lo, k, KC)
                        if r == 0 and pending is not None:
                            turn_rows(group_of(b, pending), later)
                    mm.then_inc(unit_done, 1)

                def down(b, j, u, g, slot, pending, n_hid):
                    s = j % 2
                    pe.wait_ge(w_split, u + (SPLIT_BEFORE[n] + 1))
                    if j >= 2:
                        pe.wait_ge(res_done, b * KC + (before + FREE + 2 * (j - 1)))
                    groups = FFN_GROUPS[n][n_hid != HB]
                    if j == 1 and groups:
                        pe.wait_ge(mods_done, group_of(b, groups))
                    hi, lo = weights(slot, 2, n_hid)
                    steps = [(r, k) for r in range(2) for k in range(n_hid)]
                    if j == 0:
                        steps.sort(key=lambda rk: rk[1] == n_hid - 1)
                        pe.wait_ge(hid_done, b * HB + (FC * n + n_hid - 1))
                    for at, (r, k) in enumerate(steps):
                        if at == n_hid and pending is not None:
                            turn_rows(group_of(b, pending), later)
                        if j == 0 and at == len(steps) - 2:
                            pe.wait_ge(hid_done, b * HB + (FC * n + n_hid))
                        out_x, out_c = (bank(3 * s), bank(3 * s + 1, NCTX)) if r == 0 else (bank(3 * s + 2), bank(6 + s, NCTX))
                        mm = split_product(out_x, out_c if both else None, hi[:, r, k, :], lo[:, r, k, :],
                                           hid_hi, hid_lo, k, n_hid)
                    mm.then_inc(unit_done, 1)

                def ada(b, j, half, u, g, slot):
                    ada_unit(group_of(b, j), half, u + (SPLIT_BEFORE[n] + 1), slot)
                for_ffn_units(pe, plan, name, n, up, down, ada)

            def residual(name, n, src, blocks, per_unit, both):
                g0 = first[name]

                def unit(u, g, slot, turn):
                    landed(slot, turn)
                    w = blocks_of(slot, per_unit, blocks)
                    pe.wait_ge(res_done, u * per_unit + (added_before(n) + FREE - per_unit))
                    for j in range(per_unit):
                        s = (slot - g0) % 2 * per_unit + j
                        for k in range(blocks):
                            mm = pe.matmul(bank(2 * s), w[:, j, k, :], src[:, k, 0:NX], start=(k == 0), stop=(k == blocks - 1))
                            if both:
                                mm = pe.matmul(bank(2 * s + 1, NCTX), w[:, j, k, :], src[:, k, NX:T],
                                               start=(k == 0), stop=(k == blocks - 1))
                    mm.then_inc(unit_done, 1)
                for_units(pe, plan, name, unit)

            def attention(att, jobs, qst, probs, keysT, v_tiles=None):
                NJ, NP = att.jobs, att.pieces

                def scores(i, j):
                    if j >= 2:
                        pe.wait_ge(exp_done, i * NJ + (att.job0 + j - 1))
                    base = att.scores_at(j)
                    for q, half, keys, lo, hi in jobs[j % NJ][0]:
                        mm = pe.matmul(psum[:, base + lo:base + hi], qst[64 * half:64 * half + 64, q, :], keys,
                                       start=True, stop=True)
                    mm.then_inc(scores_done, 1)

                def turn(i, j):
                    pe.wait_ge(probs_ready, i * NJ + (att.job0 + j + 1))
                    for p in range(NP):
                        if j >= 1:
                            pe.wait_ge(turned_act if p % 2 == 0 else turned_dve, att.evacuated(i, j - 1, p))
                        lo, hi = att.keys_of(p)
                        for k in range(lo, hi, P):
                            mm = pe.transpose(psum[:, 2048 + k:2048 + k + P], probs[:, j % PROBS, k:k + P], ident)
                        mm.then_inc(turned, 1)

                def values(i, j, last):
                    if last and j == NJ - 1:
                        for p in range(NP):
                            pe.wait_ge(turned_act if p % 2 == 0 else turned_dve, att.evacuated(i, j, p))
                    pe.wait_ge(heads_out, i * NJ + (att.job0 + j - 1 + FREE_HEADS))
                    if v_tiles is not None and j == 0:
                        pe.wait_ge(v_staged, i + (v_tiles + 1))
                    half = j % 2
                    out_ = psum[64 * half:64 * half + 64, 3072 + 512 * (j % 2):3072 + 512 * (j % 2) + P]
                    for k in range(0, att.width, P):
                        mm = pe.matmul(out_, jobs[j][1][k // P], keysT[:, j % 2, k:k + P],
                                       start=(k == 0), stop=(k + P == att.width))
                    mm.then_inc(heads_done, 1)

                def tile(i, last):
                    for j in range(NJ):
                        if j + AHEAD < NJ or not last:
                            if j + AHEAD == NJ:
                                pe.wait_ge(q_staged, i + (att.tile0 + 2))
                            scores(i, j + AHEAD)
                        if j + 1 < NJ or not last:
                            turn(i, j + 1)
                        values(i, j, last)

                pe.wait_ge(q_staged, att.tile0 + 1)
                for j in range(AHEAD):
                    scores(0, j)
                turn(0, 0)
                for_tiles(pe, att, tile)
                pe.wait_ge(heads_out, att.job_end + FREE_HEADS)

            def block1_jobs(k0):
                jobs = []
                for n in range(12):
                    if n < 4:
                        q, half, kc, vcol = n // 2, n % 2, KA + n // 2, n * HD
                    else:
                        q, half, kc, vcol = 2 + (n - 4) // 2, n % 2, KG, 256 + n % 2 * HD
                    pieces = [(q, half, proj[64 * half:64 * half + 64, kc, lo:hi], lo - k0, hi - k0)
                              for lo, hi in ((k0, NX), (NX, T)) if hi > lo]
                    jobs.append((pieces, [v_tok[:, t, vcol:vcol + HD] for t in range(k0 // P, T // P)]))
                return jobs

            def mix(l):
                g0 = first[f"in{l}"]
                both = both_in[l]

                def head_sums(n):
                    pe.wait_ge(qk_sq_done, 5 * l + n + 1)
                    if n > 0:
                        pe.wait_ge(qk_root_done, 5 * l + n)
                    mm = pe.matmul(bank(4), pairs, qk_sq[:, n % 2, 0:NX], start=True, stop=True)
                    if keeps_ctx(l, QG + n):
                        mm = pe.matmul(bank(5, NCTX), pairs, qk_sq[:, n % 2, NX:T], start=True, stop=True)
                    mm.then_inc(qk_ss_done, 1)

                def rotation(n):
                    pe.wait_ge(qk_normed, 5 * l + n + 1)
                    if n >= 2:
                        pe.wait_ge(qk_roped, 5 * l + n - 1)
                    pe.matmul(bank(6 + n % 2), rot, proj[:, QG + n, 0:NX], start=True, stop=True).then_inc(qk_rotated, 1)

                for c in range(NPROJ):
                    slot = (g0 + c // 2) % RING
                    if c % 2 == 0:
                        landed(slot, (g0 + c // 2) // RING)
                    if c >= 2:
                        pe.wait_ge(proj_done, PER_PROJ * l + c - 1)
                    w = blocks_of(slot, 2, KC)
                    for k in range(KC):
                        if c == 0:
                            pe.wait_ge(normed, KC * (3 * l + 1) + k + 1)
                        mm = pe.matmul(bank(2 * (c % 2)), w[:, c % 2, k, :], a[:, k, 0:NX], start=(k == 0), stop=(k == KC - 1))
                        if keeps_ctx(l, c):
                            mm = pe.matmul(bank(2 * (c % 2) + 1, NCTX), w[:, c % 2, k, :], a[:, k, NX:T],
                                           start=(k == 0), stop=(k == KC - 1))
                    mm.then_inc(unit_done if c % 2 == 1 or c == NPROJ - 1 else even_proj, 1)
                    if 1 <= c <= 5:
                        head_sums(c - 1)
                    if 2 <= c <= 6:
                        rotation(c - 2)
                pe.wait_ge(qk_root_done, 5 * (l + 1))
                for n, cols in ((0, 256), (1, 128)):
                    slot = (g0 + 6 + n) % RING
                    landed(slot, (g0 + 6 + n) // RING)
                    w = ring[slot][:, 0:KC * cols].rearrange("p (k n) -> p k n", k=KC)
                    for t in range(T // P):
                        pe.wait_ge(proj_done, PER_PROJ * l + NPROJ + (t + 1 if n else 0))
                        mm = accumulate(bank(t, cols), [(a[:, k, t * P:(t + 1) * P], w[:, k, :]) for k in range(KC)])
                    mm.then_inc(unit_done, 1)
                for k in range(2):
                    pe.wait_ge(pool_ready, 2 * l + k + 1)
                    if k == 0:
                        pe.wait_ge(proj_done, PER_PROJ * (l + 1))
                    mm = pe.matmul(bank(2 * k), pw[:, l, k, :], pool_y[:, k, POOL_X:POOL_X + NX], start=True, stop=True)
                    if both:
                        mm = pe.matmul(bank(2 * k + 1, NCTX), pw[:, l, k, :], pool_y[:, k, POOL_C:POOL_C + NCTX],
                                       start=True, stop=True)
                    mm.then_inc(pool_done, 1)
                pe.wait_ge(pool_out, 2 * l + 2)
                attention(att_x[l], block1_jobs(0), qst_1, probs_1, keysT_1)
                if both:
                    attention(att_c0, block1_jobs(NX), qst_1, probs_1, keysT_1)
                residual(f"out{l}", 3 * l + 1, a, KC, 2, both)

            def wide(name, c0, s_read, lo, hi):
                g0 = first[name]
                for c in range(lo, hi):
                    slot = (g0 + c // 2) % RING
                    if c % 2 == 0:
                        landed(slot, (g0 + c // 2) // RING)
                    if c0 + c >= 4:
                        pe.wait_ge(s_read, c0 + c - 3)
                    elif name == "conv_h":
                        pe.wait_ge(gate_act, c + 1)
                    w = blocks_of(slot, 2, KC)
                    mm = accumulate(bank(c % 4), [(w[:, c % 2, k, :], h2[:, k, :]) for k in range(KC)])
                    if c % 2 == 1:
                        mm.then_inc(unit_done, 1)

            def queries_keys():
                g0 = first["q_h"]
                for c in range(24):
                    slot = (g0 + c // 2) % RING
                    if c % 2 == 0:
                        pe.wait_ge(w_split, SPLIT_BEFORE[2 * DEPTH] + c // 2 + 1)
                    if c >= 4:
                        pe.wait_ge(qk2_out, c - 3)
                    hi, lo = (w[slot].rearrange("p (n k m) -> p n k m", n=2, k=KC) for w in (w_hi, w_lo))
                    for k in range(KC):
                        if c == 0:
                            pe.wait_ge(h2_split, k + 1)
                        mm = split_product(bank(c % 4), None, hi[:, c % 2, k, :], lo[:, c % 2, k, :], h2_hi, h2_lo, k, KC)
                    if c % 2 == 1:
                        mm.then_inc(unit_done, 1)

            def hyena():
                for n in range(3):
                    wide("conv_h", 0, conv_in, 3 * n, 3 * n + 3)
                    if n == 0:
                        pe.wait_ge(table_in, TAB_FEATS)
                        pe.matmul(psum[0:HD, 3072:3072 + NX], fw[0:33, 0:HD], feats[0:33, :], start=True, stop=True).then_inc(f_mm, 1)
                    else:
                        pe.wait_ge(f_sin, n)
                        pe.matmul(psum[0:HD, 3072:3072 + NX], fw[0:HD, n * HD:(n + 1) * HD], f_hid[0:HD, :],
                                  start=True, stop=True).then_inc(f_mm, 1)
                wide("conv_h", 0, conv_in, 9, 12)
                pe.wait_ge(f_sin, 3)
                for o in range(2):
                    pe.wait_ge(table_in, TAB_W4[o])
                    if o == 0:
                        pe.wait_ge(conv_in, 12)
                    for t in range(QC):
                        for r in range(2):
                            n = 8 * o + 2 * t + r
                            if n % 8 >= 4:
                                pe.wait_ge(fh_out, n - 3)
                            pe.matmul(bank(n % 4), f_hid[0:HD, t * P:(t + 1) * P], w4[0:HD, r * NX:(r + 1) * NX],
                                      start=True, stop=True).then_inc(fh_mm, 1)
                    if o == 0:
                        pe.wait_ge(conv_out, 12)
                    else:
                        pe.wait_ge(zi_out, 4)
                    for c in range(4):
                        n = 4 * o + c
                        if c >= 2:
                            pe.wait_ge(zt_out, n - 1)
                        for t in range(QC):
                            mm = pe.transpose(psum[:, 2048 + 512 * (c % 2) + t * P:2048 + 512 * (c % 2) + (t + 1) * P],
                                              vxx[:, c, t * P:(t + 1) * P], ident)
                        mm.then_inc(zt_mm, 1)
                    pe.wait_ge(table_in, TAB_DFT)
                    for q in range(4):
                        n = 4 * o + q
                        if q >= 2:
                            pe.wait_ge(ft_out, n - 1)
                        for t in range(QC):
                            if q == 0:
                                pe.wait_ge(fh_ready, 4 * o + max(t + 1, 3))
                            pe.matmul(bank(2 * (q % 2)), dft[:, t, q * P:(q + 1) * P], hf[:, t, :],
                                      start=(t == 0), stop=(t == QC - 1))
                        accumulate(bank(2 * (q % 2) + 1), [(dft[:, 4 + t, q * P:(q + 1) * P], hb[:, t, :])
                                                           for t in range(QC)]).then_inc(ft_mm, 1)
                    pe.wait_ge(zt_out, 4 * (o + 1))
                    pe.wait_ge(ft_out, 4 * (o + 1))
                    for q in range(4):
                        n = 4 * o + q
                        if q >= 2:
                            pe.wait_ge(zf_out, n - 1)
                        accumulate(bank(2 * (q % 2)), [(dft[:, t, q * P:(q + 1) * P], z_tok[:, t, :]) for t in range(QC)])
                        accumulate(bank(2 * (q % 2) + 1), [(dft[:, 4 + t, q * P:(q + 1) * P], z_tok[:, t, :])
                                                           for t in range(QC)]).then_inc(zf_mm, 1)
                    pe.wait_ge(zf_out, 4 * (o + 1))
                    for c in range(4):
                        n = 4 * o + c
                        if c >= 2:
                            pe.wait_ge(zi_out, n - 1)
                        accumulate(bank(4 + c % 2),
                                   [(y_re[:, q, c * P:(c + 1) * P], dft[:, 8 + q, :]) for q in range(4)]
                                   + [(y_im[:, q, c * P:(c + 1) * P], dft[:, 12 + q, :]) for q in range(4)]).then_inc(zi_mm, 1)
                wide("ghy_h", 4, gate_mul, 0, 4)

            def merge():
                g0 = first["merge_h"]
                pe.wait_ge(gate_mul, 8)
                for q in range(KC // 2):
                    for j in range(2):
                        c, g = 2 * q + j, g0 + 3 * q + j
                        landed(g % RING, g // RING)
                        if c >= 2:
                            pe.wait_ge(merge_sig, c - 1)
                        w = blocks_of(g % RING, 2, KC)
                        for r in range(2):
                            mm = accumulate(bank(2 * j + r), [(w[:, r, k, :], h2[:, k, :]) for k in range(KC)])
                        mm.then_inc(unit_done, 1)
                    g = g0 + 3 * q + 2
                    landed(g % RING, g // RING)
                    if q >= 1:
                        pe.wait_ge(merge_out, 2 * q)
                    w = blocks_of(g % RING, 4, 4)
                    for j in range(2):
                        for r, y in enumerate((y_attn, vxx)):
                            mm = accumulate(bank(4 + 2 * j + r), [(w[:, 2 * j + r, k, :], y[:, k, :]) for k in range(4)])
                    mm.then_inc(unit_done, 1)
                pe.wait_ge(merge_out, KC)
                g0 = first["out_h"]
                for c in range(KC):
                    g = g0 + c // 2
                    if c % 2 == 0:
                        landed(g % RING, g // RING)
                    if c >= 4:
                        pe.wait_ge(out2_done, c - 3)
                    w = blocks_of(g % RING, 2, KC)
                    mm = accumulate(bank(c % 4), [(w[:, c % 2, k, :], merged[:, k, :]) for k in range(KC)])
                    if c % 2 == 1:
                        mm.then_inc(unit_done, 1)
                sum_chunks(0, res, NX, 2048, out2_done, mean_done)
                sum_chunks(KC * (RMS + 1), res_sq, NX, 3072, sq_done, ss_done)

            pe.nop().then_inc(unit_done, RING)
            pe.nop().then_inc(heads_out, FREE_HEADS)
            pe.wait_ge(c_ready, 1)
            for t in range(GROUPS_FIRST):
                for half in range(2):
                    u = 2 * t + half
                    ada_unit(t, half, u + 1, u % RING, 7 - t % 2)
                if t == 1:
                    pe.wait_ge(consts_in, N_CONSTS)
                if t == GROUPS_FIRST - 2:
                    pe.wait_ge(setup_done, 1)
                    stream_sums(0, a, T)
                if t > 0:
                    turn_rows(t - 1, False, 7 - (t - 1) % 2)
            turn_rows(GROUPS_FIRST - 1, False, 7 - (GROUPS_FIRST - 1) % 2)
            for l in range(DEPTH):
                if l > 0:
                    stream_sums(3 * l, a, T)
                ffn(f"ffn1_{l}", 2 * l, 3 * l, True)
                stream_sums(3 * l + 1, a, T)
                mix(l)
                stream_sums(3 * l + 2, sq_g, T if both_in[l] else NX)
                ffn(f"ffn2_{l}", 2 * l + 1, 3 * l + 2, both_in[l])
            stream_sums(RMS - 1, a, NX)
            pe.wait_ge(root_done, RMS)
            sum_chunks(KC * (RMS - 1), x2, NX, 2048, normed, mean_done_0)
            sum_chunks(KC * RMS, sq2, NX, 3072, sq_done, ss_done)
            queries_keys()
            for u in range(6):
                g = first["v_h"] + u
                landed(g % RING, g // RING)
                w = ring[g % RING][:, 0:KC * 256].rearrange("p (k n) -> p k n", k=KC)
                for t in range(QC):
                    if u >= 1:
                        pe.wait_ge(v2_out, 4 * (u - 1) + t + 1)
                    mm = accumulate(bank(4 + t, 256), [(h2r[:, k, t, :], w[:, k, :]) for k in range(KC)])
                mm.then_inc(unit_done, 1)
            pe.wait_ge(qk2_out, 24)
            pe.wait_ge(v2_out, 24)
            jobs = []
            for n in range(NH2):
                c, rows, cols = n // 2, slice(64 * (n % 2), 64 * (n % 2) + 64), slice(n * HD, (n + 1) * HD)
                jobs.append((
                    [(c, n % 2, kh[rows, c, :], 0, NX)]
                    + [(4 * g + c, n % 2, kst[rows, 4 * (g - 1) + c, :], NX + (g - 1) * P, NX + g * P) for g in (1, 2)],
                    [vh[:, r, cols] for r in range(RES)] + [vst[:, g, cols] for g in range(2)]))
            attention(att_h, jobs, qst_2, probs_2, keysT_2, 0)
            wide("gattn_h", 0, gate_mul, 0, 4)
            hyena()
            merge()

        @block.scalar
        def _(act):
            def squares(n, src, dst, width, ready, next_phase=None):
                for c in range(KC):
                    ready(c)
                    act.activation(dst[:, c, 0:width], src[:, c, 0:width], ACT.Square).then_inc(sq_done, 1)
                    if next_phase and c in (3, 5):
                        k = first[next_phase] + (c - 3) // 2
                        first_parts(k % RING, k // RING)

            def root(n, dst, width, eps_col, at=3072):
                act.wait_ge(ss_done, n + 1)
                act.activation(dst[:, 0:width], psum[:, at:at + width], ACT.Sqrt, scale=1.0 / D,
                               bias=eps_col).then_inc(root_done, 1)

            def modulate(n, src, dst, both, gain_of, shift_of, split=False):
                for c in range(KC):
                    act.wait_ge(scaled_done, KC * n + c + 1)
                    ins = act.activation(dst[:, c, 0:NX], src[:, c, 0:NX], ACT.Identity, scale=gain_of(c, 0), bias=shift_of(c, 0))
                    if both:
                        ins = act.activation(dst[:, c, NX:T], src[:, c, NX:T], ACT.Identity, scale=gain_of(c, 1), bias=shift_of(c, 1))
                    ins.then_inc(normed, 1)
                    if split:
                        act.wait_ge(normed, KC * n + c + 1)
                        if dst is h2:
                            act.activation(h2_hi[:, c, :], h2[:, c, :], ACT.Copy).then_inc(h2_hi_done, 1)
                        else:
                            w = T if both else NX
                            act.activation(a_hi[:, c, 0:w], a_f[:, c, 0:w], ACT.Copy).then_inc(a_hi_done, 1)

            def rms(n, width, gain_of, shift_of, ffn_name=None):
                def ready(c):
                    act.wait_ge(res_done, FREE + added_before(n) - KC + c + 1)
                if n > 0:
                    squares(n, h, sq_g if n % 3 == 2 else a, width, ready, ffn_name)
                    root(n, rstd, width, eps[:, 0:1], 0)
                elif ffn_name:
                    for k in range(first[ffn_name], first[ffn_name] + 2):
                        first_parts(k % RING, k // RING)
                if ffn_name:
                    k = first[ffn_name] + 2
                    first_parts(k % RING, k // RING)
                act.wait_ge(mod_ready, n + 1)
                x = a_f if ffn_name else a
                modulate(n, x, x, width > NX, gain_of, shift_of, bool(ffn_name))

            def first_parts(slot, turn):
                act.wait_ge(w_landed[slot], turn * 16 + 16)
                act.activation(w_hi[slot], ring[slot], ACT.Copy).then_inc(hi_done, 1)

            def take_rows(group, g, bank_no=7):
                act.wait_ge(unit_done, g + (1 + RING))
                if not isinstance(group, int) or group > 0:
                    act.wait_ge(rows_turned, group)
                act.activation(ada_rows[:], psum[0:6, 512 * bank_no:512 * bank_no + 512], ACT.Copy).then_inc(rows_out, 1)

            def ffn_gate(name, n, both):

                def up(b, j, u, g, slot, pending):
                    s = j % 2
                    act.wait_ge(unit_done, g + (1 + RING))
                    ins = act.activation(sil[:, s, 0:NX], bank(3 * s), ACT.Silu)
                    if both:
                        ins = act.activation(sil[:, s, NX:T], bank(3 * s + 2, NCTX), ACT.Silu)
                    ins.then_inc(silu_done, 1)

                def down(b, j, u, g, slot, pending, n_hid):
                    pass

                def ada(b, j, half, u, g, slot):
                    if half == 1:
                        take_rows(b * FFN_GROUPS[n][0] + (groups_before(n) + j), g)
                for_ffn_units(act, plan, name, n, up, down, ada,
                              ahead=lambda u, slot, turn: first_parts(slot, turn))

            def attention(att, probs, keysT, biased, head_dst):
                NJ, NP = att.jobs, att.pieces

                def exp(i, j):
                    act.wait_ge(max_done, i * NJ + (att.job0 + j + 1))
                    if j >= PROBS:
                        act.wait_ge(turned, i * (NJ * NP) + (att.piece0 + (j - PROBS + 1) * NP))
                    at, p = att.scores_at(j), probs[:, j % PROBS, 0:att.width]
                    src = p if biased(j % NJ) else psum[:, at:at + att.width]
                    act.activation(p, src, ACT.Exp, bias=nmax[:, j % 4:j % 4 + 1],
                                   accum_out=rsum[:, j % 4:j % 4 + 1]).then_inc(exp_done, 1)

                def take(i, j):
                    for p in att.on_act:
                        act.wait_ge(turned, i * (NJ * NP) + (att.piece0 + j * NP + p + 1))
                        lo, hi = att.keys_of(p)
                        act.activation(keysT[:, j % 2, lo:hi], psum[:, 2048 + lo:2048 + hi], ACT.Copy).then_inc(turned_act, 1)

                def tile(i, last):
                    for j in range(NJ):
                        if j + 1 < NJ or not last:
                            take(i, j + 1)
                        if j + AHEAD < NJ or not last:
                            exp(i, j + AHEAD)
                        act.wait_ge(heads_done, i * NJ + (att.job0 + j + 1))
                        rows, at = slice(64 * (j % 2), 64 * (j % 2) + 64), 3072 + 512 * (j % 2)
                        act.activation(head_dst(i, j, rows), psum[rows, at:at + P], ACT.Copy).then_inc(heads_out, 1)

                for j in range(AHEAD):
                    exp(0, j)
                take(0, 0)
                for_tiles(act, att, tile)

            def block1_attention(att, t0, latent):
                def head_dst(i, j, rows):
                    c = j // 2 if j < 4 else 2 + j // 2
                    return a[rows, c, ds(i * P + t0, P)]
                attention(att, probs_1, keysT_1, lambda j: latent and j < 4, head_dst)

            def mix(l):
                g0 = first[f"in{l}"]

                def square(n):
                    c = QG + n
                    w = T if keeps_ctx(l, c) else NX
                    act.wait_ge(proj_done, PER_PROJ * l + c + 1)
                    if n >= 2:
                        act.wait_ge(qk_ss_done, 5 * l + n - 1)
                    act.activation(qk_sq[:, n % 2, 0:w], proj[:, c, 0:w], ACT.Square).then_inc(qk_sq_done, 1)

                def head_root(n):
                    w = T if keeps_ctx(l, QG + n) else NX
                    act.wait_ge(qk_ss_done, 5 * l + n + 1)
                    if n >= 2:
                        act.wait_ge(qk_normed, 5 * l + n - 1)
                    act.activation(qk_rs[:, n % 2, 0:w], psum[:, 2048:2048 + w], ACT.Sqrt, scale=1.0 / HD,
                                   bias=eps[:, 0:1]).then_inc(qk_root_done, 1)

                for c in range(NPROJ):
                    if c % 2 == 1 or c == NPROJ - 1:
                        act.wait_ge(unit_done, g0 + c // 2 + 1 + RING)
                    else:
                        act.wait_ge(even_proj, NPROJ // 2 * l + c // 2 + 1)
                    b0 = 1024 * (c % 2)
                    if c in (UU, UU + 1):
                        act.wait_ge(upad_ready, l + 1)
                        ins = act.activation(upad[:, c - UU, POOL_X:POOL_X + NX], psum[:, b0:b0 + NX], ACT.Copy)
                        if both_in[l]:
                            ins = act.activation(upad[:, c - UU, POOL_C:POOL_C + NCTX], psum[:, b0 + NX:b0 + T], ACT.Copy)
                    else:
                        w = T if keeps_ctx(l, c) else NX
                        ins = act.activation(proj[:, c, 0:w], psum[:, b0:b0 + w], ACT.Copy,
                                             scale=SCORE_SCALE if c in (QA, QA + 1) else 1.0)
                    ins.then_inc(proj_done, 1)
                    if c < 5:
                        square(c)
                    if 1 <= c <= 5:
                        head_root(c - 1)
                for n, lo, cols in ((0, 0, 256), (1, 256, 128)):
                    act.wait_ge(unit_done, g0 + 6 + n + 1 + RING)
                    for t in range(T // P):
                        act.activation(v_tok[:, t, lo:lo + cols], bank(t, cols), ACT.Copy).then_inc(proj_done, 1)
                for k in range(2):
                    act.wait_ge(pool_done, 2 * l + k + 1)
                    scale = small[:, 4 * l + k:4 * l + k + 1]
                    ins = act.activation(a[:, 2 + k, 0:NX], bank(2 * k), ACT.Copy, scale=scale)
                    if both_in[l]:
                        ins = act.activation(a[:, 2 + k, NX:T], bank(2 * k + 1, NCTX), ACT.Copy, scale=scale)
                    ins.then_inc(pool_out, 1)
                block1_attention(att_x[l], 0, True)
                if both_in[l]:
                    block1_attention(att_c0, NX, False)

            def gates(name, n0, bias0):
                g0 = first[name]
                for c in range(4):
                    act.wait_ge(unit_done, g0 + c // 2 + 1 + RING)
                    if n0 + c >= 2:
                        act.wait_ge(gate_mul, n0 + c - 1)
                    act.activation(gate_t[:, c % 2, :], bank(c % 4), ACT.Silu,
                                   bias=vec2[:, bias0 + c:bias0 + c + 1]).then_inc(gate_act, 1)

            def hyena():
                def net_sine(n):
                    act.wait_ge(f_arg, n + 1)
                    act.activation(f_hid[0:HD, :], f_tmp[0:HD, 0, :], ACT.Sin).then_inc(f_sin, 1)

                act.wait_ge(cpad_zero, 1)
                g0 = first["conv_h"]
                for c in range(12):
                    act.wait_ge(unit_done, g0 + c // 2 + 1 + RING)
                    if c >= 2:
                        act.wait_ge(conv_out, c - 1)
                    act.activation(cpad[:, c % 2, 1:NX + 1], bank(c % 4), ACT.Identity,
                                   bias=vec2[:, OB_IN + 40 + c:OB_IN + 41 + c]).then_inc(conv_in, 1)
                    if c in NET_AFTER:
                        net_sine(NET_AFTER.index(c))
                for o in range(2):
                    for c in range(4):
                        act.wait_ge(zt_mm, 4 * o + c + 1)
                        act.activation(z_tok[:, :, c * P:(c + 1) * P],
                                       bank(4 + c % 2).rearrange("p (t m) -> p t m", t=4), ACT.Copy).then_inc(zt_out, 1)
                    for q in range(4):
                        act.wait_ge(ft_mm, 4 * o + q + 1)
                        if o == 1 and q == 0:
                            act.wait_ge(zf_out, 4)
                        act.activation(H_re[:, q, :], bank(2 * (q % 2)), ACT.Copy)
                        act.activation(H_im[:, q, :], bank(2 * (q % 2) + 1), ACT.Copy).then_inc(ft_out, 1)
                gates("ghy_h", 4, OB_IN + 52)

            def merge():
                g0 = first["merge_h"]
                for c in range(KC):
                    act.wait_ge(unit_done, g0 + 3 * (c // 2) + c % 2 + 1 + RING)
                    if c >= 2:
                        act.wait_ge(merge_out, c - 1)
                    for r in range(2):
                        b = OB_IN + 56 + 8 * r + c
                        ins = act.activation(sg_t[:, c % 2, r * NX:(r + 1) * NX], bank(2 * (c % 2) + r), ACT.Sigmoid,
                                             bias=vec2[:, b:b + 1])
                    ins.then_inc(merge_sig, 1)
                squares(RMS + 1, res, res_sq, NX, lambda c: act.wait_ge(centred, KC + c + 1))
                root(RMS + 1, sg_t[:, 0, 0:NX], NX, eps[:, 1:2])
                modulate(RMS + 1, res, fin, False, lambda c, s: vec2[:, OLG + c:OLG + c + 1],
                         lambda c, s: vec2[:, OLB + c:OLB + c + 1])

            act.wait_ge(cvec_in, 16)
            act.activation(cv[:, :, 0:2], cv[:, :, 0:2], ACT.Silu).then_inc(silu_c, 1)
            for t in range(GROUPS_FIRST + 1):
                if t < GROUPS_FIRST:
                    for u in (2 * t, 2 * t + 1):
                        first_parts(u % RING, u // RING)
                if t == GROUPS_FIRST:
                    root(0, rstd, T, eps[:, 0:1], 0)
                if t > 0:
                    take_rows(t - 1, 2 * t - 1, 7 - (t - 1) % 2)
                if t == GROUPS_FIRST // 2:
                    act.wait_ge(consts_in, N_CONSTS)
                    act.wait_ge(setup_done, 1)
                    squares(0, h, a, T, lambda c: None)
            for l in range(DEPTH):
                def gain_of(k):
                    return lambda c, s: gainv[:, k, c, s:s + 1]

                def shift_of(k):
                    return lambda c, s: mod[l][:, 3 * k, c, s:s + 1]
                rms(3 * l, T, gain_of(0), shift_of(0), f"ffn1_{l}")
                ffn_gate(f"ffn1_{l}", 2 * l, True)
                rms(3 * l + 1, T, gain_of(1), shift_of(1))
                mix(l)
                rms(3 * l + 2, T if both_in[l] else NX, gain_of(2), shift_of(2), f"ffn2_{l}")
                ffn_gate(f"ffn2_{l}", 2 * l + 1, both_in[l])
            n = RMS - 1
            squares(n, h, a, NX, lambda c: act.wait_ge(res_done, FREE + added_before(n) - KC + c + 1),
                    "q_h")
            root(n, rstd, NX, eps[:, 0:1], 0)
            modulate(n, x2, x2, False, lambda c, s: final_g[:, c:c + 1], lambda c, s: 0.0)
            squares(RMS, h2, sq2, NX, lambda c: act.wait_ge(centred, c + 1))
            qk_unit = first["q_h"]
            root(RMS, rstd2, NX, eps[:, 1:2])
            first_parts((qk_unit + 2) % RING, (qk_unit + 2) // RING)
            modulate(RMS, h2, h2, False, lambda c, s: gain2[:, c:c + 1], lambda c, s: mod2[:, c:c + 1], True)
            for c in range(24):
                ahead = qk_unit + c // 2 + LEAD
                if c % 2 == 0 and ahead < after["k_h"]:
                    first_parts(ahead % RING, ahead // RING)
                act.wait_ge(unit_done, first["q_h"] + c // 2 + 1 + RING)
                dst = (qh if c < 12 else kh)[:, c % 12, :].rearrange("p (r u) -> p u r", r=RES)
                src = bank(c % 4).rearrange("p (u r) -> p u r", r=RES)
                if c < 12:
                    act.activation(dst, src, ACT.Identity, scale=SCORE_SCALE,
                                   bias=bq[:, c:c + 1]).then_inc(qk2_out, 1)
                else:
                    act.activation(dst, src, ACT.Identity,
                                   bias=vec2[:, OB_IN + c:OB_IN + c + 1]).then_inc(qk2_out, 1)

            def head_dst(i, j, rows):
                by_residue = y_attn[rows, j // 2, :].rearrange("p (u r) -> p r u", r=RES)
                return by_residue[:, ds(i, 1), :].rearrange("p a u -> p (a u)")
            attention(att_h, probs_2, keysT_2, lambda j: True, head_dst)
            gates("gattn_h", 0, OB_IN + 36)
            hyena()
            merge()

        @block.vector
        def _(dve):
            own = Chain(dve, dve_own)

            def modulation(l, k):
                dve.wait_ge(mods_done, (GROUPS_FIRST, ADA_GROUPS)[k > 0] if l == 0 else 2 * ADA_GROUPS)
                ins = dve.scalar_tensor_tensor(gainv[:, k, :, :], mod[l][:, 3 * k + 1, :, :], 1.0, ngv[:, l, k, :, :],
                                               ALU.add, ALU.mult)
                if k != 1:
                    own.mark(ins)
                    ins = dve.tensor_scalar(hgate[:, k // 2, :, :], mod[l][:, 3 * k + 2, :, :], 0.5, None, ALU.mult)
                ins.then_inc(mod_ready, 1)
                dve.wait_ge(mod_ready, 3 * l + k + 1)

            def take_vectors(group, b, step, bank_no=7):
                dve.wait_ge(rows_turned, b * step + (group + 1))
                l, at = group // ADA_GROUPS, group % ADA_GROUPS
                if l < DEPTH:
                    cols, bias_cols = ds(b * (8 * step) + 8 * at, 8), ds(b * (8 * step) + (l * NMOD * KC * 2 + 8 * at), 8)
                    dve.tensor_tensor(mods[l][:, cols], psum[:, 512 * bank_no:512 * bank_no + 8], b_ada[:, bias_cols],
                                      ALU.add).then_inc(mods_done, 1)
                else:
                    cols, bias_cols = ds(b * (4 * step) + 4 * at, 4), ds(b * (4 * step) + (OB_ADA + 4 * at), 4)
                    dve.tensor_tensor(mod2[:, cols], psum[:, 512 * bank_no:512 * bank_no + 4], vec2[:, bias_cols],
                                      ALU.add).then_inc(mods_done, 1)

            def scale_rows(n, src, dst, root_ap, width):
                dve.wait_ge(root_done, n + 1)
                own.link(dve.reciprocal(root_ap[:, 0:width], root_ap[:, 0:width]))
                for c in range(KC):
                    dve.tensor_tensor(dst[:, c, 0:width], src[:, c, 0:width], root_ap[:, 0:width], ALU.mult)\
                       .then_inc(scaled_done, 1)

            def rest_parts(count, slot):
                dve.wait_ge(hi_done, count)
                dve.tensor_tensor(w_lo[slot], ring[slot], w_hi[slot].bitcast(F32), ALU.subtract).then_inc(w_split, 1)

            def first_rests(name, n, lo=0, hi=2):
                for k in range(lo, hi):
                    rest_parts(SPLIT_BEFORE[n] + k + 1, (first[name] + k) % RING)

            def stream_reciprocal(n, width):
                dve.wait_ge(root_done, n + 1)
                own.link(dve.reciprocal(rstd[:, 0:width], rstd[:, 0:width]))

            def scale_and_split(n, n_ffn, width):
                if n > 0:
                    stream_reciprocal(n, width)
                for c in range(KC + 2):
                    if c < KC:
                        dve.tensor_tensor(a_f[:, c, 0:width], h[:, c, 0:width], rstd[:, 0:width], ALU.mult)\
                           .then_inc(scaled_done, 1)
                    if c >= 2:
                        dve.wait_ge(a_hi_done, KC * n_ffn + c - 1)
                        dve.tensor_tensor(a_lo[:, c - 2, 0:width], a_f[:, c - 2, 0:width],
                                          a_hi[:, c - 2, 0:width].bitcast(F32), ALU.subtract).then_inc(a_split, 1)

            def ffn(name, n, part, gate_at, both):
                width = T if both else NX

                def pending_vectors(b, pending):
                    if pending is not None:
                        step = FFN_GROUPS[n][0]
                        if isinstance(b, int):
                            take_vectors(groups_before(n) + b * step + pending, 0, 0)
                        else:
                            take_vectors(groups_before(n) + pending, b, step)

                def up(b, j, u, g, slot, pending):
                    s = j % 2
                    pending_vectors(b, pending)
                    dve.wait_ge(silu_done, b * HB + (FC * n + j + 1))
                    p = sil[:, s, 0:width]
                    ins = dve.tensor_tensor(sil[:, s, 0:NX], sil[:, s, 0:NX], bank(3 * s + 1), ALU.mult)
                    if both:
                        at = (3 * s + 2) * 512 + NCTX
                        ins = dve.tensor_tensor(sil[:, s, NX:T], sil[:, s, NX:T], psum[:, at:at + NCTX], ALU.mult)
                    own.link(ins)
                    own.link(dve.tensor_copy(hid_hi[:, j, 0:width], p))
                    dve.tensor_tensor(hid_lo[:, j, 0:width], p, hid_hi[:, j, 0:width].bitcast(F32), ALU.subtract)\
                       .then_inc(hid_done, 1)

                def down(b, j, u, g, slot, pending, n_hid):
                    s = j % 2
                    pending_vectors(b, pending)
                    dve.wait_ge(unit_done, g + (1 + RING))
                    for r in range(2):
                        m = 2 * j + r
                        at_x, at_c = (3 * s, 3 * s + 1) if r == 0 else (3 * s + 2, 6 + s)
                        if j == 0 and r == 0:
                            dve.wait_ge(res_done, b * KC + (added_before(part) + FREE))
                        ins = dve.scalar_tensor_tensor(h[:, m, 0:NX], bank(at_x), gate_at(m, 0), h[:, m, 0:NX],
                                                       ALU.mult, ALU.add)
                        if both:
                            ins = dve.scalar_tensor_tensor(h[:, m, NX:T], bank(at_c, NCTX), gate_at(m, 1), h[:, m, NX:T],
                                                           ALU.mult, ALU.add)
                        ins.then_inc(res_done, 1)
                for_ffn_units(dve, plan, name, n, up, down, lambda *unit: None, own, 2 * HB,
                              lambda u, slot, turn: rest_parts(u + (SPLIT_BEFORE[n] + 1), slot))

            def add_residual(name, n, per_unit, gate_at, both):
                g0 = first[name]

                def unit(u, g, slot, turn):
                    dve.wait_ge(unit_done, g + 1 + RING)
                    for j in range(per_unit):
                        s = (slot - g0) % 2 * per_unit + j
                        m = u * per_unit + j
                        hx = h[:, ds(m, 1), 0:NX].rearrange("p a n -> p (a n)")
                        ins = dve.scalar_tensor_tensor(hx, bank(2 * s), gate_at(m, 0), hx, ALU.mult, ALU.add)
                        if both:
                            hc = h[:, ds(m, 1), NX:T].rearrange("p a n -> p (a n)")
                            ins = dve.scalar_tensor_tensor(hc, bank(2 * s + 1, NCTX), gate_at(m, 1), hc, ALU.mult, ALU.add)
                        ins.then_inc(res_done, 1)
                for_units(dve, plan, name, unit)

            def attention(att, staged, probs, keysT, bias, stage_values=None):
                NJ, NP = att.jobs, att.pieces

                def row_max(i, j):
                    dve.wait_ge(scores_done, i * NJ + (att.job0 + j + 1))
                    if bias(i, j):
                        src = probs[:, j % PROBS, 0:att.width]
                        own.wait()
                    else:
                        at = att.scores_at(j)
                        src = psum[:, at:at + att.width]
                    dve.tensor_reduce(nmax[:, j % 4:j % 4 + 1], src, AX.X, ALU.max, negate=True).then_inc(max_done, 1)

                def normalise(i, j):
                    dve.wait_ge(exp_done, i * NJ + (att.job0 + j + 1))
                    own.link(dve.reciprocal(rinv[:, j % 4:j % 4 + 1], rsum[:, j % 4:j % 4 + 1]))
                    p = probs[:, j % PROBS, 0:att.width]
                    dve.tensor_scalar(p, p, rinv[:, j % 4:j % 4 + 1], None, ALU.mult).then_inc(probs_ready, 1)

                def take(i, j):
                    for p in att.on_dve:
                        dve.wait_ge(turned, i * (NJ * NP) + (att.piece0 + j * NP + p + 1))
                        lo, hi = att.keys_of(p)
                        dve.tensor_copy(keysT[:, j % 2, lo:hi], psum[:, 2048 + lo:2048 + hi]).then_inc(turned_dve, 1)

                def stage(i, o):
                    copies = staged(i, o)
                    for n, (dst, src) in enumerate(copies):
                        ins = dve.tensor_copy(dst, src)
                        if n < len(copies) - 1:
                            own.mark(ins)
                    ins.then_inc(q_staged, 1)

                def tile(i, last):
                    for j in range(NJ):
                        if j + 1 < NJ or not last:
                            normalise(i, j + 1)
                        if j + AHEAD < NJ or not last:
                            row_max(i, j + AHEAD)
                        if j + AHEAD == NJ - 1 and not last:
                            stage(i, 1)
                        if j + 1 < NJ or not last:
                            take(i, j + 1)
                    if stage_values and not last:
                        dve.wait_ge(heads_done, i * NJ + (att.job0 + NJ))
                        stage_values(i, 1)

                stage(0, 0)
                if stage_values:
                    stage_values(0, 0)
                row_max(0, 0)
                row_max(0, 1)
                normalise(0, 0)
                row_max(0, 2)
                take(0, 0)
                for_tiles(dve, att, tile, own)
                dve.wait_ge(heads_done, att.job_end)

            def turned_before(att, i, j):
                if j >= PROBS:
                    dve.wait_ge(turned, i * (att.jobs * att.pieces) + (att.piece0 + (j - PROBS + 1) * att.pieces))

            def block1_attention(att, l, t0, latent):
                def staged(i, o):
                    return [(qst_1[:, 0:2, :], proj[:, QA:QA + 2, ds(i * P + (o * P + t0), P)]),
                            (qst_1[:, 2:6, :], proj[:, QG:QG + 4, ds(i * P + (o * P + t0), P)])]

                def bias(i, j):
                    o, n = divmod(j, att.jobs)
                    if not latent or n >= 4:
                        return False
                    turned_before(att, i, j)
                    at = att.scores_at(j)
                    own.mark(dve.tensor_tensor(probs_1[:, j % PROBS, 0:NX], psum[:, at:at + NX],
                                               rpb[:, n, ds(i * (-2 * GRID) + (7 - 2 * o) * GRID, NX)], ALU.add))
                    own.mark(dve.tensor_copy(probs_1[:, j % PROBS, NX:T], psum[:, at + NX:at + T]))
                    return True
                attention(att, staged, probs_1, keysT_1, bias)

            def qk_norm(l):
                for n in range(5):
                    c = QG + n
                    w = T if keeps_ctx(l, c) else NX
                    gain_col = qkg[:, 2 * l + (c == KG):2 * l + (c == KG) + 1]
                    dve.wait_ge(qk_root_done, 5 * l + n + 1)
                    own.link(dve.reciprocal(qk_rs[:, n % 2, 0:w], qk_rs[:, n % 2, 0:w]))
                    dve.scalar_tensor_tensor(proj[:, c, 0:w], proj[:, c, 0:w], gain_col, qk_rs[:, n % 2, 0:w],
                                             ALU.mult, ALU.mult).then_inc(qk_normed, 1)
                    dve.wait_ge(qk_normed, 5 * l + n + 1)
                    dve.wait_ge(qk_rotated, 5 * l + n + 1)
                    own.mark(dve.tensor_tensor(rope_t[:, 0, :], proj[:, c, 0:NX], cos_t, ALU.mult))
                    own.link(dve.tensor_tensor(rope_t[:, 1, :], bank(6 + n % 2), sin_t, ALU.mult))
                    dve.tensor_tensor(proj[:, c, 0:NX], rope_t[:, 0, :], rope_t[:, 1, :], ALU.add).then_inc(qk_roped, 1)
                    if n == 4:
                        dve.wait_ge(qk_roped, 5 * (l + 1))

            def pooling(l):
                w = POOL_W if both_in[l] else PAD + NX + PAD
                add = ALU.add
                dve.wait_ge(proj_done, PER_PROJ * l + UU + 2)
                own.link(dve.tensor_tensor(win2[:, :, 1:w], upad[:, :, 1:w], upad[:, :, 0:w - 1], add))
                own.link(dve.tensor_tensor(win4[:, :, 2:w - 1], win2[:, :, 1:w - 2], win2[:, :, 3:w], add))
                own.link(dve.tensor_tensor(win8[:, 4:w - 3], win4[:, 1, 2:w - 5], win4[:, 1, 6:w - 1], add))
                own.link(dve.tensor_tensor(win16[:, 8:w - 7], win8[:, 4:w - 11], win8[:, 12:w - 3], add))
                lo, hi = PAD, w - PAD
                for k, half, win in ((0, 0, win2[:, 0, :]), (0, 1, win4[:, 0, :]), (1, 0, win8), (1, 1, win16)):
                    q = slice(64 * half, 64 * half + 64)
                    own.link(dve.tensor_tensor(pool_y[q, k, lo:hi], win[q, lo:hi], pool_inv[q, k, lo:hi], ALU.mult))
                    ins = dve.tensor_tensor(pool_y[q, k, lo:hi], pool_y[q, k, lo:hi], upad[q, k, lo:hi], ALU.subtract)
                    if half == 0:
                        own.mark(ins)
                    else:
                        ins.then_inc(pool_ready, 1)

            def mix(l):
                dve.wait_ge(scaled_done, KC * (3 * l + 2))
                dve.memset(upad, 0.0).then_inc(upad_ready, 1)
                dve.wait_ge(table_in, TAB_MIX[l])
                qk_norm(l)
                pooling(l)
                dve.wait_ge(proj_done, PER_PROJ * (l + 1))
                dve.wait_ge(pool_done, 2 * l + 2)
                block1_attention(att_x[l], l, 0, True)
                if both_in[l]:
                    block1_attention(att_c0, l, NX, False)

            def gates(n0, dst):
                for c in range(4):
                    dve.wait_ge(gate_act, n0 + c + 1)
                    dve.tensor_tensor(dst[:, c, :], dst[:, c, :], gate_t[:, c % 2, :], ALU.mult).then_inc(gate_mul, 1)

            def hyena():
                freq = fw[0:HD, 3 * HD:3 * HD + 1]
                def net_argument(n):
                    dve.wait_ge(f_mm, n + 1)
                    arg, turns, rest = (f_tmp[0:HD, k, :] for k in range(3))
                    own.link(dve.tensor_scalar(rest, psum[0:HD, 3072:3072 + NX], fw[0:HD, 3 * HD + 1 + n:3 * HD + 2 + n],
                                               freq, ALU.add, ALU.mult))
                    own.link(dve.tensor_scalar(turns, rest, 1 / (2 * math.pi), ROUND_MAGIC, ALU.mult, ALU.add))
                    own.link(dve.tensor_scalar(turns, turns, -ROUND_MAGIC, None, ALU.add))
                    own.link(dve.scalar_tensor_tensor(rest, turns, -TWO_PI_HI, rest, ALU.mult, ALU.add))
                    own.link(dve.scalar_tensor_tensor(rest, turns, -TWO_PI_LO, rest, ALU.mult, ALU.add))
                    dve.tensor_scalar(arg, rest, PI_BELOW, -PI_BELOW, ALU.min, ALU.max).then_inc(f_arg, 1)

                dve.wait_ge(gate_mul, 4)
                own.mark(dve.memset(cpad[:, :, 0:1], 0.0))
                dve.memset(cpad[:, :, NX + 1:NX + 2], 0.0).then_inc(cpad_zero, 1)
                for c in range(12):
                    if c - 1 in NET_ARGUMENT_AFTER:
                        net_argument(NET_ARGUMENT_AFTER.index(c - 1))
                    dve.wait_ge(conv_in, c + 1)

                    def tap(k):
                        return vec2[:, OCW + 12 * k + c:OCW + 12 * k + c + 1]
                    own.link(dve.tensor_scalar(vxx[:, c, :], cpad[:, c % 2, 0:NX], tap(0), vec2[:, OCB + c:OCB + c + 1],
                                               ALU.mult, ALU.add))
                    own.link(dve.scalar_tensor_tensor(vxx[:, c, :], cpad[:, c % 2, 1:NX + 1], tap(1), vxx[:, c, :],
                                                      ALU.mult, ALU.add))
                    dve.scalar_tensor_tensor(vxx[:, c, :], cpad[:, c % 2, 2:NX + 2], tap(2), vxx[:, c, :],
                                             ALU.mult, ALU.add).then_inc(conv_out, 1)
                dve.wait_ge(conv_out, 12)
                dve.wait_ge(table_in, TAB_W4[0])
                for o in range(2):
                    for t in range(QC):
                        for r, dst in enumerate((hf, hb)):
                            n = 8 * o + 2 * t + r
                            dve.wait_ge(fh_mm, n + 1)
                            if o == 1:
                                dve.wait_ge(zi_mm, 4)
                            dve.tensor_tensor(dst[:, t, :], bank(n % 4), decay[:, t, :], ALU.mult).then_inc(fh_out, 1)
                        dve.wait_ge(fh_out, 8 * o + 2 * t + 2)
                        if t == 0:
                            own.link(dve.memset(hb[0:1, 0, :], 0.0))
                        own.link(dve.tensor_tensor(mul_t[:, 0, :], hb[:, t, :], hf[:, t, :], ALU.subtract))
                        own.link(dve.tensor_tensor(hf[:, t, :], hf[:, t, :], hb[:, t, :], ALU.add))
                        dve.tensor_copy(hb[:, t, :], mul_t[:, 0, :]).then_inc(fh_ready, 1)
                    for q in range(4):
                        if q > 0:
                            dve.wait_ge(zf_out, 4 * o + q)
                        dve.wait_ge(zf_mm, 4 * o + q + 1)
                        dve.wait_ge(ft_out, 4 * o + q + 1)
                        A, B = bank(2 * (q % 2)), bank(2 * (q % 2) + 1)
                        own.mark(dve.tensor_tensor(mul_t[:, 0, :], H_re[:, q, :], A, ALU.mult))
                        own.link(dve.tensor_tensor(mul_t[:, 1, :], H_im[:, q, :], B, ALU.mult))
                        own.link(dve.tensor_tensor(y_re[:, q, :], mul_t[:, 0, :], mul_t[:, 1, :], ALU.add))
                        own.mark(dve.tensor_tensor(mul_t[:, 0, :], H_re[:, q, :], B, ALU.mult))
                        own.link(dve.tensor_tensor(mul_t[:, 1, :], H_im[:, q, :], A, ALU.mult))
                        dve.tensor_tensor(y_im[:, q, :], mul_t[:, 0, :], mul_t[:, 1, :], ALU.subtract).then_inc(zf_out, 1)
                    dve.wait_ge(zf_out, 4 * (o + 1))
                    for c in range(4):
                        dve.wait_ge(zi_mm, 4 * o + c + 1)
                        fb = vec2[:, OFB + 4 * o + c:OFB + 4 * o + c + 1]
                        own.link(dve.scalar_tensor_tensor(mul_t[:, c % 2, :], vxx[:, c, :], fb, bank(4 + c % 2),
                                                          ALU.mult, ALU.add))
                        dve.tensor_tensor(vxx[:, c, :], mul_t[:, c % 2, :], vxx[:, 4 + 4 * o + c, :], ALU.mult)\
                           .then_inc(zi_out, 1)
                    dve.wait_ge(zi_out, 4 * (o + 1))
                gates(4, vxx)

            def merge():
                g0 = first["merge_h"]
                for c in range(KC):
                    dve.wait_ge(merge_sig, c + 1)
                    dve.wait_ge(unit_done, g0 + 3 * (c // 2) + 3 + RING)
                    if c > 0:
                        dve.wait_ge(merge_out, c)
                    for r in range(2):
                        own.mark(dve.tensor_tensor(mt_t[:, r, :], sg_t[:, c % 2, r * NX:(r + 1) * NX],
                                                   bank(4 + 2 * (c % 2) + r), ALU.mult))
                    own.wait()
                    dve.tensor_tensor(merged[:, c, :], mt_t[:, 0, :], mt_t[:, 1, :], ALU.add).then_inc(merge_out, 1)
                g0 = first["out_h"]
                for c in range(KC):
                    dve.wait_ge(unit_done, g0 + c // 2 + 1 + RING)
                    own.link(dve.tensor_scalar(mt_t[:, c % 2, :], bank(c % 4), vec2[:, OBO + c:OBO + c + 1],
                                               mod2[:, 2 * KC + c:2 * KC + c + 1], ALU.add, ALU.mult))
                    dve.scalar_tensor_tensor(res[:, c, :], x2[:, c, :], ALPHA, mt_t[:, c % 2, :], ALU.mult, ALU.add)\
                       .then_inc(out2_done, 1)
                dve.wait_ge(out2_done, KC)
                dve.wait_ge(mean_done, 1)
                centre(res, res)
                scale_rows(RMS + 1, res, res, sg_t[:, 0, :], NX)

            def centre(src, dst):
                for c in range(KC):
                    dve.scalar_tensor_tensor(dst[:, c, :], bank(4), -1.0 / D, src[:, c, :], ALU.mult, ALU.add)\
                       .then_inc(centred, 1)

            own.mark(dve.memset(eps[:, 0:1], EPS))
            own.mark(dve.memset(eps[:, 1:2], LN_EPS))
            own.mark(dve.memset(ones[:, 0:1], 1.0))
            dve.memset(ones[:, 2:3], 1.0).then_inc(res_done, FREE)
            def setup():
                dve.wait_ge(consts_in, N_CONSTS)
                for l in range(DEPTH):
                    own.mark(dve.tensor_scalar(qkg[:, 2 * l:2 * l + 1], small[:, 4 * l + 2:4 * l + 3], SCORE_SCALE, None, ALU.mult))
                    own.mark(dve.tensor_copy(qkg[:, 2 * l + 1:2 * l + 2], small[:, 4 * l + 3:4 * l + 4]))
                own.mark(dve.tensor_scalar(bq[:], vec2[:, OB_IN:OB_IN + 12], SCORE_SCALE, None, ALU.mult))
                own.wait()
                dve.memset(ones[:], 1.0).then_inc(setup_done, 1)

            own.link(dve.memset(c_parts_t[:].bitcast(F32), 0.0))
            dve.wait_ge(silu_c, 1)
            own.link(dve.tensor_copy(c_parts[:, :, 0:3], cv))
            dve.tensor_tensor(c_parts[:, :, 3:6], cv, c_parts[:, :, 0:3].bitcast(F32), ALU.subtract).then_inc(c_ready, 1)
            for t in range(GROUPS_FIRST + 1):
                if t < GROUPS_FIRST:
                    for u in (2 * t, 2 * t + 1):
                        rest_parts(u + 1, u % RING)
                if t > 0:
                    if t == 1:
                        setup()
                    if t == GROUPS_FIRST:
                        stream_reciprocal(0, T)
                    take_vectors(t - 1, 0, 0, 7 - (t - 1) % 2)
            for l in range(DEPTH):
                gate = mod[l][:, 5, :, :]

                def half_of(k):
                    return lambda m, s: hgate[:, k, m, s:s + 1]

                if l == 0:
                    modulation(l, 0)
                first_rests(f"ffn1_{l}", 2 * l)
                if l > 0:
                    modulation(l, 0)
                scale_and_split(3 * l, 2 * l, T)
                first_rests(f"ffn1_{l}", 2 * l, 2, LEAD)
                ffn(f"ffn1_{l}", 2 * l, 3 * l, half_of(0), True)
                dve.wait_ge(res_done, FREE + added_before(3 * l + 1))
                modulation(l, 1)
                scale_rows(3 * l + 1, h, a, rstd, T)
                mix(l)
                add_residual(f"out{l}", 3 * l + 1, 2,
                             lambda m, s: gate[:, ds(m, 1), s:s + 1].rearrange("p a b -> p (a b)"), both_in[l])
                dve.wait_ge(res_done, FREE + added_before(3 * l + 2))
                first_rests(f"ffn2_{l}", 2 * l + 1)
                modulation(l, 2)
                scale_and_split(3 * l + 2, 2 * l + 1, T if both_in[l] else NX)
                first_rests(f"ffn2_{l}", 2 * l + 1, 2, LEAD)
                ffn(f"ffn2_{l}", 2 * l + 1, 3 * l + 2, half_of(1), both_in[l])
                dve.wait_ge(res_done, FREE + added_before(3 * l + 3))
            scale_rows(RMS - 1, h, x2, rstd, NX)
            dve.wait_ge(mods_done, 2 * ADA_GROUPS + 3 * KC // 4)
            own.link(dve.tensor_scalar(gain2[:], mod2[:, KC:2 * KC], 1.0, None, ALU.add))
            dve.wait_ge(mean_done_0, 1)
            centre(x2, h2)
            dve.wait_ge(centred, KC)
            first_unit, n_split = first["q_h"], SPLIT_BEFORE[2 * DEPTH]
            for u in range(2):
                rest_parts(n_split + u + 1, (first_unit + u) % RING)
            scale_rows(RMS, h2, h2, rstd2, NX)
            for c in range(KC):
                dve.wait_ge(h2_hi_done, c + 1)
                dve.tensor_tensor(h2_lo[:, c, :], h2[:, c, :], h2_hi[:, c, :].bitcast(F32), ALU.subtract)\
                   .then_inc(h2_split, 1)
            for u in range(2, after["k_h"] - first_unit):
                rest_parts(n_split + u + 1, (first_unit + u) % RING)
            dve.wait_ge(table_in, TAB_QKV)
            for u in range(6):
                dve.wait_ge(unit_done, first["v_h"] + u + 1 + RING)
                for t in range(QC):
                    dve.tensor_tensor(vh[:, t, 256 * u:256 * (u + 1)], bank(4 + t, 256), vbias[:, 256 * u:256 * (u + 1)],
                                      ALU.add).then_inc(v2_out, 1)
            dve.wait_ge(qk2_out, 24)
            dve.wait_ge(v2_out, 24)

            def staged(i, o):
                return [(qst_2, qh[:, :, ds(i * P + o * P, P)]), (kst, kh[:, 4:12, ds(i * P + o * P, P)])]

            def stage_values(i, o):
                dve.tensor_copy(vst, vh[:, ds(i + o, 1), 512:1536].rearrange("p a (g n) -> p (a g) n", g=2))\
                   .then_inc(v_staged, 1)

            def bias(i, j):
                o, n = divmod(j, NH2)
                turned_before(att_h, i, j)
                at, p = att_h.scores_at(j), probs_2[:, j % PROBS, :]
                slope = 2.0 ** -(n + 1)
                own.mark(dve.scalar_tensor_tensor(p[:, 0:NX], alibi[:, ds(i * (-P) + (3 - o) * P, NX)], slope,
                                                  psum[:, at:at + NX], ALU.mult, ALU.add))
                own.mark(dve.scalar_tensor_tensor(p[:, NX:KEYS2], alibi[:, 7 * P:9 * P], slope,
                                                  psum[:, at + NX:at + KEYS2], ALU.mult, ALU.add))
                return True
            attention(att_h, staged, probs_2, keysT_2, bias, stage_values)
            gates(0, y_attn)
            hyena()
            merge()


def constants():
    t = np.arange(NX)
    inv = (10000.0 ** (-np.arange(0, HD // 2, 2, dtype=np.float32) / np.float32(HD // 2))).astype(np.float32)
    ang = np.stack([(t // GRID).astype(np.float32)[:, None] * inv, (t % GRID).astype(np.float32)[:, None] * inv])
    c64 = np.concatenate([np.cos(ang[0]), np.cos(ang[0]), np.cos(ang[1]), np.cos(ang[1])], 1).T
    s64 = np.concatenate([-np.sin(ang[0]), np.sin(ang[0]), -np.sin(ang[1]), np.sin(ang[1])], 1).T
    cos_t, sin_t = (np.concatenate([x, x]).astype(np.float32) for x in (c64, s64))
    rot = np.zeros((P, P), np.float32)
    for i in range(P):
        rot[i ^ 16, i] = 1.0
    pairs = np.kron(np.eye(2), np.ones((HD, HD))).astype(np.float32)
    fold = np.zeros((P, 3), np.float32)
    fold[0:3], fold[3:6] = np.eye(3), np.eye(3)
    cst = np.concatenate([np.eye(P, dtype=np.float32), rot, pairs, fold], 1)
    inv_count = np.zeros((P, 2, POOL_W), np.float32)
    for n, at in ((NX, POOL_X), (NCTX, POOL_C)):
        s = np.arange(n)
        for g, w in enumerate((2, 4, 8, 16)):
            count = np.clip(s - w // 2 + w, 0, n) - np.clip(s - w // 2, 0, n)
            inv_count[64 * (g % 2):64 * (g % 2) + 64, g // 2, at:at + n] = 1.0 / count
    alibi = np.full((P, 9, P), NEG, np.float32)
    step = np.arange(P)[None, :] - np.arange(P)[:, None]
    for k in range(7):
        dist = np.abs(RES * step + k - 3)
        alibi[:, k][dist <= 64] = -dist[dist <= 64]
    for k, dil in ((7, 4), (8, 16)):
        dist = np.abs(RES * step)
        valid = (dist % dil == 0) & (dist <= 64 * dil)
        alibi[:, k][valid] = -dist[valid]
    alibi = alibi.reshape(P, 9 * P)
    tl = np.linspace(0.0, 1.0, NX, dtype=np.float32)[:, None]
    w = (np.float32(2.0 * math.pi) * np.arange(NX, dtype=np.float32)[:, None] / np.float32(NX)).astype(np.float32)
    f = np.linspace(1e-4, 15, 16, dtype=np.float32)[None, :]
    fw_ = (f * w).astype(np.float32)
    feats = np.concatenate([tl, np.cos(fw_), -np.sin(fw_)], 1).T.astype(np.float32)
    deltas = np.linspace(math.log(1e-2) / 1.5, math.log(1e-2) / 0.3, NX, dtype=np.float32)
    decay = np.exp(-tl * np.abs(deltas)[None, :]).astype(np.float32)
    th = np.pi * (2 * np.arange(NX)[None, :] + 1) * np.arange(NX)[:, None] / (2 * NX)
    def tiles(m):
        return m.reshape(4, P, NX).transpose(1, 0, 2).astype(np.float32)
    dft = np.concatenate([tiles(np.cos(th)), tiles(np.sin(th)), tiles(np.cos(th.T) / NX), tiles(np.sin(th.T) / NX)], 1)
    return dict(cos_t=cos_t, sin_t=sin_t, cst=cst, pool_inv=inv_count, alibi=alibi, feats=np.ascontiguousarray(feats),
                decay=tiles(decay), dft=np.ascontiguousarray(dft))


def blocked(w, cols_per_unit):
    k, m = w.shape
    v = w.reshape(k // P, P, m // P // cols_per_unit, cols_per_unit, P)
    return np.ascontiguousarray(v.transpose(2, 1, 3, 0, 4)).reshape(m // P // cols_per_unit, P, -1)


def as_rhs(w, cols):
    k, m = w.shape
    v = w.reshape(k // P, P, m // cols, cols)
    return np.ascontiguousarray(v.transpose(2, 1, 0, 3)).reshape(m // cols, P, -1)


def columns(v):
    return v.reshape(-1, P).T


def layout(inputs):
    x = {k: np.asarray(v) for k, v in inputs.items()}
    d = dict(constants())
    d["xT"] = x["x"][0].T.reshape(KC, P, NX).transpose(1, 0, 2)
    d["ctxT"] = x["ctx"][0].T.reshape(KC, P, NCTX).transpose(1, 0, 2)
    d["cvec"] = np.stack([columns(x["c"][0]), columns(x["c_ctx"]), columns(x["c_2"][0])], 2).reshape(P, -1)
    d["b_ada"] = np.repeat(np.concatenate([columns(x["b_ada"][l]) for l in range(DEPTH)], 1), 2, axis=1)
    d["ng"] = np.concatenate([np.repeat(np.concatenate([columns(x["norm_g"][l, k]) for l in range(DEPTH) for k in range(3)], 1),
                                        2, axis=1), columns(x["final_g"])], 1)
    small = []
    for l in range(DEPTH):
        small += [columns(x["pool_scale"][l]), np.tile(x["q_norm_g"][l], 2)[:, None], np.tile(x["k_norm_g"][l], 2)[:, None]]
    d["small"] = np.concatenate(small, 1)
    poolw = np.zeros((P, DEPTH, 2, P), np.float32)
    for l in range(DEPTH):
        for g in range(4):
            r = 64 * (g % 2)
            poolw[r:r + 64, l, g // 2, r:r + 64] = x["pool_w"][l, g]
    d["poolw"] = poolw.reshape(P, -1)
    d["vec2"] = np.concatenate(
        [columns(x["b_ada_2"][0]), columns(x["b_in_2"][0])] + [columns(x["conv_w_2"][0, k]) for k in range(3)]
        + [columns(x["conv_b_2"][0])] + [columns(x["filt_bias_2"][0, o]) for o in range(2)]
        + [columns(x["b_out_2"][0]), columns(x["ln_g_2"][0]), columns(x["ln_b_2"][0])], 1)
    fw = np.zeros((HD, 3 * HD + 4), np.float32)
    fw[0:33, 0:HD] = x["filt_w1_2"][0]
    fw[:, HD:2 * HD], fw[:, 2 * HD:3 * HD] = x["filt_w2_2"][0], x["filt_w3_2"][0]
    for k, name in enumerate(("filt_freq_2", "filt_b1_2", "filt_b2_2", "filt_b3_2")):
        fw[:, 3 * HD + k] = x[name][0]
    d["fw"] = fw
    d["w4_0"], d["w4_1"] = x["filt_w4_2"][0][:, 0:2 * NX], x["filt_w4_2"][0][:, 2 * NX:4 * NX]
    order = np.concatenate([np.arange(HD) + HD * n for i in range(4) for n in (i, 4 + i)])
    col = np.arange(GRID)
    c0 = np.clip(col - 8, 0, GRID - 16)
    seen = (col[None, :] >= c0[:, None]) & (col[None, :] < c0[:, None] + 16)
    dx = np.clip(col[None, :] - col[:, None], -15, 15) + 15
    ada = np.concatenate([as_rhs(w, 256) for w in (x["w_ada"][0], x["w_ada"][1], x["w_ada_2"][0])])
    d["ada0"] = ada[0:2 * GROUPS_FIRST]
    for l in range(DEPTH):
        wi = x["w_in"][l]
        for k in (1, 2):
            up = x[f"ffn{k}_up"][l]
            pairs = np.stack([up[:, :FF].reshape(D, FC, P), up[:, FF:].reshape(D, FC, P)], 2).reshape(D, 2 * FF)
            ups, down = blocked(pairs, 2), x[f"ffn{k}_down"][l]
            n = 2 * l + k - 1
            (first_two, last), group = ffn_schedules(n), groups_before(n)
            units, at = np.zeros((ffn_units(n), P, SLOT), np.float32), 0
            for b, schedule in enumerate((first_two, first_two, last)):
                lo, hi = b * HB, min((b + 1) * HB, FC)
                downs = blocked(down[lo * P:hi * P], 2)
                for kind, j, half in schedule:
                    if kind == "up":
                        units[at] = ups[lo + j]
                    elif kind == "down":
                        units[at, :, 0:2 * (hi - lo) * P] = downs[j]
                    else:
                        units[at] = ada[2 * group + half]
                        group += half
                    at += 1
            d[f"ffn{k}_{l}"] = units
        u = np.zeros((8, P, 2 * D), np.float32)
        cols = np.concatenate([wi[:, 1024:1536][:, order], wi[:, 1536:1664], wi[:, 768:1024], wi[:, 0:512]], 1)
        u[0:5] = blocked(cols[:, 0:10 * P], 2)
        u[5, :, 0:D] = blocked(cols[:, 10 * P:], 1)[0]
        u[6] = as_rhs(wi[:, 512:768], 256)[0]
        u[7, :, 0:D] = as_rhs(wi[:, 1664:1792], 128)[0]
        d[f"in{l}"] = u
        wo = x["w_out"][l]
        d[f"out{l}"] = blocked(np.concatenate([wo[0:512], wo[512:1024][order]], 0), 2)
        table = np.where(seen[None, None], x["na_rpb"][l][:, :, dx], np.float32(NEG)).transpose(2, 0, 1, 3)
        rpb = np.zeros((P, 4, 15, GRID), np.float32)
        rpb[0:64] = table
        rpb[64:128, :, 1:15] = table[:, :, 0:14]
        d[f"rpb{l}"] = rpb.reshape(P, 4, 15 * GRID)
    w2 = x["w_in_2"][0]
    d["q_h"], d["k_h"] = blocked(w2[:, 0:1536], 2), blocked(w2[:, 1536:3072], 2)
    d["v_h"] = as_rhs(w2[:, 3072:4608], 256)
    d["vbias"] = np.broadcast_to(x["b_in_2"][0][3072:4608], (P, 1536))
    d["gattn_h"] = blocked(w2[:, 4608:5120], 2)
    d["conv_h"] = blocked(w2[:, 5120:6656], 2)
    d["ghy_h"] = blocked(w2[:, 6656:7168], 2)
    r = np.stack([w2[:, 7168:8192].reshape(D, KC, P), w2[:, 8192:9216].reshape(D, KC, P)], 2).reshape(D, 2 * D)
    r = blocked(r, 2)
    pj = np.stack([x["w_proj_attn_2"][0].reshape(512, KC, P), x["w_proj_hyena_2"][0].reshape(512, KC, P)], 2).reshape(512, 2 * D)
    pj = blocked(pj, 4)
    m = np.zeros((12, P, 2 * D), np.float32)
    for q in range(4):
        m[3 * q], m[3 * q + 1], m[3 * q + 2] = r[2 * q], r[2 * q + 1], pj[q]
    d["merge_h"] = m
    d["out_h"] = blocked(x["w_out_2"][0], 2)
    return {k: np.ascontiguousarray(v) for k, v in d.items()}


def kernel(**inputs):
    import concourse.bacc as bacc
    from concourse.bass_utils import run_bass_kernel_spmd

    arrays = layout(inputs)
    nc = bacc.Bacc("TRN2", target_bir_lowering=False, num_devices=1)
    io = {k: nc.dram_tensor(f"in_{k}", v.shape, mybir.dt.from_np(v.dtype), kind="ExternalInput").ap()
          for k, v in arrays.items()}
    out = nc.dram_tensor("out_T", (KC, P, NX), F32, kind="ExternalOutput").ap()
    hybrid_kernel(nc, io, out)
    r = run_bass_kernel_spmd(nc, [{f"in_{k}": v for k, v in arrays.items()}], core_ids=[0])
    return r.results[0]["out_T"].reshape(D, NX).T.reshape(1, NX, D)
```
